# Optimizing a Trainium2 kernel written in Bass

```python
import jax, jax.numpy as jnp
from jax import lax
import numpy as np

D_MODEL = 1024
BATCH = 1
SEQ = 512
DEPTH = 2

N_MIXERS = 2
N_A_LAYERS = (DEPTH + 1) // 2
N_B_LAYERS = DEPTH // 2
D_FF = ((8 * D_MODEL // 3 + 127) // 128) * 128
RMS_EPS = 1e-6

A_HEADS = 4
A_DQK = D_MODEL // 8
A_DV = D_MODEL // 4
A_CHUNK = 128
A_CONV = 5
A_QK = 2 * A_HEADS * A_DQK
A_V = A_HEADS * A_DV
A_IN = A_QK + 2 * A_V + 4 * A_HEADS

B_GROUPS = ((128, 1), (512, 4), (2048, 16))
B_HEADS = 16
B_DH = D_MODEL // B_HEADS
B_WIDTH = B_HEADS * B_DH
B_IN = len(B_GROUPS) * 3 * B_WIDTH

kernel_name = "hybrid_mlstm_dilated_macaron"

def rmsnorm(x, g):
    xf = x.astype(jnp.float32)
    y = xf * lax.rsqrt(jnp.mean(xf * xf, axis=-1, keepdims=True) + RMS_EPS)
    return (y * g.astype(jnp.float32)).astype(x.dtype)

def swiglu(x, w_gate, w_up, w_down):
    return (jax.nn.silu(x @ w_gate) * (x @ w_up)) @ w_down

def alibi_slopes(n_heads):
    return jnp.exp2(-8.0 * (jnp.arange(n_heads, dtype=jnp.float32) + 1.0) / n_heads)

def _mlstm_one_direction(q, k, v, log_i, log_f):
    bsz, nh, s, dqk = q.shape
    dv = v.shape[-1]
    L = A_CHUNK
    nc = s // L
    q = q.reshape(bsz, nh, nc, L, dqk)
    k = k.reshape(bsz, nh, nc, L, dqk)
    v = v.reshape(bsz, nh, nc, L, dv)
    log_i = log_i.reshape(bsz, nh, nc, L)
    b = jnp.cumsum(log_f.reshape(bsz, nh, nc, L), axis=-1)
    b_tot = b[..., -1]
    a = b_tot[..., None] - b + log_i
    m_loc = jnp.max(a, axis=-1)
    kw = k * jnp.exp(a - m_loc[..., None])[..., None]
    c_loc = jnp.einsum('bhcsk,bhcsv->bhckv', kw, v)
    n_loc = jnp.sum(kw, axis=3)

    def step(carry, inp):
        c, n, m = carry
        cl, nl, ml, bt = inp
        m_new = jnp.maximum(bt + m, ml)
        s_prev = jnp.exp(bt + m - m_new)
        s_loc = jnp.exp(ml - m_new)
        c_new = s_prev[..., None, None] * c + s_loc[..., None, None] * cl
        n_new = s_prev[..., None] * n + s_loc[..., None] * nl
        return (c_new, n_new, m_new), (c, n, m)

    init = (jnp.zeros((bsz, nh, dqk, dv), q.dtype),
            jnp.zeros((bsz, nh, dqk), q.dtype),
            jnp.zeros((bsz, nh), q.dtype))
    xs = (jnp.moveaxis(c_loc, 2, 0), jnp.moveaxis(n_loc, 2, 0),
          jnp.moveaxis(m_loc, 2, 0), jnp.moveaxis(b_tot, 2, 0))
    _, (c_prev, n_prev, m_prev) = lax.scan(step, init, xs)
    c_prev = jnp.moveaxis(c_prev, 0, 2)
    n_prev = jnp.moveaxis(n_prev, 0, 2)
    m_prev = jnp.moveaxis(m_prev, 0, 2)

    g = b + m_prev[..., None]
    d = b[..., :, None] - b[..., None, :] + log_i[..., None, :]
    tri = jnp.tril(jnp.ones((L, L), dtype=bool))
    d = jnp.where(tri, d, -jnp.inf)
    m_t = jnp.maximum(g, jnp.max(d, axis=-1))
    p = jnp.exp(d - m_t[..., None]) * jnp.einsum('bhctk,bhcsk->bhcts', q, k)
    s_inter = jnp.exp(g - m_t)
    num = (s_inter[..., None] * jnp.einsum('bhctk,bhckv->bhctv', q, c_prev)
           + jnp.einsum('bhcts,bhcsv->bhctv', p, v))
    den = s_inter * jnp.einsum('bhctk,bhck->bhct', q, n_prev) + jnp.sum(p, axis=-1)
    h = num / jnp.maximum(jnp.abs(den), jnp.exp(-m_t))[..., None]
    return h.reshape(bsz, nh, s, dv)

def mlstm_mixer(h, w_in, conv_w, conv_b, gate_b, head_g, w_out):
    bsz, s, _ = h.shape
    f32 = jnp.float32
    proj = h @ w_in
    qk = proj[..., :A_QK]
    v = proj[..., A_QK:A_QK + A_V]
    o = proj[..., A_QK + A_V:A_QK + 2 * A_V]
    gates = proj[..., A_QK + 2 * A_V:].astype(f32) + gate_b.astype(f32)
    qk = lax.conv_general_dilated(qk, conv_w[:, None, :], (1,), [(A_CONV // 2, A_CONV // 2)],
                                  dimension_numbers=('NWC', 'WIO', 'NWC'),
                                  feature_group_count=A_QK)
    qk = jax.nn.silu(qk + conv_b)
    q = qk[..., :A_QK // 2].reshape(bsz, s, A_HEADS, A_DQK).transpose(0, 2, 1, 3).astype(f32) * (A_DQK ** -0.5)
    k = qk[..., A_QK // 2:].reshape(bsz, s, A_HEADS, A_DQK).transpose(0, 2, 1, 3).astype(f32)
    v = v.reshape(bsz, s, A_HEADS, A_DV).transpose(0, 2, 1, 3).astype(f32)
    gates = gates.reshape(bsz, s, 4, A_HEADS).transpose(2, 0, 3, 1)
    i_f, f_f, i_b, f_b = gates[0], gates[1], gates[2], gates[3]
    h_f = _mlstm_one_direction(q, k, v, i_f, jax.nn.log_sigmoid(f_f))
    flip = lambda t: jnp.flip(t, axis=2)
    h_b = flip(_mlstm_one_direction(flip(q), flip(k), flip(v), flip(i_b),
                                    flip(jax.nn.log_sigmoid(f_b))))
    y = h_f + h_b
    y = y * lax.rsqrt(jnp.mean(y * y, axis=-1, keepdims=True) + RMS_EPS)
    y = y.transpose(0, 2, 1, 3).reshape(bsz, s, A_V) * head_g.astype(f32) * jax.nn.sigmoid(o.astype(f32))
    return y.astype(h.dtype) @ w_out

def _dilated_group(q, k, v, dil, half, slopes):
    bsz, s, nh, dh = q.shape
    f32 = jnp.float32
    n = s // dil
    nb = -(-n // half)
    npad = nb * half

    def to_blocks(t):
        t = t.astype(f32).reshape(bsz, n, dil, nh, dh).transpose(0, 2, 1, 3, 4)
        t = jnp.pad(t, ((0, 0), (0, 0), (0, npad - n), (0, 0), (0, 0)))
        return t.reshape(bsz, dil, nb, half, nh, dh)

    def neighbours(t):
        tp = jnp.pad(t, ((0, 0), (0, 0), (1, 1), (0, 0), (0, 0), (0, 0)))
        return jnp.concatenate([tp[:, :, :-2], tp[:, :, 1:-1], tp[:, :, 2:]], axis=3)

    qb = to_blocks(q)
    kn = neighbours(to_blocks(k))
    vn = neighbours(to_blocks(v))
    qi = jnp.arange(nb)[:, None] * half + jnp.arange(half)[None, :]
    ki = (jnp.arange(nb)[:, None] - 1) * half + jnp.arange(3 * half)[None, :]
    rel = jnp.abs(ki[:, None, :] - qi[:, :, None])
    valid = (rel <= half) & (ki[:, None, :] >= 0) & (ki[:, None, :] < n)
    penalty = slopes[None, :, None, None] * (rel * dil).astype(f32)[:, None]
    sc = jnp.einsum('brcqhd,brckhd->brchqk', qb, kn) * (dh ** -0.5) - penalty
    sc = jnp.where(valid[:, None], sc, -jnp.inf)
    mx = jnp.max(sc, axis=-1, keepdims=True)
    e = jnp.exp(sc - mx)
    den = jnp.sum(e, axis=-1, keepdims=True)
    out = jnp.einsum('brchqk,brckhd->brcqhd', e / den, vn)
    lse = (mx + jnp.log(den))[..., 0]
    out = out.reshape(bsz, dil, npad, nh, dh)[:, :, :n].transpose(0, 2, 1, 3, 4).reshape(bsz, s, nh, dh)
    lse = lse.transpose(0, 1, 2, 4, 3).reshape(bsz, dil, npad, nh)[:, :, :n]
    lse = lse.transpose(0, 2, 1, 3).reshape(bsz, s, nh)
    return out, lse

def dilated_mixer(h, w_in, w_out):
    bsz, s, _ = h.shape
    proj = (h @ w_in).reshape(bsz, s, len(B_GROUPS), 3, B_HEADS, B_DH)
    slopes = alibi_slopes(B_HEADS)
    outs, lses = [], []
    for gi, (window, dil) in enumerate(B_GROUPS):
        o, l = _dilated_group(proj[:, :, gi, 0], proj[:, :, gi, 1], proj[:, :, gi, 2],
                              dil, window // (2 * dil), slopes)
        outs.append(o)
        lses.append(l)
    alpha = jax.nn.softmax(jnp.stack(lses, axis=0), axis=0)
    y = jnp.sum(alpha[..., None] * jnp.stack(outs, axis=0), axis=0).reshape(bsz, s, B_WIDTH)
    return y.astype(h.dtype) @ w_out

def setup_inputs(seed: int = 0) -> dict:
    key = jax.random.key(seed)
    ks = iter(jax.random.split(key, 24))
    f32 = jnp.float32

    def nrm(shape, scale):
        return jax.random.normal(next(ks), shape, f32) * scale

    def gain(shape):
        return 1.0 + nrm(shape, 0.05)

    x = nrm((BATCH, SEQ, D_MODEL), 1.0)
    norm_ffn1 = gain((DEPTH, D_MODEL))
    ffn1_gate = nrm((DEPTH, D_MODEL, D_FF), D_MODEL ** -0.5)
    ffn1_up = nrm((DEPTH, D_MODEL, D_FF), D_MODEL ** -0.5)
    ffn1_down = nrm((DEPTH, D_FF, D_MODEL), D_FF ** -0.5)
    norm_mix = gain((DEPTH, D_MODEL))
    a_w_in = nrm((N_A_LAYERS, D_MODEL, A_IN), D_MODEL ** -0.5)
    a_conv_w = nrm((N_A_LAYERS, A_CONV, A_QK), A_CONV ** -0.5)
    a_conv_b = nrm((N_A_LAYERS, A_QK), 0.02)
    ig_b = nrm((N_A_LAYERS, 2, A_HEADS), 0.1)
    fg_b = jnp.linspace(3.0, 6.0, A_HEADS, dtype=f32) + nrm((N_A_LAYERS, 2, A_HEADS), 0.1)
    a_gate_b = jnp.stack([ig_b[:, 0], fg_b[:, 0], ig_b[:, 1], fg_b[:, 1]], axis=1).reshape(N_A_LAYERS, 4 * A_HEADS)
    a_head_g = gain((N_A_LAYERS, A_V))
    a_w_out = nrm((N_A_LAYERS, A_V, D_MODEL), A_V ** -0.5)
    b_w_in = nrm((N_B_LAYERS, D_MODEL, B_IN), D_MODEL ** -0.5)
    b_w_out = nrm((N_B_LAYERS, B_WIDTH, D_MODEL), B_WIDTH ** -0.5)
    norm_ffn2 = gain((DEPTH, D_MODEL))
    ffn2_gate = nrm((DEPTH, D_MODEL, D_FF), D_MODEL ** -0.5)
    ffn2_up = nrm((DEPTH, D_MODEL, D_FF), D_MODEL ** -0.5)
    ffn2_down = nrm((DEPTH, D_FF, D_MODEL), D_FF ** -0.5)
    norm_final = gain((D_MODEL,))
    return {"x": x, "norm_ffn1": norm_ffn1, "ffn1_gate": ffn1_gate, "ffn1_up": ffn1_up,
            "ffn1_down": ffn1_down, "norm_mix": norm_mix, "a_w_in": a_w_in,
            "a_conv_w": a_conv_w, "a_conv_b": a_conv_b, "a_gate_b": a_gate_b,
            "a_head_g": a_head_g, "a_w_out": a_w_out, "b_w_in": b_w_in, "b_w_out": b_w_out,
            "norm_ffn2": norm_ffn2, "ffn2_gate": ffn2_gate, "ffn2_up": ffn2_up,
            "ffn2_down": ffn2_down, "norm_final": norm_final}

def reference(x, norm_ffn1, ffn1_gate, ffn1_up, ffn1_down, norm_mix, a_w_in, a_conv_w,
              a_conv_b, a_gate_b, a_head_g, a_w_out, b_w_in, b_w_out, norm_ffn2,
              ffn2_gate, ffn2_up, ffn2_down, norm_final):
    for i in range(DEPTH):
        x = x + 0.5 * swiglu(rmsnorm(x, norm_ffn1[i]), ffn1_gate[i], ffn1_up[i], ffn1_down[i])
        h = rmsnorm(x, norm_mix[i])
        j = i // N_MIXERS
        if i % N_MIXERS == 0:
            x = x + mlstm_mixer(h, a_w_in[j], a_conv_w[j], a_conv_b[j], a_gate_b[j],
                                a_head_g[j], a_w_out[j])
        else:
            x = x + dilated_mixer(h, b_w_in[j], b_w_out[j])
        x = x + 0.5 * swiglu(rmsnorm(x, norm_ffn2[i]), ffn2_gate[i], ffn2_up[i], ffn2_down[i])
    return rmsnorm(x, norm_final)


_drawn_inputs = setup_inputs


def setup_inputs(seed=0):
    import zlib

    import numpy as np

    out = dict(_drawn_inputs(seed))
    spreads = {}
    factors = {'a_conv_b': 6.294}
    for name, (base, spread) in spreads.items():
        noise = np.random.default_rng([zlib.crc32(name.encode()), seed]).standard_normal(out[name].shape)
        drawn = base * np.exp(spread * noise) if base else spread * noise
        out[name] = __import__('jax').numpy.asarray(drawn.astype(out[name].dtype))
    for name, factor in factors.items():
        out[name] = (out[name] * factor).astype(out[name].dtype)
    return out
```

```python
from contextlib import ExitStack

import numpy as np

import concourse.bass as bass
from concourse import mybir
from concourse.alu_op_type import AluOpType as ALU

ACT = mybir.ActivationFunctionType
F32 = mybir.dt.float32
F32R = mybir.dt.float32r
AX = mybir.AxisListType

P = 128
D = 1024
SEQ = 512
FF = 2816
DEPTH = 2
DT = D // P
ST = SEQ // P
FT = FF // P
EPS = 1e-6

HEADS_A = 4
DQK = 128
DV = 256
TAPS = 5
SPAN = 36
BACK = 32

HEADS_B = 16
DH = 64
HALF = 64
PAIRS = HEADS_B // 2
PAIRS_A_PASS = PAIRS // 2
NPASS = 2
VCOLS = D // NPASS
FAR = 1e30
OC = DH + 2


class Stage:

    def __init__(self, name, tensor, chunks, cols, skip=0):
        self.name, self.tensor, self.chunks, self.cols, self.skip = name, tensor, chunks, cols, skip
        self.first = 0


UP_COLS = 2 * DT * P
DOWN_HALF = FT // 2
DOWN_COLS = DOWN_HALF * P
TILE_COLS = DT * P
GATE_COLS = DT * P // 2
V_K = 4
V_COLS = V_K * 512


def stages():
    s = [Stage("up0", "w_up0", FT, UP_COLS), Stage("down0", "w_down0", 2 * DT, DOWN_COLS),
         Stage("a_qk", "w_a_qk", 8, TILE_COLS), Stage("a_gates", "w_a_gates", 2, GATE_COLS),
         Stage("a_v", "w_a_v", 4, V_COLS), Stage("a_o", "w_a_o", 8, TILE_COLS),
         Stage("a_out", "w_a_out", DT, TILE_COLS)]
    for n in (1, 2):
        s += [Stage(f"up{n}", f"w_up{n}", FT, UP_COLS), Stage(f"down{n}", f"w_down{n}", 2 * DT, DOWN_COLS)]
    ahead = 6 * (PAIRS_A_PASS + 1)
    s += [Stage("b_v0", "w_b_v", 6, V_COLS), Stage("b_qk0", "w_b_qk", ahead, TILE_COLS),
          Stage("b_v1", "w_b_v", 6, V_COLS, 6), Stage("b_qk1", "w_b_qk", 6 * PAIRS - ahead, TILE_COLS, ahead)]
    s += [Stage("b_out", "w_b_out", DT, TILE_COLS),
          Stage("up3", "w_up3", FT, UP_COLS), Stage("down3", "w_down3", 2 * DT, DOWN_COLS)]
    at = 0
    for x in s:
        x.first = at
        at += x.chunks
    return s, at


STAGES, CHUNKS = stages()
STAGE = {s.name: s for s in STAGES}
COLS = [s.cols for s in STAGES for _ in range(s.chunks)]

NORMS = ["ffn1_0", "mix_0", "ffn2_0", "ffn1_1", "mix_1", "ffn2_1", "final"]
N_NORMS = len(NORMS)

C_ID = 0
C_GAIN = C_ID + P
C_CONVW = C_GAIN + N_NORMS * DT
C_CONVB = C_CONVW + 8 * TAPS
C_HEADG = C_CONVB + 8
C_GATEB = C_HEADG + 8
C_SLOPE = C_GATEB + 1
C_END = C_SLOPE + HEADS_B


def band(si, backward):
    if backward:
        return 0, P * (si + 1), P * si * (si + 1) // 2
    return P * si, SEQ, sum(SEQ - P * j for j in range(si))


BAND_COLS = sum(SEQ - P * j for j in range(ST))


def window(i):
    return min(max(P * i - HALF, 0), SEQ - 2 * P)


class Named:
    pass


def allocate(nc, ctx):
    b = Named()

    def sb(name, shape, dt=F32):
        return ctx.enter_context(nc.sbuf_tensor(name, shape, dt))

    b.x = sb("x", [P, DT, SEQ])
    b.xg_hi = sb("xg_hi", [P, DT, SEQ], F32R)
    b.xg_lo = sb("xg_lo", [P, DT, SEQ], F32R)
    b.raw = sb("raw", [P, 2, UP_COLS])
    b.w_hi = sb("w_hi", [P, 2, UP_COLS], F32R)
    b.w_lo = sb("w_lo", [P, 2, UP_COLS], F32R)
    b.ssq = sb("ssq", [P, SEQ])
    b.xsq = sb("xsq", [P, SEQ])
    b.rinv = sb("rinv", [P, SEQ])
    b.small = sb("small", [P, C_END])
    b.dist1 = sb("dist1", [P, 3, 2 * P])
    b.dist2 = sb("dist2", [P, 1, 2 * P])
    b.ones = sb("ones", [P, 1])
    b.exponent = sb("exponent", [P, 16])
    b.mean_sq = sb("mean_sq", [P, 16])
    b.rsqrt = sb("rsqrt", [P, 16])
    b.newton = sb("newton", [P, 16])
    b.rcol = sb("rcol", [P, 16])

    base = (nc.sbuf_base + 63) // 64 * 64
    room = nc.sbuf_usable_end - base - 64
    sb("shared", [P, room // 4])

    at = [0]

    def place(name, shape, dt=F32):
        t = nc.alloc_sbuf_tensor_at(name, shape, dt, offset=base + at[0])
        at[0] += (4 * int(np.prod(shape[1:])) + 63) // 64 * 64
        assert at[0] <= room, (name, at, room)
        return t

    at[0] = 0
    b.h_hi = place("h_hi", [P, FT, SEQ], F32R)
    b.h_lo = place("h_lo", [P, FT, SEQ], F32R)
    b.gate = place("gate", [P, 1, SEQ])
    b.up = place("up", [P, 1, SEQ])
    b.silu = place("silu", [P, 1, SEQ])
    b.h = place("h", [P, 1, SEQ])
    at[0] = 0
    b.out_t = place("out_t", [P, DT, SEQ])
    at[0] = 0
    b.z_hi = place("z_hi", [P, DT, SEQ], F32R)
    b.z_lo = place("z_lo", [P, DT, SEQ], F32R)
    at[0] = 0
    b.qk = place("qk", [P, 2 * HEADS_A, SEQ])
    b.v = place("v", [P, ST, D])
    b.y = place("y", [P, DT, SEQ])
    b.p = place("p", [P, 2, BAND_COLS])
    b.wt = place("wt", [P, 2, SEQ])
    b.ysq = place("ysq", [P, HEADS_A, SEQ])
    b.part = place("part", [P, 2, SEQ])
    b.dbc = place("dbc", [P, SEQ])
    b.padded = place("padded", [P, SEQ + TAPS - 1])
    b.conv = place("conv", [P, SEQ])
    b.gates = place("gates", [P, SEQ])
    b.fg = place("fg", [P, SEQ])
    b.soft = place("soft", [P, SEQ])
    b.logf = place("logf", [P, SEQ])
    b.bsum = place("bsum", [P, SEQ])
    b.arow = place("arow", [P, SEQ])
    b.mrow = place("mrow", [P, SEQ])
    b.floor = place("floor", [P, SEQ])
    b.afcol = place("afcol", [P, 2, ST, SPAN])
    b.dcol = place("dcol", [P, 4])
    b.rden = place("rden", [P, 2, 4])
    at[0] = 0
    b.v1 = place("v1", [P, ST, VCOLS])
    b.v2 = place("v2", [P, ST, VCOLS])
    b.v3 = place("v3", [P, ST, VCOLS])
    b.vs = place("vs", [P, ST - 1, VCOLS])
    b.qkb = place("qkb", [P, 2, 6, SEQ])
    b.yb_hi = place("yb_hi", [P, DT, SEQ], F32R)
    b.yb_lo = place("yb_lo", [P, DT, SEQ], F32R)
    b.o1 = place("o1", [P, ST, 2, OC])
    b.o2 = place("o2", [P, ST, 2, OC])
    b.o2t = place("o2t", [P, ST, 2, OC])
    b.neg = place("neg", [P, SEQ])
    b.prob = place("prob", [P, SEQ])
    b.prob_t = place("prob_t", [P, SEQ])
    b.mn = place("mn", [P, 8])
    b.wg = place("wg", [P, 2, 8])
    b.wd = place("wd", [P, 2, 8])
    b.den = place("den", [P, 8])
    b.ps = ctx.enter_context(nc.psum_tensor("ps", [P, 8, SEQ], F32))
    return b


def signals(nc, ctx):
    s = Named()

    def sem(name):
        return ctx.enter_context(nc.semaphore(name))

    s.x_landed = sem("x_landed")
    s.small_landed = sem("small_landed")
    s.tables_landed = sem("tables_landed")
    s.w_hi_ready = sem("w_hi_ready")
    s.w_lo_ready = sem("w_lo_ready")
    s.chunk_done = sem("chunk_done")
    s.consts_ready = sem("consts_ready")
    s.x_ready = sem("x_ready")
    s.xg_hi_ready = sem("xg_hi_ready")
    s.xg_lo_ready = sem("xg_lo_ready")
    s.xsq_ready = sem("xsq_ready")
    s.ssq_ready = sem("ssq_ready")
    s.sums_done = sem("sums_done")
    s.mean_ready = sem("mean_ready")
    s.rsqrt_ready = sem("rsqrt_ready")
    s.newton_step = sem("newton_step")
    s.rcol_ready = sem("rcol_ready")
    s.bcast_done = sem("bcast_done")
    s.rinv_ready = sem("rinv_ready")
    s.gate_scaled = sem("gate_scaled")
    s.gu_drained = sem("gu_drained")
    s.silu_ready = sem("silu_ready")
    s.h_ready = sem("h_ready")
    s.h_hi_ready = sem("h_hi_ready")
    s.h_lo_ready = sem("h_lo_ready")
    s.qk_drained = sem("qk_drained")
    s.conv_step = sem("conv_step")
    s.qk_ready = sem("qk_ready")
    s.gates_drained = sem("gates_drained")
    s.gate_step = sem("gate_step")
    s.fg_ready = sem("fg_ready")
    s.exp_ready = sem("exp_ready")
    s.ln_ready = sem("ln_ready")
    s.floor_ready = sem("floor_ready")
    s.cols_done = sem("cols_done")
    s.cols_ready = sem("cols_ready")
    s.v_ready = sem("v_ready")
    s.mrow_bcast = sem("mrow_bcast")
    s.s_done = sem("s_done")
    s.wt_ready = sem("wt_ready")
    s.wt_masked = sem("wt_masked")
    s.p_ready = sem("p_ready")
    s.den_done = sem("den_done")
    s.den_step = sem("den_step")
    s.rden_ready = sem("rden_ready")
    s.dbc_done = sem("dbc_done")
    s.dbc_ready = sem("dbc_ready")
    s.o_done = sem("o_done")
    s.o_drained = sem("o_drained")
    s.y_ready = sem("y_ready")
    s.part_sq_ready = sem("part_sq_ready")
    s.ysq_ready = sem("ysq_ready")
    s.os_ready = sem("os_ready")
    s.og_ready = sem("og_ready")
    s.z_step = sem("z_step")
    s.z_ready = sem("z_ready")
    s.z_hi_ready = sem("z_hi_ready")
    s.z_lo_ready = sem("z_lo_ready")
    s.head_bcast = sem("head_bcast")
    s.bv_ready = sem("bv_ready")
    s.vs_landed = sem("vs_landed")
    s.qkb_ready = sem("qkb_ready")
    s.s2_done = sem("s2_done")
    s.neg_ready = sem("neg_ready")
    s.min_ready = sem("min_ready")
    s.prob_ready = sem("prob_ready")
    s.pt_done = sem("pt_done")
    s.pt_ready = sem("pt_ready")
    s.pv_done = sem("pv_done")
    s.out_ready = sem("out_ready")
    s.o2t_landed = sem("o2t_landed")
    s.mix_step = sem("mix_step")
    s.mix_exp = sem("mix_exp")
    s.mix_ready = sem("mix_ready")
    s.yt_done = sem("yt_done")
    s.yb_hi_ready = sem("yb_hi_ready")
    s.yb_lo_ready = sem("yb_lo_ready")
    s.final_ready = sem("final_ready")
    s.stored = sem("stored")
    s.raw_landed = [sem(f"raw_landed{slot}") for slot in range(2)]
    return s


def event(nu):
    return nu + (nu >= 2)


HEAD_EVENT = 2

UNITS = [(o, hd, tp) for o in (1, 0) for tp in (0, 1) for hd in (0, 1)]
SLOTS = [(0, 1), (2, 3), (4, 5), (6, 7), (8,), (9,)]


def order_2(ap, r):
    return ap[:, r::ST]


def build(nc, d):
    with ExitStack() as ctx:
        b = allocate(nc, ctx)
        s = signals(nc, ctx)
        block = ctx.enter_context(nc.Block())

        @block.sync
        def _(sp):
            sync_program(sp, b, s, d)

        @block.scalar
        def _(act):
            scalar_program(act, b, s)

        @block.vector
        def _(dve):
            vector_program(dve, b, s)

        @block.tensor
        def _(pe):
            tensor_program(pe, b, s)

        @block.gpsimd
        def _(pool):
            gpsimd_program(pool, b, s)


def sync_program(sp, b, s, d):
    sp.dma_start(b.small[:, :], d["small"]).then_inc(s.small_landed, 16)
    for m in range(DT):
        sp.dma_start(b.x[:, m, :], d["x_t"][m]).then_inc(s.x_landed, 16)

    def load(stage, c, g, slot, wait=True):
        if wait:
            sp.wait_ge(s.w_lo_ready, g - 1)
        src = d[stage.tensor][bass.ds(c + stage.skip, 1)].rearrange("a p c -> p (a c)")
        sp.dma_start(b.raw[:, slot, 0:stage.cols], src).then_inc(s.raw_landed[slot], 16)

    for stage in STAGES:
        start = 0
        if stage.first == 0:
            for j in range(2):
                load(stage, j, j, j, wait=False)
            sp.dma_start(b.dist1[:, :, :], d["dist1"]).then_inc(s.tables_landed, 16)
            sp.dma_start(b.dist2[:, :, :], d["dist2"]).then_inc(s.tables_landed, 16)
            start = 1
        if stage.chunks == 2:
            for j in range(2):
                load(stage, j, stage.first + j, j)
            continue
        with sp.Fori(start, stage.chunks // 2) as i:
            for j in range(2):
                load(stage, i * 2 + j, i * 2 + (stage.first + j), j)

    for m in range(DT):
        sp.wait_ge(s.final_ready, m + 1)
        sp.dma_start(d["out_t"][m], b.out_t[:, m, :]).then_inc(s.stored, 16)
    sp.wait_ge(s.stored, 16 * DT)


def scalar_program(act, b, s):

    def split(g, slot, cols, landed):
        act.wait_ge(s.raw_landed[slot], landed)
        if not (isinstance(g, int) and g < 2):
            act.wait_ge(s.chunk_done, g - 1)
        act.activation(b.w_hi[:, slot, 0:cols], b.raw[:, slot, 0:cols], ACT.Copy).then_inc(s.w_hi_ready, 1)

    def split_ahead(g):
        if g + 2 < CHUNKS:
            split(g + 2, g % 2, COLS[g + 2], 16 * ((g + 2) // 2 + 1))

    def update(nu, m):
        if nu == 0:
            act.wait_ge(s.x_landed, 16 * DT)
        else:
            act.wait_ge(s.x_ready, DT * (nu - 1) + m + 1)
        if nu < N_NORMS - 1:
            g = C_GAIN + nu * DT + m
            act.activation(b.xg_hi[:, m, :], b.x[:, m, :], ACT.Copy,
                           scale=b.small[:, g:g + 1]).then_inc(s.xg_hi_ready, 1)
        if nu + m:
            act.wait_ge(s.ssq_ready, DT * nu + m)
        act.activation(b.xsq[:, :], b.x[:, m, :], ACT.Square).then_inc(s.xsq_ready, 1)

    def up(n):
        stage, hidden = STAGE[f"up{n}"], FT * n

        def silu(c):
            act.wait_ge(s.gate_scaled, hidden + c + 1)
            act.activation(b.silu[:, 0, :], b.gate[:, 0, :], ACT.Silu).then_inc(s.silu_ready, 1)

        with act.Fori(0, FT // 2 - 1) as i:
            for j in range(2):
                split(i * 2 + (stage.first + j + 2), j, UP_COLS, i * 16 + 16 * (stage.first // 2 + 2))
                silu(i * 2 + j)
        for c in (FT - 2, FT - 1):
            split_ahead(stage.first + c)
            silu(c)

    def down(n, nu):
        stage = STAGE[f"down{n}"]
        for m in range(DT):
            split_ahead(stage.first + 2 * m)
            split_ahead(stage.first + 2 * m + 1)
            update(nu, m)

    def out_projection(name, nu):
        stage = STAGE[name]
        for m in range(DT):
            split_ahead(stage.first + m)
            update(nu, m)

    def mlstm():
        stage = STAGE["a_qk"]
        for c in range(8):
            split_ahead(stage.first + c)
            for t in {0: (), 1: (0, 1)}.get(c, (c,)):
                act.wait_ge(s.conv_step, TAPS * (t + 1))
                bias = b.small[:, C_CONVB + t:C_CONVB + t + 1]
                act.activation(b.qk[:, t, :], b.conv[:, :], ACT.Silu, bias=bias).then_inc(s.qk_ready, 1)
        for c in range(2):
            split_ahead(STAGE["a_gates"].first + c)
        act.wait_ge(s.gate_step, 3)
        act.activation(b.fg[0:SPAN, :], b.gates[64:64 + SPAN, :], ACT.Copy).then_inc(s.fg_ready, 1)
        act.wait_ge(s.gate_step, 4)
        act.activation(b.soft[0:SPAN, :], b.soft[0:SPAN, :], ACT.Exp).then_inc(s.exp_ready, 1)
        act.wait_ge(s.exp_ready, 1)
        act.activation(b.soft[0:SPAN, :], b.soft[0:SPAN, :], ACT.Ln, bias=1.0).then_inc(s.ln_ready, 1)
        for c in range(4):
            split_ahead(STAGE["a_v"].first + c)
            if c == 0:
                act.wait_ge(s.gate_step, 12)
                act.activation(b.floor[0:SPAN, :], b.floor[0:SPAN, :], ACT.Exp,
                               scale=-1.0).then_inc(s.floor_ready, 1)
            if c % 2:
                act.wait_ge(s.chunk_done, STAGE["a_v"].first + c + 1)
                for i in range(ST):
                    bank = i if c == 3 else 4 + i
                    cols = slice(512 * (c // 2), 512 * (c // 2) + 512)
                    act.activation(b.v[:, i, cols], b.ps[:, bank, :], ACT.Copy,
                                   scale=b.rcol[:, i:i + 1]).then_inc(s.v_ready, 1)

        def weights(u):
            h, backward = u // 2, u % 2
            row = h + BACK * backward
            act.wait_ge(s.mrow_bcast, u + 1)
            if u == 0:
                act.wait_ge(s.cols_ready, 1)
            for j in range(ST):
                si, n = (ST - 1 - j if backward else j), ST * u + j
                lo, hi, _ = band(si, backward)
                if n >= 2:
                    act.wait_ge(s.p_ready, n - 1)
                act.activation(b.wt[:, n % 2, lo:hi], b.ps[:, u % 2, lo:hi], ACT.Exp,
                               bias=b.afcol[:, 0, si, row:row + 1]).then_inc(s.wt_ready, 1)

        weights(0)
        for u in range(2 * HEADS_A + 1):
            if u and u % 2 == 0:
                h = u // 2 - 1
                act.wait_ge(s.y_ready, h + 1)
                act.activation(b.part[:, :, :], b.y[:, 2 * h:2 * h + 2, :], ACT.Square).then_inc(s.part_sq_ready, 1)
            if u + 1 < 2 * HEADS_A:
                weights(u + 1)
        stage = STAGE["a_o"]
        for c in range(8):
            split_ahead(stage.first + c)
            for t in {0: (), 1: (0, 1)}.get(c, (c,)):
                act.wait_ge(s.os_ready, t + 1)
                act.activation(b.part[:, 1, :], b.part[:, 0, :], ACT.Sigmoid).then_inc(s.og_ready, 1)
                act.wait_ge(s.z_ready, t + 1)
                act.activation(b.z_hi[:, t, :], b.dbc[:, :], ACT.Copy).then_inc(s.z_hi_ready, 1)

    def b_values(pas):
        stage = STAGE[f"b_v{pas}"]
        for c in range(6):
            split_ahead(stage.first + c)
            if c % 2:
                group = c // 2
                v = (b.v1, b.v2, b.v3)[group]
                act.wait_ge(s.chunk_done, stage.first + c + 1)
                if pas and group == 0:
                    act.wait_ge(s.pv_done, 8 * PAIRS_A_PASS)
                if pas == 0 and group == 0:
                    act.wait_ge(s.rcol_ready, event(4) + 1)
                for i in range(ST):
                    col = i + (ST if group else 0)
                    act.activation(v[:, i, :], b.ps[:, 4 * (group % 2) + i, :], ACT.Copy,
                                   scale=b.rcol[:, col:col + 1]).then_inc(s.bv_ready, 1)

    def b_slot(pair, k):
        n = 8 * pair + k
        if k < 8:
            o, hd, tp = UNITS[k]
            ob = (b.o1, b.o2)[o]
            act.wait_ge(s.min_ready, n + 1)
            if n:
                act.wait_ge(s.pt_done, n)
            for t in range(2):
                i = 2 * tp + t
                act.activation(b.prob[:, 256 * t:256 * t + 256], b.neg[:, 256 * t:256 * t + 256], ACT.Exp,
                               bias=ob[:, i, hd, DH + 1:DH + 2], scale=-1.0,
                               accum_out=ob[:, i, hd, DH:DH + 1]).then_inc(s.prob_ready, 1)
        if 1 <= k <= 8:
            act.wait_ge(s.pt_done, n)
            if n >= 2:
                act.wait_ge(s.pv_done, n - 1)
            act.activation(b.prob_t[:, :], b.ps[:, 4 + (n - 1) % 2, :], ACT.Copy).then_inc(s.pt_ready, 1)

    def b_mix(pair):
        act.wait_ge(s.mix_step, 9 * pair + 3)
        act.activation(b.wg[:, :, :], b.wg[:, :, :], ACT.Exp).then_inc(s.mix_exp, 1)

    def b_finish(pair):
        act.wait_ge(s.yt_done, pair + 1)
        act.activation(b.yb_hi[:, pair, :], b.ps[:, 7, :], ACT.Copy).then_inc(s.yb_hi_ready, 1)

    def b_pair(first, attend):
        for c in range(6):
            if first is not None:
                split_ahead(first + c)
            if attend is not None:
                for k in SLOTS[c]:
                    b_slot(attend, k)
                if c == 0 and attend:
                    b_finish(attend - 1)
        if attend is not None:
            b_mix(attend)

    def dilated():
        b_values(0)
        qk0, qk1 = STAGE["b_qk0"].first, STAGE["b_qk1"].first
        b_pair(qk0, None)
        for pair in range(PAIRS_A_PASS):
            b_pair(qk0 + 6 * (pair + 1), pair)
        b_values(1)
        for pair in range(PAIRS_A_PASS, PAIRS):
            b_pair(qk1 + 6 * (pair - PAIRS_A_PASS) if pair < PAIRS - 1 else None, pair)
        b_finish(PAIRS - 1)

    act.wait_ge(s.small_landed, 16)
    for m in range(DT):
        update(0, m)
    for g in range(2):
        split(g, g, COLS[g], 16)
    up(0)
    down(0, 1)
    mlstm()
    out_projection("a_out", 2)
    up(1)
    down(1, 3)
    up(2)
    down(2, 4)
    dilated()
    out_projection("b_out", 5)
    up(3)
    down(3, 6)


def vector_program(dve, b, s):

    def split(g, slot, cols):
        dve.wait_ge(s.w_hi_ready, g + 1)
        dve.tensor_tensor(b.w_lo[:, slot, 0:cols], b.raw[:, slot, 0:cols],
                          b.w_hi[:, slot, 0:cols].bitcast(F32), ALU.subtract).then_inc(s.w_lo_ready, 1)

    def split_ahead(g):
        if g + 2 < CHUNKS:
            split(g + 2, g % 2, COLS[g + 2])

    def update(nu, m, bank=None, scale=1.0, done=None):
        x = b.x[:, m, :]
        if bank is not None:
            dve.wait_ge(s.chunk_done, done)
            dve.scalar_tensor_tensor(out=x, in0=b.ps[:, bank, :], scalar=scale, in1=x,
                                     op0=ALU.mult, op1=ALU.add).then_inc(s.x_ready, 1)
        if nu < N_NORMS - 1:
            g = C_GAIN + nu * DT + m
            dve.wait_ge(s.xg_hi_ready, DT * nu + m + 1)
            dve.scalar_tensor_tensor(out=b.xg_lo[:, m, :], in0=x, scalar=b.small[:, g:g + 1],
                                     in1=b.xg_hi[:, m, :].bitcast(F32), op0=ALU.mult,
                                     op1=ALU.subtract).then_inc(s.xg_lo_ready, 1)
        dve.wait_ge(s.xsq_ready, DT * nu + m + 1)
        if m == 0:
            dve.tensor_copy(b.ssq[:, :], b.xsq[:, :]).then_inc(s.ssq_ready, 1)
        else:
            dve.wait_ge(s.ssq_ready, DT * nu + m)
            dve.tensor_tensor(b.ssq[:, :], b.ssq[:, :], b.xsq[:, :], ALU.add).then_inc(s.ssq_ready, 1)

    def rsqrt_columns(e, cols, n):
        ms, rs, nt = b.mean_sq[:, 0:cols], b.rsqrt[:, 0:cols], b.newton[:, 0:cols]
        dve.wait_ge(s.sums_done, e + 1)
        dve.tensor_scalar(ms, b.ps[:, 6, 0:cols], 1.0 / n, EPS, ALU.mult, ALU.add).then_inc(s.mean_ready, 1)
        dve.wait_ge(s.rsqrt_ready, e + 1)
        dve.tensor_tensor(nt, ms, rs, ALU.mult).then_inc(s.newton_step, 1)
        dve.wait_ge(s.newton_step, 3 * e + 1)
        dve.tensor_tensor(nt, nt, rs, ALU.mult).then_inc(s.newton_step, 1)
        dve.wait_ge(s.newton_step, 3 * e + 2)
        dve.tensor_scalar(nt, nt, -0.5, 1.5, ALU.mult, ALU.add).then_inc(s.newton_step, 1)
        dve.wait_ge(s.newton_step, 3 * e + 3)
        dve.tensor_tensor(b.rcol[:, 0:cols], rs, nt, ALU.mult).then_inc(s.rcol_ready, 1)

    def keep_rinv(nu):
        dve.wait_ge(s.bcast_done, nu + 1)
        dve.tensor_copy(b.rinv[:, :], b.ps[:, 7, :]).then_inc(s.rinv_ready, 1)

    def up(n, nu):
        stage, hidden = STAGE[f"up{n}"], FT * n

        def evict(c, par):
            dve.wait_ge(s.chunk_done, c + (stage.first + 1))
            dve.wait_ge(s.rinv_ready, nu + 1)
            dve.tensor_tensor(b.gate[:, 0, :], b.ps[:, 2 * par, :], b.rinv[:, :], ALU.mult).then_inc(s.gate_scaled, 1)
            dve.tensor_tensor(b.up[:, 0, :], b.ps[:, 2 * par + 1, :], b.rinv[:, :], ALU.mult).then_inc(s.gu_drained, 1)
            dve.wait_ge(s.gu_drained, c + (hidden + 1))
            dve.wait_ge(s.silu_ready, c + (hidden + 1))
            dve.tensor_tensor(b.h[:, 0, :], b.silu[:, 0, :], b.up[:, 0, :], ALU.mult).then_inc(s.h_ready, 1)
            tile = bass.ds(c, 1)
            dve.wait_ge(s.h_ready, c + (hidden + 1))
            dve.tensor_copy(b.h_hi[:, tile, :], b.h[:, :, :]).then_inc(s.h_hi_ready, 1)
            dve.wait_ge(s.h_hi_ready, c + (hidden + 1))
            dve.tensor_tensor(b.h_lo[:, tile, :], b.h[:, :, :], b.h_hi[:, tile, :].bitcast(F32),
                              ALU.subtract).then_inc(s.h_lo_ready, 1)

        rsqrt_columns(event(nu), ST, D)
        keep_rinv(nu)
        with dve.Fori(0, FT // 2 - 1) as i:
            for j in range(2):
                split(i * 2 + (stage.first + j + 2), j, UP_COLS)
                evict(i * 2 + j, j)
        for c in (FT - 2, FT - 1):
            split_ahead(stage.first + c)
            evict(c, c % 2)

    def down(n, nu):
        stage = STAGE[f"down{n}"]
        for m in range(DT):
            split_ahead(stage.first + 2 * m)
            split_ahead(stage.first + 2 * m + 1)
            update(nu, m, 4 + m % 2, 0.5, stage.first + 2 * m + 2)

    def out_projection(name, nu):
        stage = STAGE[name]
        for m in range(DT):
            split_ahead(stage.first + m)
            update(nu, m, 4 + m % 2, 1.0, stage.first + m + 1)

    def mlstm():
        nu = 1
        stage = STAGE["a_qk"]
        dve.memset(b.padded[:, :], 0.0)

        def convolve(t):
            step = TAPS * t
            dve.wait_ge(s.chunk_done, stage.first + t + 1)
            if t:
                dve.wait_ge(s.conv_step, step)
            dve.tensor_tensor(b.padded[:, 2:2 + SEQ], b.ps[:, t % 4, :], b.rinv[:, :], ALU.mult).then_inc(s.qk_drained, 1)
            dve.wait_ge(s.qk_drained, t + 1)
            if t:
                dve.wait_ge(s.qk_ready, t)
            for k in range(TAPS):
                w = b.small[:, C_CONVW + TAPS * t + k:C_CONVW + TAPS * t + k + 1]
                src = b.padded[:, k:k + SEQ]
                if k == 0:
                    dve.tensor_scalar(b.conv[:, :], src, w, None, ALU.mult).then_inc(s.conv_step, 1)
                else:
                    dve.wait_ge(s.conv_step, step + k)
                    dve.scalar_tensor_tensor(out=b.conv[:, :], in0=src, scalar=w, in1=b.conv[:, :],
                                             op0=ALU.mult, op1=ALU.add).then_inc(s.conv_step, 1)

        for c in range(8):
            split_ahead(stage.first + c)
            if c == 0:
                rsqrt_columns(event(nu), ST, D)
            elif c == 1:
                keep_rinv(nu)
                dve.wait_ge(s.rinv_ready, nu + 1)
                convolve(0)
                convolve(1)
            else:
                convolve(c)
        gates_stage = STAGE["a_gates"]
        for c in range(2):
            split_ahead(gates_stage.first + c)
        fwd, bwd, rows = slice(0, HEADS_A), slice(BACK, SPAN), slice(0, SPAN)
        dve.memset(b.bsum[rows, :], 0.0).then_inc(s.gate_step, 1)
        dve.memset(b.mrow[rows, :], 0.0).then_inc(s.gate_step, 1)
        dve.wait_ge(s.chunk_done, gates_stage.first + 2)
        dve.tensor_tensor(b.gates[:, :], b.ps[:, 2, :], b.rinv[:, :], ALU.mult).then_inc(s.gates_drained, 1)
        dve.wait_ge(s.gates_drained, 1)
        dve.tensor_scalar(b.gates[:, :], b.gates[:, :], b.small[:, C_GATEB:C_GATEB + 1], None,
                          ALU.add).then_inc(s.gate_step, 1)
        dve.wait_ge(s.fg_ready, 1)
        dve.scalar_tensor_tensor(out=b.soft[rows, :], in0=b.fg[rows, :], scalar=-1.0, in1=b.fg[rows, :],
                                 op0=ALU.mult, op1=ALU.min).then_inc(s.gate_step, 1)
        dve.wait_ge(s.ln_ready, 1)
        dve.scalar_tensor_tensor(out=b.logf[rows, :], in0=b.fg[rows, :], scalar=0.0, in1=b.soft[rows, :],
                                 op0=ALU.min, op1=ALU.subtract).then_inc(s.gate_step, 1)
        dve.wait_ge(s.gate_step, 5)
        dve.tensor_tensor_scan(b.bsum[fwd, :], b.logf[fwd, :], b.logf[fwd, :], 0.0, ALU.add,
                               ALU.bypass).then_inc(s.gate_step, 1)
        dve.tensor_tensor_scan(b.bsum[bwd, ::-1], b.logf[bwd, ::-1], b.logf[bwd, ::-1], 0.0, ALU.add,
                               ALU.bypass).then_inc(s.gate_step, 1)
        dve.wait_ge(s.gate_step, 7)
        dve.tensor_tensor(b.arow[rows, :], b.gates[rows, :], b.bsum[rows, :], ALU.subtract).then_inc(s.gate_step, 1)
        dve.wait_ge(s.gate_step, 8)
        dve.tensor_tensor_scan(b.mrow[fwd, :], b.arow[fwd, :], b.arow[fwd, :], 0.0, ALU.max,
                               ALU.max).then_inc(s.gate_step, 1)
        dve.tensor_tensor_scan(b.mrow[bwd, ::-1], b.arow[bwd, ::-1], b.arow[bwd, ::-1], 0.0, ALU.max,
                               ALU.max).then_inc(s.gate_step, 1)
        dve.wait_ge(s.gate_step, 10)
        dve.tensor_tensor(b.floor[rows, :], b.bsum[rows, :], b.mrow[rows, :], ALU.add).then_inc(s.gate_step, 1)
        dve.wait_ge(s.gate_step, 11)
        dve.tensor_scalar(b.mrow[rows, :], b.mrow[rows, :], -1.0, None, ALU.mult).then_inc(s.gate_step, 1)
        for c in range(4):
            split_ahead(STAGE["a_v"].first + c)
        dve.wait_ge(s.cols_done, 1)
        dve.tensor_copy(b.afcol[:, :, :, :], b.ps[:, 6, 0:2 * ST * SPAN].rearrange(
            "p (k i r) -> p k i r", k=2, i=ST)).then_inc(s.cols_ready, 1)

        def products(u):
            backward = u % 2
            if u >= 2:
                dve.wait_ge(s.o_done, u - 1)
            for j in range(ST):
                si, n = (ST - 1 - j if backward else j), ST * u + j
                lo, hi, at = band(si, backward)
                dve.wait_ge(s.wt_masked, n + 1)
                dve.wait_ge(s.s_done, n + 1)
                dve.scalar_tensor_tensor(out=b.p[:, u % 2, at:at + hi - lo], in0=b.ps[:, 2 + n % 2, lo:hi],
                                         scalar=DQK ** -0.5, in1=b.wt[:, n % 2, lo:hi], op0=ALU.mult,
                                         op1=ALU.mult).then_inc(s.p_ready, 1)

        def denominators(u):
            row = u // 2 + BACK * (u % 2)
            den = b.ps[:, 6, 320 + ST * u:320 + ST * u + ST]
            dve.wait_ge(s.den_done, u + 1)
            dve.scalar_tensor_tensor(out=b.dcol[:, :], in0=den, scalar=-1.0, in1=b.afcol[:, 1, :, row],
                                     op0=ALU.mult, op1=ALU.max).then_inc(s.den_step, 1)
            dve.wait_ge(s.den_step, 2 * u + 1)
            dve.tensor_tensor(b.dcol[:, :], den, b.dcol[:, :], ALU.max).then_inc(s.den_step, 1)
            dve.wait_ge(s.den_step, 2 * u + 2)
            dve.reciprocal(b.rden[:, u % 2, :], b.dcol[:, :]).then_inc(s.rden_ready, 1)

        def evict(u):
            h, backward = u // 2, u % 2
            dve.wait_ge(s.dbc_done, u + 1)
            dve.tensor_copy(b.dbc[:, :], b.ps[:, 7, :]).then_inc(s.dbc_ready, 1)
            dve.wait_ge(s.dbc_ready, u + 1)
            dve.wait_ge(s.o_done, u + 1)
            y = b.y[:, 2 * h:2 * h + 2, :]
            out = b.part if backward else y
            if backward and h:
                dve.wait_ge(s.ysq_ready, h)
            for e in range(2):
                ins = dve.tensor_tensor(out[:, e, :], b.ps[:, 4 + e, :], b.dbc[:, :], ALU.mult)
            ins.then_inc(s.o_drained, 1)
            if backward:
                dve.wait_ge(s.o_drained, u + 1)
                dve.tensor_tensor(y, y, b.part[:, :, :], ALU.add).then_inc(s.y_ready, 1)

        def head_squares(h):
            dve.wait_ge(s.part_sq_ready, h + 1)
            dve.tensor_tensor(b.ysq[:, h, :], b.part[:, 0, :], b.part[:, 1, :], ALU.add).then_inc(s.ysq_ready, 1)

        products(0)
        for u in range(2 * HEADS_A + 1):
            if u:
                evict(u - 1)
            if u + 1 < 2 * HEADS_A:
                products(u + 1)
            if u and u % 2 == 0:
                head_squares(u // 2 - 1)
            if u < 2 * HEADS_A:
                denominators(u)

        stage = STAGE["a_o"]

        def gated(t):
            dve.wait_ge(s.chunk_done, stage.first + t + 1)
            if t:
                dve.wait_ge(s.z_step, t)
            dve.tensor_tensor(b.part[:, 0, :], b.ps[:, t % 4, :], b.rinv[:, :], ALU.mult).then_inc(s.os_ready, 1)
            dve.wait_ge(s.og_ready, t + 1)
            if t:
                dve.wait_ge(s.z_lo_ready, t)
            dve.scalar_tensor_tensor(out=b.dbc[:, :], in0=b.part[:, 1, :],
                                     scalar=b.small[:, C_HEADG + t:C_HEADG + t + 1], in1=b.y[:, t, :],
                                     op0=ALU.mult, op1=ALU.mult).then_inc(s.z_step, 1)
            dve.wait_ge(s.z_step, t + 1)
            dve.wait_ge(s.head_bcast, t // 2 + 1)
            dve.tensor_tensor(b.dbc[:, :], b.ps[:, 7, :], b.dbc[:, :], ALU.mult).then_inc(s.z_ready, 1)
            dve.wait_ge(s.z_hi_ready, t + 1)
            dve.tensor_tensor(b.z_lo[:, t, :], b.dbc[:, :], b.z_hi[:, t, :].bitcast(F32),
                              ALU.subtract).then_inc(s.z_lo_ready, 1)

        for c in range(8):
            split_ahead(stage.first + c)
            if c == 0:
                rsqrt_columns(HEAD_EVENT, ST * HEADS_A, DV)
            elif c == 1:
                gated(0)
                gated(1)
            else:
                gated(c)

    def b_values(pas):
        stage = STAGE[f"b_v{pas}"]
        for c in range(6):
            split_ahead(stage.first + c)
            if pas == 0 and c == 0:
                rsqrt_columns(event(4), 2 * ST, D)
            if pas == 0 and c == 1:
                keep_rinv(4)

    def b_slot(pair, k):
        n = 8 * pair + k
        if k < 8:
            o, hd, tp = UNITS[k]
            ob = (b.o1, b.o2)[o]
            head = 2 * pair + hd
            dist = b.dist2[:, :, :].to_broadcast([P, 2, 2 * P]) if o else b.dist1[:, tp:tp + 2, :]
            dve.wait_ge(s.s2_done, n + 1)
            if n:
                dve.wait_ge(s.prob_ready, 2 * n)
            neg = b.neg[:, :].rearrange("p (t k) -> p t k", t=2)
            dve.scalar_tensor_tensor(out=neg, in0=dist, scalar=b.small[:, C_SLOPE + head:C_SLOPE + head + 1],
                                     in1=b.ps[:, 2 + hd, :].rearrange("p (t k) -> p t k", t=2),
                                     op0=ALU.mult, op1=ALU.subtract).then_inc(s.neg_ready, 1)
            dve.wait_ge(s.neg_ready, n + 1)
            dve.tensor_reduce(ob[:, 2 * tp:2 * tp + 2, hd, DH + 1:DH + 2], neg, AX.X, ALU.min).then_inc(s.min_ready, 1)
        if k >= 2:
            o, hd, tp = UNITS[k - 2]
            ob = (b.o1, b.o2)[o]
            dve.wait_ge(s.pv_done, n - 1)
            half = 128 * (k % 2)
            dve.tensor_copy(ob[:, 2 * tp:2 * tp + 2, hd, 0:DH], b.ps[:, 6, half:half + 128].rearrange(
                "p (t d) -> p t d", t=2)).then_inc(s.out_ready, 1)

    def b_mix(pair):
        step = 9 * pair
        o1 = b.o1[:, :, :, :].rearrange("p i h c -> p (i h) c")
        o2 = b.o2t[:, :, :, :].rearrange("p i h c -> p (i h) c")

        def flat(ap, c):
            return ap[:, :, c]

        dve.wait_ge(s.o2t_landed, 64 * (pair + 1))
        dve.wait_ge(s.prob_ready, 16 * (pair + 1))
        dve.tensor_tensor(b.mn[:, :], flat(o1, DH + 1), flat(o2, DH + 1), ALU.min).then_inc(s.mix_step, 1)
        dve.wait_ge(s.mix_step, step + 1)
        for k, o in enumerate((o1, o2)):
            dve.tensor_tensor(b.wg[:, k, :], b.mn[:, :], flat(o, DH + 1), ALU.subtract).then_inc(s.mix_step, 1)
        dve.wait_ge(s.mix_exp, pair + 1)
        for k, o in enumerate((o1, o2)):
            dve.tensor_tensor(b.wd[:, k, :], b.wg[:, k, :], flat(o, DH), ALU.mult).then_inc(s.mix_step, 1)
        dve.wait_ge(s.mix_step, step + 5)
        dve.tensor_tensor(b.den[:, :], b.wd[:, 0, :], b.wd[:, 1, :], ALU.add).then_inc(s.mix_step, 1)
        dve.wait_ge(s.mix_step, step + 6)
        dve.reciprocal(b.den[:, :], b.den[:, :]).then_inc(s.mix_step, 1)
        dve.wait_ge(s.mix_step, step + 7)
        den = b.den[:, :].unsqueeze(1).to_broadcast([P, 2, 8])
        dve.tensor_tensor(b.wg[:, :, :], b.wg[:, :, :], den, ALU.mult).then_inc(s.mix_step, 1)
        dve.wait_ge(s.mix_step, step + 8)
        if pair:
            dve.wait_ge(s.yt_done, pair)
        for k, (o, out) in enumerate(((o1, b.ssq), (o2, b.xsq))):
            w = b.wg[:, k, :].unsqueeze(2).to_broadcast([P, 8, DH])
            ins = dve.tensor_tensor(out[:, :].rearrange("p (g d) -> p g d", g=8), o[:, :, 0:DH], w, ALU.mult)
        ins.then_inc(s.mix_step, 1)
        dve.wait_ge(s.mix_step, step + 9)
        dve.tensor_tensor(b.ssq[:, :], b.ssq[:, :], b.xsq[:, :], ALU.add).then_inc(s.mix_ready, 1)

    def b_finish(pair):
        dve.wait_ge(s.yb_hi_ready, pair + 1)
        dve.tensor_tensor(b.yb_lo[:, pair, :], b.ps[:, 7, :], b.yb_hi[:, pair, :].bitcast(F32),
                          ALU.subtract).then_inc(s.yb_lo_ready, 1)

    def b_pair(first, attend, project):
        for c in range(6):
            if first is not None:
                split_ahead(first + c)
                dve.wait_ge(s.chunk_done, first + c + 1)
                if project >= 2 and c == 0:
                    dve.wait_ge(s.s2_done, 8 * (project - 1))
                out, src, rinv = b.qkb[:, project % 2, c, :], b.ps[:, c % 2, :], b.rinv[:, :]
                if c >= 2:
                    out = out.rearrange("p (r j) -> p j r", r=ST)
                    src, rinv = (a.rearrange("p (j r) -> p j r", r=ST) for a in (src, rinv))
                if c % 2 == 0:
                    dve.scalar_tensor_tensor(out=out, in0=src, scalar=DH ** -0.5, in1=rinv, op0=ALU.mult,
                                             op1=ALU.mult).then_inc(s.qkb_ready, 1)
                else:
                    dve.tensor_tensor(out, src, rinv, ALU.mult).then_inc(s.qkb_ready, 1)
            if attend is not None:
                for k in SLOTS[c]:
                    b_slot(attend, k)
                if c == 0 and attend:
                    b_finish(attend - 1)
        if attend is not None:
            b_mix(attend)

    def dilated():
        b_values(0)
        dve.wait_ge(s.rinv_ready, 5)
        dve.wait_ge(s.tables_landed, 32)
        qk0, qk1 = STAGE["b_qk0"].first, STAGE["b_qk1"].first
        b_pair(qk0, None, 0)
        for pair in range(PAIRS_A_PASS):
            b_pair(qk0 + 6 * (pair + 1), pair, pair + 1)
        b_values(1)
        for pair in range(PAIRS_A_PASS, PAIRS):
            b_pair(qk1 + 6 * (pair - PAIRS_A_PASS) if pair < PAIRS - 1 else None, pair, pair + 1)
        b_finish(PAIRS - 1)

    def final():
        rsqrt_columns(event(6), ST, D)
        keep_rinv(6)
        dve.wait_ge(s.rinv_ready, 7)
        for m in range(DT):
            g = C_GAIN + 6 * DT + m
            dve.scalar_tensor_tensor(out=b.out_t[:, m, :], in0=b.x[:, m, :], scalar=b.small[:, g:g + 1],
                                     in1=b.rinv[:, :], op0=ALU.mult, op1=ALU.mult).then_inc(s.final_ready, 1)

    dve.memset(b.ones[:, :], 1.0).then_inc(s.consts_ready, 1)
    dve.memset(b.exponent[:, :], -0.5).then_inc(s.consts_ready, 1)
    dve.wait_ge(s.small_landed, 16)
    for m in range(DT):
        update(0, m)
    for g in range(2):
        split(g, g, COLS[g])
    up(0, 0)
    down(0, 1)
    mlstm()
    out_projection("a_out", 2)
    up(1, 2)
    down(1, 3)
    up(2, 3)
    down(2, 4)
    dilated()
    out_projection("b_out", 5)
    up(3, 5)
    down(3, 6)
    final()


def tensor_program(pe, b, s):
    ident = b.small[:, C_ID:C_ID + P]

    def split_matmul(out, a_hi, a_lo, x_hi, x_lo, start, stop):
        pe.matmul(out, a_hi, x_hi, start=start, stop=False)
        pe.matmul(out, a_hi, x_lo, start=False, stop=False)
        return pe.matmul(out, a_lo, x_hi, start=False, stop=stop)

    def weight_tile(slot, n):
        cols = slice(P * n, P * n + P)
        return b.w_hi[:, slot, cols], b.w_lo[:, slot, cols]

    def column_sums(out, rows, tiles=None):
        for i in range(ST):
            lhs = tiles(rows, i) if tiles else rows[:, P * i:P * i + P]
            ins = pe.matmul(out[:, i:i + 1], lhs, b.ones[:, :], start=True, stop=True)
        return ins

    def broadcast(out, cols):
        for i in range(ST):
            ins = pe.matmul(out[:, P * i:P * i + P], cols[:, i:i + 1].to_broadcast([P, P]), ident,
                            start=True, stop=True)
        return ins

    def norm_sums(nu):
        pe.wait_ge(s.ssq_ready, DT * (nu + 1))
        ins = column_sums(b.ps[:, 6, 0:ST], b.ssq[:, :])
        if nu == 4:
            ins = column_sums(b.ps[:, 6, ST:2 * ST], b.ssq[:, :], order_2)
        ins.then_inc(s.sums_done, 1)

    def norm_broadcast(nu):
        pe.wait_ge(s.rcol_ready, event(nu) + 1)
        broadcast(b.ps[:, 7, :], b.rcol[:, 0:ST]).then_inc(s.bcast_done, 1)

    def project(bank, slot, tiles, x_hi, x_lo, first=True, last=True, k0=0, w0=0, ready=None):
        for k in range(tiles):
            if ready is not None:
                pe.wait_ge(ready[0], ready[1] + k0 + k + 1)
            w_hi, w_lo = weight_tile(slot, w0 + k)
            ins = split_matmul(b.ps[:, bank, :], w_hi, w_lo, x_hi[:, k0 + k, :], x_lo[:, k0 + k, :],
                               first and k == 0, last and k == tiles - 1)
        return ins

    def up(n, nu):
        stage, hidden = STAGE[f"up{n}"], FT * n

        def chunk(c, par, first=False):
            pe.wait_ge(s.w_lo_ready, c + (stage.first + 1))
            if not (isinstance(c, int) and c < 2):
                pe.wait_ge(s.gu_drained, c + (hidden - 1))
            ready = (s.xg_lo_ready, DT * nu) if first else None
            project(2 * par, par, DT, b.xg_hi, b.xg_lo, ready=ready)
            if first:
                norm_sums(nu)
            ins = project(2 * par + 1, par, DT, b.xg_hi, b.xg_lo, w0=DT)
            ins.then_inc(s.chunk_done, 1)
            if first:
                norm_broadcast(nu)

        chunk(0, 0, True)
        chunk(1, 1)
        with pe.Fori(1, FT // 2) as i:
            for j in range(2):
                chunk(i * 2 + j, j)

    def down(n, nu):
        stage, hidden = STAGE[f"down{n}"], FT * n

        def pair(m, wait=True):
            for e in range(2):
                if wait:
                    pe.wait_ge(s.x_ready, m + (DT * (nu - 1) + e - 1))
                for half in range(2):
                    pe.wait_ge(s.w_lo_ready, m * 2 + (stage.first + 2 * e + half + 1))
                    pe.wait_ge(s.h_lo_ready, hidden + DOWN_HALF * (half + 1))
                    project(4 + e, half, DOWN_HALF, b.h_hi, b.h_lo, half == 0, half == 1,
                            DOWN_HALF * half).then_inc(s.chunk_done, 1)

        pair(0, False)
        with pe.Fori(1, DT // 2) as i:
            pair(i * 2)

    def out_projection(name, nu, z_hi, z_lo, ready):
        stage = STAGE[name]
        for m in range(DT):
            pe.wait_ge(s.w_lo_ready, stage.first + m + 1)
            if m >= 2:
                pe.wait_ge(s.x_ready, DT * (nu - 1) + m - 1)
            project(4 + m % 2, m % 2, DT, z_hi, z_lo, ready=(ready, 0) if m == 0 else None).then_inc(s.chunk_done, 1)

    def mlstm():
        nu = 1
        stage = STAGE["a_qk"]
        for c in range(8):
            pe.wait_ge(s.w_lo_ready, stage.first + c + 1)
            if c >= 4:
                pe.wait_ge(s.qk_drained, c - 3)
            ready = (s.xg_lo_ready, DT * nu) if c == 0 else None
            project(c % 4, c % 2, DT, b.xg_hi, b.xg_lo, ready=ready).then_inc(s.chunk_done, 1)
            if c == 0:
                norm_sums(nu)
            if c == 1:
                norm_broadcast(nu)
        stage = STAGE["a_gates"]
        pe.wait_ge(s.qk_drained, 7)
        for c in range(2):
            pe.wait_ge(s.w_lo_ready, stage.first + c + 1)
            project(2, c, DT // 2, b.xg_hi, b.xg_lo, c == 0, c == 1, DT // 2 * c).then_inc(s.chunk_done, 1)
        stage = STAGE["a_v"]
        for c in range(4):
            pe.wait_ge(s.w_lo_ready, stage.first + c + 1)
            if c == 0:
                pe.wait_ge(s.rinv_ready, nu + 1)
            if c == 2:
                pe.wait_ge(s.qk_drained, 8)
                pe.wait_ge(s.gates_drained, 1)
            values(c, c % 2, 0 if c >= 2 else 4, None).then_inc(s.chunk_done, 1)
        pe.wait_ge(s.floor_ready, 1)
        pe.wait_ge(s.v_ready, ST)
        for k, rows in enumerate((b.arow, b.floor)):
            for i in range(ST):
                at = (ST * k + i) * SPAN
                ins = pe.transpose(b.ps[:, 6, at:at + SPAN], rows[0:SPAN, P * i:P * i + P], ident[0:SPAN, 0:SPAN])
        ins.then_inc(s.cols_done, 1)

        def scores(u):
            h, backward = u // 2, u % 2
            row = h + BACK * backward
            if u >= 2:
                pe.wait_ge(s.wt_ready, ST * (u - 1))
            pe.matmul(b.ps[:, u % 2, :], ident[0:SPAN, row:row + 1].to_broadcast([SPAN, P]), b.mrow[0:SPAN, :],
                      start=True, stop=True).then_inc(s.mrow_bcast, 1)
            for j in range(ST):
                si, n = (ST - 1 - j if backward else j), ST * u + j
                lo, hi, _ = band(si, backward)
                if n >= 2:
                    pe.wait_ge(s.p_ready, n - 1)
                pe.matmul(b.ps[:, 2 + n % 2, lo:hi], b.qk[:, HEADS_A + h, P * si:P * si + P], b.qk[:, h, lo:hi],
                          start=True, stop=True).then_inc(s.s_done, 1)

        def outputs(u):
            h, backward = u // 2, u % 2
            order = range(ST)[::-1] if backward else range(ST)
            pe.wait_ge(s.p_ready, ST * (u + 1))
            for i in range(ST):
                seen = [si for si in order if (si >= i if backward else si <= i)]
                for si in seen:
                    lo, _, at = band(si, backward)
                    at += P * i - lo
                    col = 320 + ST * u + i
                    ins = pe.matmul(b.ps[:, 6, col:col + 1], b.p[:, u % 2, at:at + P], b.ones[:, :],
                                    start=si == seen[0], stop=si == seen[-1])
            ins.then_inc(s.den_done, 1)
            if u:
                pe.wait_ge(s.o_drained, u)
            for e in range(2):
                for j, si in enumerate(order):
                    lo, hi, at = band(si, backward)
                    v = b.v[:, si, DV * h + P * e:DV * h + P * e + P]
                    ins = pe.matmul(b.ps[:, 4 + e, lo:hi], v, b.p[:, u % 2, at:at + hi - lo],
                                    start=j == 0, stop=j == ST - 1)
            ins.then_inc(s.o_done, 1)

        def spread(u):
            pe.wait_ge(s.rden_ready, u + 1)
            if u:
                pe.wait_ge(s.dbc_ready, u)
            broadcast(b.ps[:, 7, :], b.rden[:, u % 2, :]).then_inc(s.dbc_done, 1)

        pe.wait_ge(s.qk_ready, 8)
        pe.wait_ge(s.v_ready, 2 * ST)
        pe.wait_ge(s.cols_ready, 1)
        scores(0)
        for u in range(2 * HEADS_A):
            if u:
                spread(u - 1)
            if u + 1 < 2 * HEADS_A:
                scores(u + 1)
            outputs(u)
        spread(2 * HEADS_A - 1)

        stage = STAGE["a_o"]
        for c in range(8):
            pe.wait_ge(s.w_lo_ready, stage.first + c + 1)
            if c >= 4:
                pe.wait_ge(s.os_ready, c - 3)
            project(c % 4, c % 2, DT, b.xg_hi, b.xg_lo).then_inc(s.chunk_done, 1)
            if c == 0:
                pe.wait_ge(s.ysq_ready, HEADS_A)
                for h in range(HEADS_A):
                    ins = column_sums(b.ps[:, 6, ST * h:ST * h + ST], b.ysq[:, h, :])
                ins.then_inc(s.sums_done, 1)
            if c % 2:
                h = c // 2
                if h == 0:
                    pe.wait_ge(s.rcol_ready, HEAD_EVENT + 1)
                    pe.wait_ge(s.dbc_ready, 2 * HEADS_A)
                else:
                    pe.wait_ge(s.z_ready, 2 * h)
                broadcast(b.ps[:, 7, :], b.rcol[:, ST * h:ST * h + ST]).then_inc(s.head_bcast, 1)

    def values(c, slot, bank, tiles, ready=None):
        for kk in range(V_K):
            k = V_K * (c % 2) + kk
            if ready is not None:
                pe.wait_ge(ready[0], ready[1] + k + 1)
            cols = slice(512 * kk, 512 * kk + 512)
            for i in range(ST):
                hi, lo = b.xg_hi[:, k, :], b.xg_lo[:, k, :]
                if tiles:
                    hi, lo = tiles(hi, i), tiles(lo, i)
                else:
                    hi, lo = hi[:, P * i:P * i + P], lo[:, P * i:P * i + P]
                ins = split_matmul(b.ps[:, bank + i, :], hi, lo, b.w_hi[:, slot, cols], b.w_lo[:, slot, cols],
                                   k == 0, k == DT - 1)
        return ins

    def b_values(pas):
        stage, nu = STAGE[f"b_v{pas}"], 4
        for c in range(6):
            group = c // 2
            pe.wait_ge(s.w_lo_ready, stage.first + c + 1)
            if c % 2 == 0:
                if pas == 0 and group == 1:
                    pe.wait_ge(s.rinv_ready, nu + 1)
                if group == 2:
                    pe.wait_ge(s.bv_ready, 12 * pas + 4)
                if pas and group == 0:
                    pe.wait_ge(s.qkb_ready, 6 * (PAIRS_A_PASS + 1))
                if pas and group == 1:
                    pe.wait_ge(s.yb_lo_ready, PAIRS_A_PASS - 1)
                    pe.wait_ge(s.out_ready, 8 * PAIRS_A_PASS)
                    pe.wait_ge(s.pt_ready, 8 * PAIRS_A_PASS)
            ready = (s.xg_lo_ready, DT * nu) if pas == 0 and group == 0 else None
            values(c, c % 2, 4 * (group % 2), order_2 if group else None, ready).then_inc(s.chunk_done, 1)
            if pas == 0 and c == 0:
                norm_sums(nu)
            if pas == 0 and c == 1:
                norm_broadcast(nu)

    def b_slot(pair, k):
        n, buf = 8 * pair + k, pair % 2
        if k < 8:
            o, hd, tp = UNITS[k]
            rows = slice(DH * hd, DH * hd + DH)
            if n >= 2:
                pe.wait_ge(s.neg_ready, n - 1)
            for t in range(2):
                i = 2 * tp + t
                q = slice(P * i, P * i + P)
                at = 2 * P * t
                if o == 0:
                    ks = slice(window(i), window(i) + 2 * P)
                    ins = pe.matmul(b.ps[:, 2 + hd, at:at + 2 * P], b.qkb[rows, buf, 0, q], b.qkb[rows, buf, 1, ks],
                                    start=True, stop=True)
                else:
                    for g in range(2):
                        ins = pe.matmul(b.ps[:, 2 + hd, at + P * g:at + P * g + P], b.qkb[rows, buf, 2 + 2 * g, q],
                                        b.qkb[rows, buf, 3 + 2 * g, q], start=True, stop=True)
            ins.then_inc(s.s2_done, 1)
        if 1 <= k <= 8:
            m = n - 1
            pe.wait_ge(s.prob_ready, 2 * m + 2)
            if m >= 2:
                pe.wait_ge(s.pt_ready, m - 1)
            for q in range(4):
                ins = pe.transpose(b.ps[:, 4 + m % 2, P * q:P * q + P], b.prob[:, P * q:P * q + P], ident)
            ins.then_inc(s.pt_done, 1)
        if k >= 2:
            o, hd, tp = UNITS[k - 2]
            m = n - 2
            pe.wait_ge(s.pt_ready, m + 1)
            if m:
                pe.wait_ge(s.out_ready, m)
            at = 2 * DH * (k % 2)
            cols = slice(P * (pair % PAIRS_A_PASS) + DH * hd, P * (pair % PAIRS_A_PASS) + DH * hd + DH)
            for t in range(2):
                i = 2 * tp + t
                if o:
                    vals = (b.v2[:, i, cols], b.v3[:, i, cols])
                elif i in (0, ST - 1):
                    vals = tuple(b.v1[:, window(i) // P + e, cols] for e in range(2))
                else:
                    vals = tuple(b.vs[:, window(i) // P + e, cols] for e in range(2))
                for e in range(2):
                    ins = pe.matmul(b.ps[:, 6, at + DH * t:at + DH * t + DH],
                                    b.prob_t[:, 2 * P * t + P * e:2 * P * t + P * e + P], vals[e],
                                    start=e == 0, stop=e == 1)
            ins.then_inc(s.pv_done, 1)

    def b_finish(pair):
        pe.wait_ge(s.mix_ready, pair + 1)
        if pair:
            pe.wait_ge(s.yb_lo_ready, pair)
        for i in range(ST):
            ins = pe.transpose(b.ps[:, 7, P * i:P * i + P], b.ssq[:, P * i:P * i + P], ident)
        ins.then_inc(s.yt_done, 1)

    def b_pair(first, attend, project_pair):
        for c in range(6):
            if first is not None:
                pe.wait_ge(s.w_lo_ready, first + c + 1)
                n = 6 * project_pair + c
                if n >= 2:
                    pe.wait_ge(s.qkb_ready, n - 1)
                if c == 0 and project_pair in (0, PAIRS_A_PASS + 1):
                    pe.wait_ge(s.bv_ready, 12 if project_pair == 0 else 24)
                project(c % 2, c % 2, DT, b.xg_hi, b.xg_lo).then_inc(s.chunk_done, 1)
            if attend is not None:
                if c == 0:
                    pe.wait_ge(s.qkb_ready, 6 * (attend + 1))
                    if attend % PAIRS_A_PASS == 0:
                        pe.wait_ge(s.bv_ready, 12 * (attend // PAIRS_A_PASS + 1))
                        pe.wait_ge(s.vs_landed, 32 * (attend // PAIRS_A_PASS + 1))
                for k in SLOTS[c]:
                    b_slot(attend, k)
                if c == 0 and attend:
                    b_finish(attend - 1)

    def dilated():
        b_values(0)
        qk0, qk1 = STAGE["b_qk0"].first, STAGE["b_qk1"].first
        b_pair(qk0, None, 0)
        for pair in range(PAIRS_A_PASS):
            b_pair(qk0 + 6 * (pair + 1), pair, pair + 1)
        b_values(1)
        for pair in range(PAIRS_A_PASS, PAIRS):
            b_pair(qk1 + 6 * (pair - PAIRS_A_PASS) if pair < PAIRS - 1 else None, pair, pair + 1)
        b_finish(PAIRS - 1)

    pe.wait_ge(s.small_landed, 16)
    pe.wait_ge(s.consts_ready, 2)
    up(0, 0)
    down(0, 1)
    mlstm()
    out_projection("a_out", 2, b.z_hi, b.z_lo, s.z_lo_ready)
    up(1, 2)
    down(1, 3)
    up(2, 3)
    down(2, 4)
    dilated()
    out_projection("b_out", 5, b.yb_hi, b.yb_lo, s.yb_lo_ready)
    up(3, 5)
    down(3, 6)
    norm_sums(6)
    norm_broadcast(6)


def gpsimd_program(pool, b, s):

    def power(e, cols):
        pool.wait_ge(s.mean_ready, e + 1)
        pool.tensor_tensor(b.rsqrt[:, 0:cols], b.mean_sq[:, 0:cols], b.exponent[:, 0:cols],
                           ALU.pow).then_inc(s.rsqrt_ready, 1)

    def mlstm_masks():
        for u in range(2 * HEADS_A):
            backward = u % 2
            for j in range(ST):
                si, n = (ST - 1 - j if backward else j), ST * u + j
                block = b.wt[:, n % 2, P * si:P * si + P]
                sign = -1 if backward else 1
                pool.wait_ge(s.wt_ready, n + 1)
                pool.affine_select(out=block, in_=block, pattern=[[sign, P]], compare_op=ALU.is_ge, fill=0.0,
                                   base=0, channel_multiplier=-sign).then_inc(s.wt_masked, 1)

    def shift_values(pas):
        pool.wait_ge(s.bv_ready, 12 * pas + 4)
        pool.dma_start(b.vs[0:HALF, :, :], b.v1[HALF:P, 0:ST - 1, :]).then_inc(s.vs_landed, 16)
        pool.dma_start(b.vs[HALF:P, :, :], b.v1[0:HALF, 1:ST, :]).then_inc(s.vs_landed, 16)

    def reorder(pair):
        pool.wait_ge(s.out_ready, 8 * pair + 4)
        pool.wait_ge(s.prob_ready, 16 * pair + 8)
        if pair:
            pool.wait_ge(s.mix_ready, pair)
        for i in range(ST):
            pool.dma_start(b.o2t[:, i, :, :], b.o2[32 * i:32 * i + 32, :, :, :]).then_inc(s.o2t_landed, 16)

    pool.wait_ge(s.consts_ready, 2)
    power(0, ST)
    power(1, ST)
    mlstm_masks()
    power(HEAD_EVENT, ST * HEADS_A)
    for nu in (2, 3):
        power(event(nu), ST)
    power(event(4), 2 * ST)
    for pas in range(NPASS):
        shift_values(pas)
        for pair in range(PAIRS_A_PASS):
            reorder(PAIRS_A_PASS * pas + pair)
    for nu in (5, 6):
        power(event(nu), ST)



def tiled(w, rows=P):
    return w.reshape(w.shape[0] // rows, rows, w.shape[1])


def output_tiles(w):
    k, n = w.shape
    return np.ascontiguousarray(w.reshape(k // P, P, n // P, P).transpose(2, 1, 0, 3)).reshape(n // P, P, k)


def value_chunks(w):
    n = w.shape[1]
    a = w.reshape(2, V_K, P, n // 512, 512).transpose(3, 0, 2, 1, 4)
    return np.ascontiguousarray(a).reshape(2 * (n // 512), P, V_COLS)


def down_chunks(w):
    a = w.reshape(2, DOWN_HALF, P, DT, P).transpose(3, 0, 2, 1, 4)
    return np.ascontiguousarray(a).reshape(2 * DT, P, DOWN_COLS)


def columns(v):
    return np.ascontiguousarray(v.reshape(-1, P).T)


def lay_out(inputs):
    i = {k: np.asarray(v) for k, v in inputs.items()}
    out = {"x_t": np.ascontiguousarray(i["x"][0].T).reshape(DT, P, SEQ)}
    ffns = [("ffn1", 0), ("ffn2", 0), ("ffn1", 1), ("ffn2", 1)]
    for n, (name, layer) in enumerate(ffns):
        gate, up = output_tiles(i[f"{name}_gate"][layer]), output_tiles(i[f"{name}_up"][layer])
        out[f"w_up{n}"] = np.concatenate([gate, up], axis=2)
        out[f"w_down{n}"] = down_chunks(i[f"{name}_down"][layer])
    w = i["a_w_in"][0]
    qk, v = 2 * HEADS_A * DQK, HEADS_A * DV
    out["w_a_qk"] = output_tiles(w[:, :qk])
    out["w_a_v"] = value_chunks(w[:, qk:qk + v])
    out["w_a_o"] = output_tiles(w[:, qk + v:qk + 2 * v])
    gates, gate_b = np.zeros((D, P), np.float32), np.zeros(P, np.float32)
    for k, row in enumerate((0, 64, 32, 96)):
        src = slice(qk + 2 * v + HEADS_A * k, qk + 2 * v + HEADS_A * (k + 1))
        gates[:, row:row + HEADS_A] = w[:, src]
        gate_b[row:row + HEADS_A] = i["a_gate_b"][0][HEADS_A * k:HEADS_A * (k + 1)]
    out["w_a_gates"] = np.ascontiguousarray(gates.reshape(2, DT // 2, P, P).transpose(0, 2, 1, 3)).reshape(2, P, GATE_COLS)
    out["w_a_out"] = output_tiles(i["a_w_out"][0])
    w = i["b_w_in"][0].reshape(D, 3, 3, D)
    v = [value_chunks(np.ascontiguousarray(w[:, g, 2, VCOLS * h:VCOLS * h + VCOLS])) for h in range(NPASS) for g in range(3)]
    out["w_b_v"] = np.concatenate(v)
    tiles = [output_tiles(np.ascontiguousarray(w[:, g, j])) for g in range(3) for j in range(2)]
    out["w_b_qk"] = np.ascontiguousarray(np.stack(tiles, axis=1)).reshape(6 * PAIRS, P, TILE_COLS)
    out["w_b_out"] = output_tiles(i["b_w_out"][0])
    gains = [i["norm_ffn1"][0], i["norm_mix"][0], i["norm_ffn2"][0], i["norm_ffn1"][1], i["norm_mix"][1],
             i["norm_ffn2"][1], i["norm_final"]]
    conv_w = i["a_conv_w"][0].reshape(TAPS, 8, P).transpose(2, 1, 0).reshape(P, 8 * TAPS)
    slopes = np.exp2(-8.0 * (np.arange(HEADS_B) + 1.0) / HEADS_B).astype(np.float32)
    out["small"] = np.ascontiguousarray(np.concatenate(
        [np.eye(P, dtype=np.float32), *[columns(g) for g in gains], conv_w, columns(i["a_conv_b"][0]),
         columns(i["a_head_g"][0]), gate_b[:, None], np.broadcast_to(slopes, (P, HEADS_B))], axis=1))
    q = np.arange(P)[:, None, None]
    first = np.array([window(t) - P * t for t in (0, 1, ST - 1)])[None, :, None]
    dist = np.abs(first + np.arange(2 * P)[None, None, :] - q)
    out["dist1"] = np.where(dist <= HALF, dist, FAR).astype(np.float32)
    j = np.abs(np.arange(P)[None, :] - np.arange(P)[:, None])
    out["dist2"] = np.concatenate([np.where(j <= HALF, 4 * j, FAR), np.where(j % 4 == 0, 4 * j, FAR)],
                                  axis=1).astype(np.float32)[:, None, :]
    return out


def kernel(**inputs):
    import concourse.bacc as bacc
    from concourse.bass_utils import run_bass_kernel_spmd

    arrays = lay_out(inputs)
    nc = bacc.Bacc("TRN2", target_bir_lowering=False, num_devices=1)
    arrays = {f"in_{name}": a for name, a in arrays.items()}
    d = {name[3:]: nc.dram_tensor(name, a.shape, mybir.dt.from_np(a.dtype), kind="ExternalInput").ap()
         for name, a in arrays.items()}
    d["out_t"] = nc.dram_tensor("result_t", (DT, P, SEQ), F32, kind="ExternalOutput").ap()
    build(nc, d)
    r = run_bass_kernel_spmd(nc, [arrays], core_ids=[0])
    out = r.results[0]["result_t"].reshape(D, SEQ)
    return np.ascontiguousarray(out.T)[None]
```

```python
from contextlib import ExitStack

import numpy as np

import concourse.bass as bass
from concourse import mybir
from concourse.alu_op_type import AluOpType as ALU

ACT = mybir.ActivationFunctionType
F32 = mybir.dt.float32
F32R = mybir.dt.float32r
AX = mybir.AxisListType

P = 128
D = 1024
SEQ = 512
FF = 2816
DEPTH = 2
DT = D // P
ST = SEQ // P
FT = FF // P
EPS = 1e-6

HEADS_A = 4
DQK = 128
DV = 256
TAPS = 5
SPAN = 36
BACK = 32

HEADS_B = 16
DH = 64
HALF = 64
PAIRS = HEADS_B // 2
PAIRS_A_PASS = PAIRS // 2
NPASS = 2
VCOLS = D // NPASS
FAR = 1e30
OC = DH + 2


class Stage:

    def __init__(self, name, tensor, chunks, cols, skip=0):
        self.name, self.tensor, self.chunks, self.cols, self.skip = name, tensor, chunks, cols, skip
        self.first = 0


UP_COLS = 2 * DT * P
DOWN_HALF = FT // 2
DOWN_COLS = DOWN_HALF * P
TILE_COLS = DT * P
GATE_COLS = DT * P // 2
V_K = 4
V_COLS = V_K * 512


def stages():
    s = [Stage("up0", "w_up0", FT, UP_COLS), Stage("down0", "w_down0", 2 * DT, DOWN_COLS),
         Stage("a_qk", "w_a_qk", 8, TILE_COLS), Stage("a_gates", "w_a_gates", 2, GATE_COLS),
         Stage("a_v", "w_a_v", 4, V_COLS), Stage("a_o", "w_a_o", 8, TILE_COLS),
         Stage("a_out", "w_a_out", DT, TILE_COLS)]
    for n in (1, 2):
        s += [Stage(f"up{n}", f"w_up{n}", FT, UP_COLS), Stage(f"down{n}", f"w_down{n}", 2 * DT, DOWN_COLS)]
    ahead = 6 * (PAIRS_A_PASS + 1)
    s += [Stage("b_v0", "w_b_v", 6, V_COLS), Stage("b_qk0", "w_b_qk", ahead, TILE_COLS),
          Stage("b_v1", "w_b_v", 6, V_COLS, 6), Stage("b_qk1", "w_b_qk", 6 * PAIRS - ahead, TILE_COLS, ahead)]
    s += [Stage("b_out", "w_b_out", DT, TILE_COLS),
          Stage("up3", "w_up3", FT, UP_COLS), Stage("down3", "w_down3", 2 * DT, DOWN_COLS)]
    at = 0
    for x in s:
        x.first = at
        at += x.chunks
    return s, at


STAGES, CHUNKS = stages()
STAGE = {s.name: s for s in STAGES}
COLS = [s.cols for s in STAGES for _ in range(s.chunks)]

NORMS = ["ffn1_0", "mix_0", "ffn2_0", "ffn1_1", "mix_1", "ffn2_1", "final"]
N_NORMS = len(NORMS)

C_ID = 0
C_GAIN = C_ID + P
C_CONVW = C_GAIN + N_NORMS * DT
C_CONVB = C_CONVW + 8 * TAPS
C_HEADG = C_CONVB + 8
C_GATEB = C_HEADG + 8
C_SLOPE = C_GATEB + 1
C_END = C_SLOPE + HEADS_B


def band(si, backward):
    if backward:
        return 0, P * (si + 1), P * si * (si + 1) // 2
    return P * si, SEQ, sum(SEQ - P * j for j in range(si))


BAND_COLS = sum(SEQ - P * j for j in range(ST))


def window(i):
    return min(max(P * i - HALF, 0), SEQ - 2 * P)


class Named:
    pass


def allocate(nc, ctx):
    b = Named()

    def sb(name, shape, dt=F32):
        return ctx.enter_context(nc.sbuf_tensor(name, shape, dt))

    b.x = sb("x", [P, DT, SEQ])
    b.xg_hi = sb("xg_hi", [P, DT, SEQ], F32R)
    b.xg_lo = sb("xg_lo", [P, DT, SEQ], F32R)
    b.raw = sb("raw", [P, 2, UP_COLS])
    b.w_hi = sb("w_hi", [P, 2, UP_COLS], F32R)
    b.w_lo = sb("w_lo", [P, 2, UP_COLS], F32R)
    b.ssq = sb("ssq", [P, SEQ])
    b.xsq = sb("xsq", [P, SEQ])
    b.rinv = sb("rinv", [P, SEQ])
    b.small = sb("small", [P, C_END])
    b.dist1 = sb("dist1", [P, 3, 2 * P])
    b.dist2 = sb("dist2", [P, 1, 2 * P])
    b.ones = sb("ones", [P, 1])
    b.exponent = sb("exponent", [P, 16])
    b.mean_sq = sb("mean_sq", [P, 16])
    b.rsqrt = sb("rsqrt", [P, 16])
    b.newton = sb("newton", [P, 16])
    b.rcol = sb("rcol", [P, 16])

    base = (nc.sbuf_base + 63) // 64 * 64
    room = nc.sbuf_usable_end - base - 64
    sb("shared", [P, room // 4])

    at = [0]

    def place(name, shape, dt=F32):
        t = nc.alloc_sbuf_tensor_at(name, shape, dt, offset=base + at[0])
        at[0] += (4 * int(np.prod(shape[1:])) + 63) // 64 * 64
        assert at[0] <= room, (name, at, room)
        return t

    at[0] = 0
    b.h_hi = place("h_hi", [P, FT, SEQ], F32R)
    b.h_lo = place("h_lo", [P, FT, SEQ], F32R)
    b.gate = place("gate", [P, 1, SEQ])
    b.up = place("up", [P, 1, SEQ])
    b.silu = place("silu", [P, 1, SEQ])
    b.h = place("h", [P, 1, SEQ])
    at[0] = 0
    b.out_t = place("out_t", [P, DT, SEQ])
    at[0] = 0
    b.qk = place("qk", [P, 2 * HEADS_A, SEQ])
    b.v = place("v", [P, ST, D])
    b.p = place("p", [P, 2, BAND_COLS])
    b.wt = place("wt", [P, 2, SEQ])
    b.ysq = place("ysq", [P, SEQ])
    b.part = place("part", [P, 2, SEQ])
    b.dbc = place("dbc", [P, SEQ])
    b.z = place("z", [P, SEQ])
    b.mrow = place("mrow", [P, SEQ])
    b.afcol = place("afcol", [P, 2, ST, SPAN])
    b.dcol = place("dcol", [P, 4])
    b.rden = place("rden", [P, 2, 4])
    y_at = at[0]
    b.y = place("y", [P, DT, SEQ])
    og_at = at[0]
    b.og = place("og", [P, DT, SEQ])
    at[0] = y_at
    b.z_hi = place("z_hi", [P, DT, SEQ], F32R)
    at[0] = og_at
    b.z_lo = place("z_lo", [P, DT, SEQ], F32R)
    at[0] = y_at
    b.padded = place("padded", [P, SEQ + TAPS - 1])
    b.conv = place("conv", [P, SEQ])
    b.gates = place("gates", [P, SEQ])
    b.fg = place("fg", [P, SEQ])
    b.soft = place("soft", [P, SEQ])
    b.logf = place("logf", [P, SEQ])
    b.bsum = place("bsum", [P, SEQ])
    b.arow = place("arow", [P, SEQ])
    b.floor = place("floor", [P, SEQ])
    at[0] = 0
    b.v1 = place("v1", [P, ST, VCOLS])
    b.v2 = place("v2", [P, ST, VCOLS])
    b.v3 = place("v3", [P, ST, VCOLS])
    b.vs = place("vs", [P, ST - 1, VCOLS])
    b.qkb = place("qkb", [P, 2, 6, SEQ])
    b.yb_hi = place("yb_hi", [P, DT, SEQ], F32R)
    b.yb_lo = place("yb_lo", [P, DT, SEQ], F32R)
    b.o1 = place("o1", [P, ST, 2, OC])
    b.o2 = place("o2", [P, ST, 2, OC])
    b.o2t = place("o2t", [P, ST, 2, OC])
    b.neg = place("neg", [P, SEQ])
    b.prob = place("prob", [P, SEQ])
    b.prob_t = place("prob_t", [P, SEQ])
    b.mn = place("mn", [P, 8])
    b.wg = place("wg", [P, 2, 8])
    b.wd = place("wd", [P, 2, 8])
    b.den = place("den", [P, 8])
    b.ps = ctx.enter_context(nc.psum_tensor("ps", [P, 8, SEQ], F32))
    return b


def signals(nc, ctx):
    s = Named()

    def sem(name):
        return ctx.enter_context(nc.semaphore(name))

    s.x_landed = [sem(f"x_landed{k}") for k in range(DT // 2)]
    s.first_landed = sem("first_landed")
    s.first_hi_ready = sem("first_hi_ready")
    s.first_lo_ready = sem("first_lo_ready")
    s.small_landed = sem("small_landed")
    s.tables_landed = sem("tables_landed")
    s.w_hi_ready = sem("w_hi_ready")
    s.w_lo_ready = sem("w_lo_ready")
    s.chunk_done = sem("chunk_done")
    s.consts_ready = sem("consts_ready")
    s.x_ready = sem("x_ready")
    s.xg_hi_ready = sem("xg_hi_ready")
    s.xg_lo_ready = sem("xg_lo_ready")
    s.xsq_ready = sem("xsq_ready")
    s.ssq_ready = sem("ssq_ready")
    s.sums_done = sem("sums_done")
    s.mean_ready = sem("mean_ready")
    s.rsqrt_ready = sem("rsqrt_ready")
    s.newton_step = sem("newton_step")
    s.rcol_ready = sem("rcol_ready")
    s.bcast_done = sem("bcast_done")
    s.rinv_ready = sem("rinv_ready")
    s.gate_scaled = sem("gate_scaled")
    s.gu_drained = sem("gu_drained")
    s.silu_ready = sem("silu_ready")
    s.h_ready = sem("h_ready")
    s.h_hi_ready = sem("h_hi_ready")
    s.h_lo_ready = sem("h_lo_ready")
    s.qk_drained = sem("qk_drained")
    s.conv_step = sem("conv_step")
    s.qk_ready = sem("qk_ready")
    s.gates_drained = sem("gates_drained")
    s.gate_step = sem("gate_step")
    s.fg_ready = sem("fg_ready")
    s.exp_ready = sem("exp_ready")
    s.ln_ready = sem("ln_ready")
    s.floor_ready = sem("floor_ready")
    s.cols_done = sem("cols_done")
    s.cols_ready = sem("cols_ready")
    s.v_ready = sem("v_ready")
    s.mrow_bcast = sem("mrow_bcast")
    s.s_done = sem("s_done")
    s.wt_ready = sem("wt_ready")
    s.wt_masked = sem("wt_masked")
    s.p_ready = sem("p_ready")
    s.den_done = sem("den_done")
    s.den_step = sem("den_step")
    s.rden_ready = sem("rden_ready")
    s.dbc_done = sem("dbc_done")
    s.dbc_ready = sem("dbc_ready")
    s.o_done = sem("o_done")
    s.o_drained = sem("o_drained")
    s.y_ready = sem("y_ready")
    s.part_sq_ready = sem("part_sq_ready")
    s.ysq_ready = sem("ysq_ready")
    s.os_ready = sem("os_ready")
    s.og_ready = sem("og_ready")
    s.z_step = sem("z_step")
    s.z_ready = sem("z_ready")
    s.z_hi_ready = sem("z_hi_ready")
    s.z_lo_ready = sem("z_lo_ready")
    s.head_bcast = sem("head_bcast")
    s.bv_ready = sem("bv_ready")
    s.vs_landed = sem("vs_landed")
    s.qkb_ready = sem("qkb_ready")
    s.s2_done = sem("s2_done")
    s.neg_ready = sem("neg_ready")
    s.min_ready = sem("min_ready")
    s.prob_ready = sem("prob_ready")
    s.pt_done = sem("pt_done")
    s.pt_ready = sem("pt_ready")
    s.pv_done = sem("pv_done")
    s.out_ready = sem("out_ready")
    s.o2t_landed = sem("o2t_landed")
    s.mix_step = sem("mix_step")
    s.mix_exp = sem("mix_exp")
    s.mix_ready = sem("mix_ready")
    s.yt_done = sem("yt_done")
    s.yb_hi_ready = sem("yb_hi_ready")
    s.yb_lo_ready = sem("yb_lo_ready")
    s.final_ready = sem("final_ready")
    s.stored = sem("stored")
    s.raw_landed = [sem(f"raw_landed{slot}") for slot in range(2)]
    return s


def event(nu):
    return nu + HEADS_A * (nu >= 2)


HEAD_EVENT = 2

UNITS = [(o, hd, tp) for o in (1, 0) for tp in (0, 1) for hd in (0, 1)]
N_UNITS = len(UNITS)
SLOTS = N_UNITS + 2
MIX_SLOTS = (1, 2)
FINISH_SLOT = 4


def order_2(ap, r):
    return ap[:, r::ST]


def build(nc, d):
    with ExitStack() as ctx:
        b = allocate(nc, ctx)
        s = signals(nc, ctx)
        block = ctx.enter_context(nc.Block())

        @block.sync
        def _(sp):
            sync_program(sp, b, s, d)

        @block.scalar
        def _(act):
            scalar_program(act, b, s)

        @block.vector
        def _(dve):
            vector_program(dve, b, s)

        @block.tensor
        def _(pe):
            tensor_program(pe, b, s)

        @block.gpsimd
        def _(pool):
            gpsimd_program(pool, b, s)


def sync_program(sp, b, s, d):
    def load_x(k):
        sp.dma_start(b.x[:, 2 * k:2 * k + 2, :], d["x_t"][2 * k:2 * k + 2].rearrange("m p t -> p m t")).then_inc(
            s.x_landed[k], 16)

    sp.dma_start(b.small[:, :], d["small"]).then_inc(s.small_landed, 16)
    load_x(0)
    half = UP_COLS // 2
    sp.dma_start(b.raw[:, 0, 0:half], d["w_up0"][0, :, 0:half]).then_inc(s.first_landed, 16)
    for k in range(1, DT // 2):
        load_x(k)

    def load(stage, c, g, slot, wait=True):
        if wait:
            sp.wait_ge(s.w_lo_ready, g - 1)
        src = d[stage.tensor][bass.ds(c + stage.skip, 1)].rearrange("a p c -> p (a c)")
        sp.dma_start(b.raw[:, slot, 0:stage.cols], src).then_inc(s.raw_landed[slot], 16)

    for stage in STAGES:
        start = 0
        if stage.first == 0:
            sp.dma_start(b.raw[:, 0, half:], d["w_up0"][0, :, half:]).then_inc(s.raw_landed[0], 16)
            load(stage, 1, 1, 1, wait=False)
            sp.dma_start(b.dist1[:, :, :], d["dist1"]).then_inc(s.tables_landed, 16)
            sp.dma_start(b.dist2[:, :, :], d["dist2"]).then_inc(s.tables_landed, 16)
            start = 1
        if stage.chunks == 2:
            for j in range(2):
                load(stage, j, stage.first + j, j)
            continue
        with sp.Fori(start, stage.chunks // 2) as i:
            for j in range(2):
                load(stage, i * 2 + j, i * 2 + (stage.first + j), j)

    for m in range(DT):
        sp.wait_ge(s.final_ready, m + 1)
        sp.dma_start(d["out_t"][m], b.out_t[:, m, :]).then_inc(s.stored, 16)
    sp.wait_ge(s.stored, 16 * DT)


def scalar_program(act, b, s):

    def split(g, slot, cols, landed):
        act.wait_ge(s.raw_landed[slot], landed)
        if not (isinstance(g, int) and g < 2):
            act.wait_ge(s.chunk_done, g - 1)
        act.activation(b.w_hi[:, slot, 0:cols], b.raw[:, slot, 0:cols], ACT.Copy).then_inc(s.w_hi_ready, 1)

    def split_ahead(g):
        if g + 2 < CHUNKS:
            split(g + 2, g % 2, COLS[g + 2], 16 * ((g + 2) // 2 + 1))

    def gained(nu, m):
        g = C_GAIN + nu * DT + m
        act.activation(b.xg_hi[:, m, :], b.x[:, m, :], ACT.Copy,
                       scale=b.small[:, g:g + 1]).then_inc(s.xg_hi_ready, 1)

    def squared(nu, m):
        if nu + m:
            act.wait_ge(s.ssq_ready, DT * nu + m)
        act.activation(b.xsq[:, :], b.x[:, m, :], ACT.Square).then_inc(s.xsq_ready, 1)

    def update(nu, m):
        act.wait_ge(s.x_ready, DT * (nu - 1) + m + 1)
        if nu < N_NORMS - 1:
            gained(nu, m)
        squared(nu, m)

    def up(n):
        stage, hidden = STAGE[f"up{n}"], FT * n

        def silu(c):
            act.wait_ge(s.gate_scaled, hidden + c + 1)
            act.activation(b.silu[:, 0, :], b.gate[:, 0, :], ACT.Silu).then_inc(s.silu_ready, 1)

        with act.Fori(0, FT // 2 - 1) as i:
            for j in range(2):
                split(i * 2 + (stage.first + j + 2), j, UP_COLS, i * 16 + 16 * (stage.first // 2 + 2))
                silu(i * 2 + j)
        for c in (FT - 2, FT - 1):
            split_ahead(stage.first + c)
            silu(c)

    def down(n, nu):
        stage = STAGE[f"down{n}"]
        for m in range(DT):
            split_ahead(stage.first + 2 * m)
            split_ahead(stage.first + 2 * m + 1)
            update(nu, m)

    def out_projection(name, nu):
        stage = STAGE[name]
        for m in range(DT):
            split_ahead(stage.first + m)
            update(nu, m)

    def mlstm():
        def convolved(t):
            act.wait_ge(s.conv_step, TAPS * (t + 1))
            bias = b.small[:, C_CONVB + t:C_CONVB + t + 1]
            act.activation(b.qk[:, t, :], b.conv[:, :], ACT.Silu, bias=bias).then_inc(s.qk_ready, 1)

        stage = STAGE["a_qk"]
        for c in range(8):
            split_ahead(stage.first + c)
            if c:
                convolved(c - 1)
        for c in range(2):
            split_ahead(STAGE["a_gates"].first + c)
            if c == 0:
                convolved(7)
        act.wait_ge(s.gate_step, 3)
        act.activation(b.fg[0:SPAN, :], b.gates[64:64 + SPAN, :], ACT.Copy).then_inc(s.fg_ready, 1)
        act.wait_ge(s.gate_step, 4)
        act.activation(b.soft[0:SPAN, :], b.soft[0:SPAN, :], ACT.Exp).then_inc(s.exp_ready, 1)
        act.wait_ge(s.exp_ready, 1)
        act.activation(b.soft[0:SPAN, :], b.soft[0:SPAN, :], ACT.Ln, bias=1.0).then_inc(s.ln_ready, 1)
        for c in range(4):
            split_ahead(STAGE["a_v"].first + c)
            if c == 0:
                act.wait_ge(s.gate_step, 12)
                act.activation(b.floor[0:SPAN, :], b.floor[0:SPAN, :], ACT.Exp,
                               scale=-1.0).then_inc(s.floor_ready, 1)
            if c % 2:
                act.wait_ge(s.chunk_done, STAGE["a_v"].first + c + 1)
                for i in range(ST):
                    bank = i if c == 3 else 4 + i
                    cols = slice(512 * (c // 2), 512 * (c // 2) + 512)
                    act.activation(b.v[:, i, cols], b.ps[:, bank, :], ACT.Copy,
                                   scale=b.rcol[:, i:i + 1]).then_inc(s.v_ready, 1)

        def weights(u):
            h, backward = u // 2, u % 2
            row = h + BACK * backward
            act.wait_ge(s.mrow_bcast, u + 1)
            if u == 0:
                act.wait_ge(s.cols_ready, 1)
            for j in range(ST):
                si, n = (ST - 1 - j if backward else j), ST * u + j
                lo, hi, _ = band(si, backward)
                if n >= 2:
                    act.wait_ge(s.p_ready, n - 1)
                act.activation(b.wt[:, n % 2, lo:hi], b.ps[:, 0, lo:hi], ACT.Exp,
                               bias=b.afcol[:, 0, si, row:row + 1]).then_inc(s.wt_ready, 1)

        def squares(h):
            act.wait_ge(s.y_ready, h + 1)
            act.activation(b.part[:, :, :], b.y[:, 2 * h:2 * h + 2, :], ACT.Square).then_inc(s.part_sq_ready, 1)

        weights(0)
        stage = STAGE["a_o"]
        for u in range(2 * HEADS_A):
            if u and u % 2 == 0:
                squares(u // 2 - 1)
            if u + 1 < 2 * HEADS_A:
                weights(u + 1)
            split_ahead(stage.first + u)
            if u % 2:
                for t in (u - 1, u):
                    act.wait_ge(s.os_ready, t + 1)
                    act.activation(b.og[:, t, :], b.og[:, t, :], ACT.Sigmoid).then_inc(s.og_ready, 1)
        squares(HEADS_A - 1)

    def b_values(pas):
        stage = STAGE[f"b_v{pas}"]
        for c in range(6):
            split_ahead(stage.first + c)
            if c % 2:
                group = c // 2
                v = (b.v1, b.v2, b.v3)[group]
                act.wait_ge(s.chunk_done, stage.first + c + 1)
                if pas and group == 0:
                    act.wait_ge(s.pv_done, 8 * PAIRS_A_PASS)
                if pas == 0 and group == 0:
                    act.wait_ge(s.rcol_ready, event(4) + 1)
                for i in range(ST):
                    col = i + (ST if group else 0)
                    act.activation(v[:, i, :], b.ps[:, 4 * (group % 2) + i, :], ACT.Copy,
                                   scale=b.rcol[:, col:col + 1]).then_inc(s.bv_ready, 1)

    def b_slot(pair, k):
        n = 8 * pair + k
        if k < 8:
            o, hd, tp = UNITS[k]
            ob = (b.o1, b.o2)[o]
            act.wait_ge(s.min_ready, n + 1)
            if n:
                act.wait_ge(s.pt_done, n)
            for t in range(2):
                i = 2 * tp + t
                act.activation(b.prob[:, 256 * t:256 * t + 256], b.neg[:, 256 * t:256 * t + 256], ACT.Exp,
                               bias=ob[:, i, hd, DH + 1:DH + 2], scale=-1.0,
                               accum_out=ob[:, i, hd, DH:DH + 1]).then_inc(s.prob_ready, 1)
        if 1 <= k <= 8:
            act.wait_ge(s.pt_done, n)
            if n >= 2:
                act.wait_ge(s.pv_done, n - 1)
            act.activation(b.prob_t[:, :], b.ps[:, 4 + (n - 1) % 2, :], ACT.Copy).then_inc(s.pt_ready, 1)

    def b_mix(pair):
        act.wait_ge(s.mix_step, 9 * pair + 3)
        act.activation(b.wg[:, :, :], b.wg[:, :, :], ACT.Exp).then_inc(s.mix_exp, 1)

    def b_finish(pair):
        act.wait_ge(s.yt_done, pair + 1)
        act.activation(b.yb_hi[:, pair, :], b.ps[:, 7, :], ACT.Copy).then_inc(s.yb_hi_ready, 1)

    def b_pair(first, attend):
        for slot in range(2 * 6):
            if attend is not None and slot < SLOTS:
                b_slot(attend, slot)
                if attend and slot == MIX_SLOTS[0]:
                    b_mix(attend - 1)
                if attend and slot == FINISH_SLOT:
                    b_finish(attend - 1)
            if first is not None and slot % 2:
                split_ahead(first + slot // 2)

    def dilated():
        b_values(0)
        qk0, qk1 = STAGE["b_qk0"].first, STAGE["b_qk1"].first
        b_pair(qk0, None)
        for pair in range(PAIRS_A_PASS):
            b_pair(qk0 + 6 * (pair + 1), pair)
        b_values(1)
        for pair in range(PAIRS_A_PASS, PAIRS):
            b_pair(qk1 + 6 * (pair - PAIRS_A_PASS) if pair < PAIRS - 1 else None, pair)
        b_mix(PAIRS - 1)
        b_finish(PAIRS - 1)

    act.wait_ge(s.small_landed, 16)
    half = UP_COLS // 2
    for m in range(DT):
        if m % 2 == 0:
            act.wait_ge(s.x_landed[m // 2], 16)
        gained(0, m)
        if m == 1:
            act.wait_ge(s.first_landed, 16)
            act.activation(b.w_hi[:, 0, 0:half], b.raw[:, 0, 0:half], ACT.Copy).then_inc(s.first_hi_ready, 1)
    act.wait_ge(s.raw_landed[0], 16)
    act.activation(b.w_hi[:, 0, half:], b.raw[:, 0, half:], ACT.Copy).then_inc(s.w_hi_ready, 1)
    split(1, 1, COLS[1], 16)
    for m in range(DT):
        squared(0, m)
    up(0)
    down(0, 1)
    mlstm()
    out_projection("a_out", 2)
    up(1)
    down(1, 3)
    up(2)
    down(2, 4)
    dilated()
    out_projection("b_out", 5)
    up(3)
    down(3, 6)


def vector_program(dve, b, s):

    def split(g, slot, cols):
        dve.wait_ge(s.w_hi_ready, g + 1)
        dve.tensor_tensor(b.w_lo[:, slot, 0:cols], b.raw[:, slot, 0:cols],
                          b.w_hi[:, slot, 0:cols].bitcast(F32), ALU.subtract).then_inc(s.w_lo_ready, 1)

    def split_ahead(g):
        if g + 2 < CHUNKS:
            split(g + 2, g % 2, COLS[g + 2])

    def low_gained(nu, m):
        g = C_GAIN + nu * DT + m
        dve.wait_ge(s.xg_hi_ready, DT * nu + m + 1)
        dve.scalar_tensor_tensor(out=b.xg_lo[:, m, :], in0=b.x[:, m, :], scalar=b.small[:, g:g + 1],
                                 in1=b.xg_hi[:, m, :].bitcast(F32), op0=ALU.mult,
                                 op1=ALU.subtract).then_inc(s.xg_lo_ready, 1)

    def add_squares(nu, m):
        dve.wait_ge(s.xsq_ready, DT * nu + m + 1)
        if m == 0:
            dve.tensor_copy(b.ssq[:, :], b.xsq[:, :]).then_inc(s.ssq_ready, 1)
        else:
            dve.wait_ge(s.ssq_ready, DT * nu + m)
            dve.tensor_tensor(b.ssq[:, :], b.ssq[:, :], b.xsq[:, :], ALU.add).then_inc(s.ssq_ready, 1)

    def update(nu, m, bank, scale, done):
        x = b.x[:, m, :]
        dve.wait_ge(s.chunk_done, done)
        dve.scalar_tensor_tensor(out=x, in0=b.ps[:, bank, :], scalar=scale, in1=x,
                                 op0=ALU.mult, op1=ALU.add).then_inc(s.x_ready, 1)
        if nu < N_NORMS - 1:
            low_gained(nu, m)
        add_squares(nu, m)

    def rsqrt_columns(e, cols, n):
        ms, rs, nt = b.mean_sq[:, 0:cols], b.rsqrt[:, 0:cols], b.newton[:, 0:cols]
        dve.wait_ge(s.sums_done, e + 1)
        dve.tensor_scalar(ms, b.ps[:, 6, 0:cols], 1.0 / n, EPS, ALU.mult, ALU.add).then_inc(s.mean_ready, 1)
        dve.wait_ge(s.rsqrt_ready, e + 1)
        dve.tensor_tensor(nt, ms, rs, ALU.mult).then_inc(s.newton_step, 1)
        dve.wait_ge(s.newton_step, 3 * e + 1)
        dve.tensor_tensor(nt, nt, rs, ALU.mult).then_inc(s.newton_step, 1)
        dve.wait_ge(s.newton_step, 3 * e + 2)
        dve.tensor_scalar(nt, nt, -0.5, 1.5, ALU.mult, ALU.add).then_inc(s.newton_step, 1)
        dve.wait_ge(s.newton_step, 3 * e + 3)
        dve.tensor_tensor(b.rcol[:, 0:cols], rs, nt, ALU.mult).then_inc(s.rcol_ready, 1)

    def keep_rinv(nu):
        dve.wait_ge(s.bcast_done, nu + 1)
        dve.tensor_copy(b.rinv[:, :], b.ps[:, 7, :]).then_inc(s.rinv_ready, 1)

    def up(n, nu):
        stage, hidden = STAGE[f"up{n}"], FT * n

        def evict(c, par):
            dve.wait_ge(s.chunk_done, c + (stage.first + 1))
            dve.wait_ge(s.rinv_ready, nu + 1)
            dve.tensor_tensor(b.gate[:, 0, :], b.ps[:, 2 * par, :], b.rinv[:, :], ALU.mult).then_inc(s.gate_scaled, 1)
            dve.tensor_tensor(b.up[:, 0, :], b.ps[:, 2 * par + 1, :], b.rinv[:, :], ALU.mult).then_inc(s.gu_drained, 1)
            dve.wait_ge(s.gu_drained, c + (hidden + 1))
            dve.wait_ge(s.silu_ready, c + (hidden + 1))
            dve.tensor_tensor(b.h[:, 0, :], b.silu[:, 0, :], b.up[:, 0, :], ALU.mult).then_inc(s.h_ready, 1)
            tile = bass.ds(c, 1)
            dve.wait_ge(s.h_ready, c + (hidden + 1))
            dve.tensor_copy(b.h_hi[:, tile, :], b.h[:, :, :]).then_inc(s.h_hi_ready, 1)
            dve.wait_ge(s.h_hi_ready, c + (hidden + 1))
            dve.tensor_tensor(b.h_lo[:, tile, :], b.h[:, :, :], b.h_hi[:, tile, :].bitcast(F32),
                              ALU.subtract).then_inc(s.h_lo_ready, 1)

        rsqrt_columns(event(nu), ST, D)
        keep_rinv(nu)
        with dve.Fori(0, FT // 2 - 1) as i:
            for j in range(2):
                split(i * 2 + (stage.first + j + 2), j, UP_COLS)
                evict(i * 2 + j, j)
        for c in (FT - 2, FT - 1):
            split_ahead(stage.first + c)
            evict(c, c % 2)

    def down(n, nu):
        stage = STAGE[f"down{n}"]
        for m in range(DT):
            split_ahead(stage.first + 2 * m)
            split_ahead(stage.first + 2 * m + 1)
            update(nu, m, 4 + m % 2, 0.5, stage.first + 2 * m + 2)

    def out_projection(name, nu, bank, later):
        stage = STAGE[name]
        for m in range(DT):
            split_ahead(stage.first + m)
            update(nu, m, (bank if m < 2 else later) + m % 2, 1.0, stage.first + m + 1)

    def mlstm():
        nu = 1
        stage = STAGE["a_qk"]
        dve.memset(b.padded[:, :], 0.0)

        def convolve(t):
            step = TAPS * t
            dve.wait_ge(s.chunk_done, stage.first + t + 1)
            if t:
                dve.wait_ge(s.conv_step, step)
            dve.tensor_tensor(b.padded[:, 2:2 + SEQ], b.ps[:, t % 4, :], b.rinv[:, :], ALU.mult).then_inc(s.qk_drained, 1)
            dve.wait_ge(s.qk_drained, t + 1)
            if t:
                dve.wait_ge(s.qk_ready, t)
            for k in range(TAPS):
                w = b.small[:, C_CONVW + TAPS * t + k:C_CONVW + TAPS * t + k + 1]
                src = b.padded[:, k:k + SEQ]
                if k == 0:
                    dve.tensor_scalar(b.conv[:, :], src, w, None, ALU.mult).then_inc(s.conv_step, 1)
                else:
                    dve.wait_ge(s.conv_step, step + k)
                    dve.scalar_tensor_tensor(out=b.conv[:, :], in0=src, scalar=w, in1=b.conv[:, :],
                                             op0=ALU.mult, op1=ALU.add).then_inc(s.conv_step, 1)

        for c in range(8):
            split_ahead(stage.first + c)
            if c == 0:
                rsqrt_columns(event(nu), ST, D)
            if c == 1:
                keep_rinv(nu)
                dve.wait_ge(s.rinv_ready, nu + 1)
            if c:
                convolve(c - 1)
        gates_stage = STAGE["a_gates"]
        for c in range(2):
            split_ahead(gates_stage.first + c)
            if c == 0:
                convolve(7)
        fwd, bwd, rows = slice(0, HEADS_A), slice(BACK, SPAN), slice(0, SPAN)
        dve.memset(b.bsum[rows, :], 0.0).then_inc(s.gate_step, 1)
        dve.memset(b.mrow[rows, :], 0.0).then_inc(s.gate_step, 1)
        dve.wait_ge(s.chunk_done, gates_stage.first + 2)
        dve.tensor_tensor(b.gates[:, :], b.ps[:, 2, :], b.rinv[:, :], ALU.mult).then_inc(s.gates_drained, 1)
        dve.wait_ge(s.gates_drained, 1)
        dve.tensor_scalar(b.gates[:, :], b.gates[:, :], b.small[:, C_GATEB:C_GATEB + 1], None,
                          ALU.add).then_inc(s.gate_step, 1)
        dve.wait_ge(s.fg_ready, 1)
        dve.scalar_tensor_tensor(out=b.soft[rows, :], in0=b.fg[rows, :], scalar=-1.0, in1=b.fg[rows, :],
                                 op0=ALU.mult, op1=ALU.min).then_inc(s.gate_step, 1)
        dve.wait_ge(s.ln_ready, 1)
        dve.scalar_tensor_tensor(out=b.logf[rows, :], in0=b.fg[rows, :], scalar=0.0, in1=b.soft[rows, :],
                                 op0=ALU.min, op1=ALU.subtract).then_inc(s.gate_step, 1)
        dve.wait_ge(s.gate_step, 5)
        dve.tensor_tensor_scan(b.bsum[fwd, :], b.logf[fwd, :], b.logf[fwd, :], 0.0, ALU.add,
                               ALU.bypass).then_inc(s.gate_step, 1)
        dve.tensor_tensor_scan(b.bsum[bwd, ::-1], b.logf[bwd, ::-1], b.logf[bwd, ::-1], 0.0, ALU.add,
                               ALU.bypass).then_inc(s.gate_step, 1)
        dve.wait_ge(s.gate_step, 7)
        dve.tensor_tensor(b.arow[rows, :], b.gates[rows, :], b.bsum[rows, :], ALU.subtract).then_inc(s.gate_step, 1)
        dve.wait_ge(s.gate_step, 8)
        dve.tensor_tensor_scan(b.mrow[fwd, :], b.arow[fwd, :], b.arow[fwd, :], 0.0, ALU.max,
                               ALU.max).then_inc(s.gate_step, 1)
        dve.tensor_tensor_scan(b.mrow[bwd, ::-1], b.arow[bwd, ::-1], b.arow[bwd, ::-1], 0.0, ALU.max,
                               ALU.max).then_inc(s.gate_step, 1)
        dve.wait_ge(s.gate_step, 10)
        dve.tensor_tensor(b.floor[rows, :], b.bsum[rows, :], b.mrow[rows, :], ALU.add).then_inc(s.gate_step, 1)
        dve.wait_ge(s.gate_step, 11)
        dve.tensor_scalar(b.mrow[rows, :], b.mrow[rows, :], -1.0, None, ALU.mult).then_inc(s.gate_step, 1)
        for c in range(4):
            split_ahead(STAGE["a_v"].first + c)
        dve.wait_ge(s.cols_done, 1)
        dve.tensor_copy(b.afcol[:, :, :, :], b.ps[:, 6, 0:2 * ST * SPAN].rearrange(
            "p (k i r) -> p k i r", k=2, i=ST)).then_inc(s.cols_ready, 1)

        def products(u):
            backward = u % 2
            if u >= 2:
                dve.wait_ge(s.o_done, u - 1)
            for j in range(ST):
                si, n = (ST - 1 - j if backward else j), ST * u + j
                lo, hi, at = band(si, backward)
                dve.wait_ge(s.wt_masked, n + 1)
                dve.wait_ge(s.s_done, n + 1)
                dve.scalar_tensor_tensor(out=b.p[:, u % 2, at:at + hi - lo], in0=b.ps[:, 2 + n % 2, lo:hi],
                                         scalar=DQK ** -0.5, in1=b.wt[:, n % 2, lo:hi], op0=ALU.mult,
                                         op1=ALU.mult).then_inc(s.p_ready, 1)

        def denominators(u):
            row = u // 2 + BACK * (u % 2)
            den = b.ps[:, 6, 320 + ST * u:320 + ST * u + ST]
            dve.wait_ge(s.den_done, u + 1)
            dve.scalar_tensor_tensor(out=b.dcol[:, :], in0=den, scalar=-1.0, in1=b.afcol[:, 1, :, row],
                                     op0=ALU.mult, op1=ALU.max).then_inc(s.den_step, 1)
            dve.wait_ge(s.den_step, 2 * u + 1)
            dve.tensor_tensor(b.dcol[:, :], den, b.dcol[:, :], ALU.max).then_inc(s.den_step, 1)
            dve.wait_ge(s.den_step, 2 * u + 2)
            dve.reciprocal(b.rden[:, u % 2, :], b.dcol[:, :]).then_inc(s.rden_ready, 1)

        def evict(u):
            h, backward = u // 2, u % 2
            dve.wait_ge(s.dbc_done, u + 1)
            dve.tensor_copy(b.dbc[:, :], b.ps[:, 7, :]).then_inc(s.dbc_ready, 1)
            dve.wait_ge(s.dbc_ready, u + 1)
            dve.wait_ge(s.o_done, u + 1)
            y = b.y[:, 2 * h:2 * h + 2, :]
            out = b.part if backward else y
            if backward and h:
                dve.wait_ge(s.ysq_ready, h)
            for e in range(2):
                ins = dve.tensor_tensor(out[:, e, :], b.ps[:, 4 + e, :], b.dbc[:, :], ALU.mult)
            ins.then_inc(s.o_drained, 1)
            if backward:
                dve.wait_ge(s.o_drained, u + 1)
                dve.tensor_tensor(y, y, b.part[:, :, :], ALU.add).then_inc(s.y_ready, 1)

        def head_squares(h):
            dve.wait_ge(s.part_sq_ready, h + 1)
            dve.tensor_tensor(b.ysq[:, :], b.part[:, 0, :], b.part[:, 1, :], ALU.add).then_inc(s.ysq_ready, 1)

        def gated(h):
            for t in (2 * h, 2 * h + 1):
                dve.wait_ge(s.og_ready, t + 1)
                if t:
                    dve.wait_ge(s.z_lo_ready, t)
                dve.scalar_tensor_tensor(out=b.z[:, :], in0=b.og[:, t, :],
                                         scalar=b.small[:, C_HEADG + t:C_HEADG + t + 1], in1=b.y[:, t, :],
                                         op0=ALU.mult, op1=ALU.mult).then_inc(s.z_step, 1)
                dve.wait_ge(s.z_step, t + 1)
                dve.wait_ge(s.head_bcast, h + 1)
                dve.tensor_tensor(b.z[:, :], b.ps[:, 7, :], b.z[:, :], ALU.mult).then_inc(s.z_ready, 1)
                dve.wait_ge(s.z_ready, t + 1)
                dve.tensor_copy(b.z_hi[:, t, :], b.z[:, :]).then_inc(s.z_hi_ready, 1)
                dve.wait_ge(s.z_hi_ready, t + 1)
                dve.tensor_tensor(b.z_lo[:, t, :], b.z[:, :], b.z_hi[:, t, :].bitcast(F32),
                                  ALU.subtract).then_inc(s.z_lo_ready, 1)

        stage = STAGE["a_o"]
        products(0)
        for u in range(2 * HEADS_A):
            if u:
                evict(u - 1)
            if u >= 3 and u % 2:
                rsqrt_columns(HEAD_EVENT + (u - 3) // 2, ST, DV)
            if u + 1 < 2 * HEADS_A:
                products(u + 1)
            if u and u % 2 == 0:
                head_squares(u // 2 - 1)
            denominators(u)
            split_ahead(stage.first + u)
            dve.wait_ge(s.chunk_done, stage.first + u + 1)
            dve.tensor_tensor(b.og[:, u, :], b.ps[:, 1, :], b.rinv[:, :], ALU.mult).then_inc(s.os_ready, 1)
            if u >= 4 and u % 2 == 0:
                gated(u // 2 - 2)
        evict(2 * HEADS_A - 1)
        gated(HEADS_A - 2)
        head_squares(HEADS_A - 1)
        rsqrt_columns(HEAD_EVENT + HEADS_A - 1, ST, DV)
        gated(HEADS_A - 1)

    def b_values(pas):
        stage = STAGE[f"b_v{pas}"]
        for c in range(6):
            split_ahead(stage.first + c)
            if pas == 0 and c == 0:
                rsqrt_columns(event(4), 2 * ST, D)
            if pas == 0 and c == 1:
                keep_rinv(4)

    def b_slot(pair, k):
        n = 8 * pair + k
        if k < 8:
            o, hd, tp = UNITS[k]
            ob = (b.o1, b.o2)[o]
            head = 2 * pair + hd
            dist = b.dist2[:, :, :].to_broadcast([P, 2, 2 * P]) if o else b.dist1[:, tp:tp + 2, :]
            if pair and k in (0, N_UNITS // 2):
                if k:
                    dve.wait_ge(s.mix_ready, pair)
                else:
                    dve.wait_ge(s.o2t_landed, 64 * pair)
            dve.wait_ge(s.s2_done, n + 1)
            if n:
                dve.wait_ge(s.prob_ready, 2 * n)
            neg = b.neg[:, :].rearrange("p (t k) -> p t k", t=2)
            dve.scalar_tensor_tensor(out=neg, in0=dist, scalar=b.small[:, C_SLOPE + head:C_SLOPE + head + 1],
                                     in1=b.ps[:, 2 + hd, :].rearrange("p (t k) -> p t k", t=2),
                                     op0=ALU.mult, op1=ALU.subtract).then_inc(s.neg_ready, 1)
            dve.wait_ge(s.neg_ready, n + 1)
            dve.tensor_reduce(ob[:, 2 * tp:2 * tp + 2, hd, DH + 1:DH + 2], neg, AX.X, ALU.min).then_inc(s.min_ready, 1)
        if k >= 2:
            o, hd, tp = UNITS[k - 2]
            ob = (b.o1, b.o2)[o]
            dve.wait_ge(s.pv_done, n - 1)
            half = 128 * (k % 2)
            dve.tensor_copy(ob[:, 2 * tp:2 * tp + 2, hd, 0:DH], b.ps[:, 6, half:half + 128].rearrange(
                "p (t d) -> p t d", t=2)).then_inc(s.out_ready, 1)

    def flat(ap, c):
        return ap[:, :, c]

    def orders():
        return [o[:, :, :, :].rearrange("p i h c -> p (i h) c") for o in (b.o1, b.o2t)]

    def b_mix_maxima(pair):
        step = 9 * pair
        o1, o2 = orders()
        dve.wait_ge(s.o2t_landed, 64 * (pair + 1))
        dve.wait_ge(s.prob_ready, 16 * (pair + 1))
        dve.tensor_tensor(b.mn[:, :], flat(o1, DH + 1), flat(o2, DH + 1), ALU.min).then_inc(s.mix_step, 1)
        dve.wait_ge(s.mix_step, step + 1)
        for k, o in enumerate((o1, o2)):
            dve.tensor_tensor(b.wg[:, k, :], b.mn[:, :], flat(o, DH + 1), ALU.subtract).then_inc(s.mix_step, 1)

    def b_mix(pair):
        step = 9 * pair
        o1, o2 = orders()
        dve.wait_ge(s.mix_exp, pair + 1)
        for k, o in enumerate((o1, o2)):
            dve.tensor_tensor(b.wd[:, k, :], b.wg[:, k, :], flat(o, DH), ALU.mult).then_inc(s.mix_step, 1)
        dve.wait_ge(s.mix_step, step + 5)
        dve.tensor_tensor(b.den[:, :], b.wd[:, 0, :], b.wd[:, 1, :], ALU.add).then_inc(s.mix_step, 1)
        dve.wait_ge(s.mix_step, step + 6)
        dve.reciprocal(b.den[:, :], b.den[:, :]).then_inc(s.mix_step, 1)
        dve.wait_ge(s.mix_step, step + 7)
        den = b.den[:, :].unsqueeze(1).to_broadcast([P, 2, 8])
        dve.tensor_tensor(b.wg[:, :, :], b.wg[:, :, :], den, ALU.mult).then_inc(s.mix_step, 1)
        dve.wait_ge(s.mix_step, step + 8)
        if pair:
            dve.wait_ge(s.yt_done, pair)
        for k, (o, out) in enumerate(((o1, b.ssq), (o2, b.xsq))):
            w = b.wg[:, k, :].unsqueeze(2).to_broadcast([P, 8, DH])
            ins = dve.tensor_tensor(out[:, :].rearrange("p (g d) -> p g d", g=8), o[:, :, 0:DH], w, ALU.mult)
        ins.then_inc(s.mix_step, 1)
        dve.wait_ge(s.mix_step, step + 9)
        dve.tensor_tensor(b.ssq[:, :], b.ssq[:, :], b.xsq[:, :], ALU.add).then_inc(s.mix_ready, 1)

    def b_finish(pair):
        dve.wait_ge(s.yb_hi_ready, pair + 1)
        dve.tensor_tensor(b.yb_lo[:, pair, :], b.ps[:, 7, :], b.yb_hi[:, pair, :].bitcast(F32),
                          ALU.subtract).then_inc(s.yb_lo_ready, 1)

    def b_evict(done, project, c):
        dve.wait_ge(s.chunk_done, done)
        if project >= 2 and c == 0:
            dve.wait_ge(s.s2_done, N_UNITS * (project - 1))
        out, src, rinv = b.qkb[:, project % 2, c, :], b.ps[:, c % 2, :], b.rinv[:, :]
        if c >= 2:
            out = out.rearrange("p (r j) -> p j r", r=ST)
            src, rinv = (a.rearrange("p (j r) -> p j r", r=ST) for a in (src, rinv))
        if c % 2 == 0:
            dve.scalar_tensor_tensor(out=out, in0=src, scalar=DH ** -0.5, in1=rinv, op0=ALU.mult,
                                     op1=ALU.mult).then_inc(s.qkb_ready, 1)
        else:
            dve.tensor_tensor(out, src, rinv, ALU.mult).then_inc(s.qkb_ready, 1)

    def b_pair(first, attend, project):
        for slot in range(2 * 6):
            if attend is not None and slot < SLOTS:
                b_slot(attend, slot)
                if attend and slot == MIX_SLOTS[0]:
                    b_mix_maxima(attend - 1)
                if attend and slot == MIX_SLOTS[1]:
                    b_mix(attend - 1)
                if attend and slot == FINISH_SLOT:
                    b_finish(attend - 1)
            if first is not None and slot % 2:
                c = slot // 2
                split_ahead(first + c)
                b_evict(first + c + 1, project, c)

    def dilated():
        b_values(0)
        dve.wait_ge(s.rinv_ready, 5)
        dve.wait_ge(s.tables_landed, 32)
        qk0, qk1 = STAGE["b_qk0"].first, STAGE["b_qk1"].first
        b_pair(qk0, None, 0)
        for pair in range(PAIRS_A_PASS):
            b_pair(qk0 + 6 * (pair + 1), pair, pair + 1)
        b_values(1)
        for pair in range(PAIRS_A_PASS, PAIRS):
            b_pair(qk1 + 6 * (pair - PAIRS_A_PASS) if pair < PAIRS - 1 else None, pair, pair + 1)
        b_mix_maxima(PAIRS - 1)
        b_mix(PAIRS - 1)
        b_finish(PAIRS - 1)

    def final():
        rsqrt_columns(event(6), ST, D)
        dve.wait_ge(s.bcast_done, 7)
        for m in range(DT):
            g = C_GAIN + 6 * DT + m
            dve.scalar_tensor_tensor(out=b.out_t[:, m, :], in0=b.x[:, m, :], scalar=b.small[:, g:g + 1],
                                     in1=b.ps[:, 7, :], op0=ALU.mult, op1=ALU.mult).then_inc(s.final_ready, 1)

    dve.memset(b.ones[:, :], 1.0).then_inc(s.consts_ready, 1)
    dve.memset(b.exponent[:, :], -0.5).then_inc(s.consts_ready, 1)
    dve.wait_ge(s.small_landed, 16)
    half = UP_COLS // 2
    for m in range(DT):
        low_gained(0, m)
        if m == 1:
            dve.wait_ge(s.first_hi_ready, 1)
            dve.tensor_tensor(b.w_lo[:, 0, 0:half], b.raw[:, 0, 0:half], b.w_hi[:, 0, 0:half].bitcast(F32),
                              ALU.subtract).then_inc(s.first_lo_ready, 1)
    dve.wait_ge(s.w_hi_ready, 1)
    dve.tensor_tensor(b.w_lo[:, 0, half:], b.raw[:, 0, half:], b.w_hi[:, 0, half:].bitcast(F32),
                      ALU.subtract).then_inc(s.w_lo_ready, 1)
    split(1, 1, COLS[1])
    for m in range(DT):
        add_squares(0, m)
    up(0, 0)
    down(0, 1)
    mlstm()
    out_projection("a_out", 2, 2, 2)
    up(1, 2)
    down(1, 3)
    up(2, 3)
    down(2, 4)
    dilated()
    out_projection("b_out", 5, 0, 4)
    up(3, 5)
    down(3, 6)
    final()


def tensor_program(pe, b, s):
    ident = b.small[:, C_ID:C_ID + P]

    def split_matmul(out, a_hi, a_lo, x_hi, x_lo, start, stop):
        pe.matmul(out, a_hi, x_hi, start=start, stop=False)
        pe.matmul(out, a_hi, x_lo, start=False, stop=False)
        return pe.matmul(out, a_lo, x_hi, start=False, stop=stop)

    def weight_tile(slot, n):
        cols = slice(P * n, P * n + P)
        return b.w_hi[:, slot, cols], b.w_lo[:, slot, cols]

    def column_sums(out, rows, tiles=None):
        for i in range(ST):
            lhs = tiles(rows, i) if tiles else rows[:, P * i:P * i + P]
            ins = pe.matmul(out[:, i:i + 1], lhs, b.ones[:, :], start=True, stop=True)
        return ins

    def broadcast(out, cols):
        for i in range(ST):
            ins = pe.matmul(out[:, P * i:P * i + P], cols[:, i:i + 1].to_broadcast([P, P]), ident,
                            start=True, stop=True)
        return ins

    def norm_sums(nu):
        pe.wait_ge(s.ssq_ready, DT * (nu + 1))
        ins = column_sums(b.ps[:, 6, 0:ST], b.ssq[:, :])
        if nu == 4:
            ins = column_sums(b.ps[:, 6, ST:2 * ST], b.ssq[:, :], order_2)
        ins.then_inc(s.sums_done, 1)

    def norm_broadcast(nu):
        pe.wait_ge(s.rcol_ready, event(nu) + 1)
        broadcast(b.ps[:, 7, :], b.rcol[:, 0:ST]).then_inc(s.bcast_done, 1)

    def project(bank, slot, tiles, x_hi, x_lo, first=True, last=True, k0=0, w0=0, ready=None):
        for k in range(tiles):
            if ready is not None:
                pe.wait_ge(ready[0], ready[1] + k0 + k + 1)
            w_hi, w_lo = weight_tile(slot, w0 + k)
            ins = split_matmul(b.ps[:, bank, :], w_hi, w_lo, x_hi[:, k0 + k, :], x_lo[:, k0 + k, :],
                               first and k == 0, last and k == tiles - 1)
        return ins

    def up(n, nu):
        stage, hidden = STAGE[f"up{n}"], FT * n

        def chunk(c, par, first=False):
            if isinstance(c, int) and c == 0:
                if stage.first == 0:
                    pe.wait_ge(s.first_lo_ready, 1)
                else:
                    pe.wait_ge(s.w_lo_ready, stage.first + 1)
            else:
                pe.wait_ge(s.w_lo_ready, c + (stage.first + 1))
            if not (isinstance(c, int) and c < 2):
                pe.wait_ge(s.gu_drained, c + (hidden - 1))
            ready = (s.xg_lo_ready, DT * nu) if first else None
            project(2 * par, par, DT, b.xg_hi, b.xg_lo, ready=ready)
            if first and nu:
                norm_sums(nu)
            if isinstance(c, int) and c == 0:
                pe.wait_ge(s.w_lo_ready, stage.first + 1)
            ins = project(2 * par + 1, par, DT, b.xg_hi, b.xg_lo, w0=DT)
            ins.then_inc(s.chunk_done, 1)
            if first and nu:
                norm_broadcast(nu)

        chunk(0, 0, True)
        if nu == 0:
            norm_sums(nu)
        chunk(1, 1)
        if nu == 0:
            norm_broadcast(nu)
        with pe.Fori(1, FT // 2) as i:
            for j in range(2):
                chunk(i * 2 + j, j)

    def down(n, nu):
        stage, hidden = STAGE[f"down{n}"], FT * n

        def pair(m, wait=True):
            for e in range(2):
                if wait:
                    pe.wait_ge(s.x_ready, m + (DT * (nu - 1) + e - 1))
                for half in range(2):
                    pe.wait_ge(s.w_lo_ready, m * 2 + (stage.first + 2 * e + half + 1))
                    pe.wait_ge(s.h_lo_ready, hidden + DOWN_HALF * (half + 1))
                    project(4 + e, half, DOWN_HALF, b.h_hi, b.h_lo, half == 0, half == 1,
                            DOWN_HALF * half).then_inc(s.chunk_done, 1)

        pair(0, False)
        with pe.Fori(1, DT // 2) as i:
            pair(i * 2)

    class Early:

        def __init__(self, name, nu, z_hi, z_lo, ready, bank, later, safe):
            self.stage, self.z_hi, self.z_lo, self.ready = STAGE[name], z_hi, z_lo, ready
            self.bank, self.later = bank, later
            self.x_before = DT * (nu - 1)
            early = [(m, k) for m in range(2) for k in range(safe)]
            self.todo = early + [(m, k) for k in range(safe, DT) for m in range(2)]
            self.begun, self.seen = [False, False], 0

        def do(self, n):
            for m, k in self.todo[:n]:
                if not self.begun[m]:
                    pe.wait_ge(s.w_lo_ready, self.stage.first + m + 1)
                    self.begun[m] = True
                if k + 1 > self.seen:
                    pe.wait_ge(self.ready, k + 1)
                    self.seen = k + 1
                w_hi, w_lo = weight_tile(m, k)
                ins = split_matmul(b.ps[:, self.bank + m, :], w_hi, w_lo, self.z_hi[:, k, :], self.z_lo[:, k, :],
                                   k == 0, k == DT - 1)
                if k == DT - 1:
                    ins.then_inc(s.chunk_done, 1)
            del self.todo[:n]

        def rest(self):
            self.do(len(self.todo))
            for m in range(2, DT):
                pe.wait_ge(s.w_lo_ready, self.stage.first + m + 1)
                if m >= 4 or self.later == self.bank:
                    pe.wait_ge(s.x_ready, self.x_before + m - 1)
                project(self.later + m % 2, m % 2, DT, self.z_hi, self.z_lo).then_inc(s.chunk_done, 1)

    def mlstm():
        nu = 1
        stage = STAGE["a_qk"]
        for c in range(8):
            pe.wait_ge(s.w_lo_ready, stage.first + c + 1)
            if c >= 4:
                pe.wait_ge(s.qk_drained, c - 3)
            ready = (s.xg_lo_ready, DT * nu) if c == 0 else None
            project(c % 4, c % 2, DT, b.xg_hi, b.xg_lo, ready=ready).then_inc(s.chunk_done, 1)
            if c == 0:
                norm_sums(nu)
            if c == 1:
                norm_broadcast(nu)
        stage = STAGE["a_gates"]
        pe.wait_ge(s.qk_drained, 7)
        for c in range(2):
            pe.wait_ge(s.w_lo_ready, stage.first + c + 1)
            project(2, c, DT // 2, b.xg_hi, b.xg_lo, c == 0, c == 1, DT // 2 * c).then_inc(s.chunk_done, 1)
        stage = STAGE["a_v"]
        for c in range(4):
            pe.wait_ge(s.w_lo_ready, stage.first + c + 1)
            if c == 0:
                pe.wait_ge(s.rinv_ready, nu + 1)
            if c == 2:
                pe.wait_ge(s.gates_drained, 1)
            values(c, c % 2, 0 if c >= 2 else 4, None).then_inc(s.chunk_done, 1)
        pe.wait_ge(s.floor_ready, 1)
        pe.wait_ge(s.v_ready, ST)
        for k, rows in enumerate((b.arow, b.floor)):
            for i in range(ST):
                at = (ST * k + i) * SPAN
                ins = pe.transpose(b.ps[:, 6, at:at + SPAN], rows[0:SPAN, P * i:P * i + P], ident[0:SPAN, 0:SPAN])
        ins.then_inc(s.cols_done, 1)

        def scores(u, beside):
            h, backward = u // 2, u % 2
            row = h + BACK * backward
            if u:
                pe.wait_ge(s.wt_ready, ST * u)
            pe.matmul(b.ps[:, 0, :], ident[0:SPAN, row:row + 1].to_broadcast([SPAN, P]), b.mrow[0:SPAN, :],
                      start=True, stop=True).then_inc(s.mrow_bcast, 1)
            for j in range(ST):
                si, n = (ST - 1 - j if backward else j), ST * u + j
                lo, hi, _ = band(si, backward)
                if n >= 2:
                    pe.wait_ge(s.p_ready, n - 1)
                pe.matmul(b.ps[:, 2 + n % 2, lo:hi], b.qk[:, HEADS_A + h, P * si:P * si + P], b.qk[:, h, lo:hi],
                          start=True, stop=True).then_inc(s.s_done, 1)
                beside(j)

        def outputs(u):
            h, backward = u // 2, u % 2
            order = range(ST)[::-1] if backward else range(ST)
            pe.wait_ge(s.p_ready, ST * (u + 1))
            for i in range(ST):
                seen = [si for si in order if (si >= i if backward else si <= i)]
                for si in seen:
                    lo, _, at = band(si, backward)
                    at += P * i - lo
                    col = 320 + ST * u + i
                    ins = pe.matmul(b.ps[:, 6, col:col + 1], b.p[:, u % 2, at:at + P], b.ones[:, :],
                                    start=si == seen[0], stop=si == seen[-1])
            ins.then_inc(s.den_done, 1)
            if u:
                pe.wait_ge(s.o_drained, u)
            for e in range(2):
                for j, si in enumerate(order):
                    lo, hi, at = band(si, backward)
                    v = b.v[:, si, DV * h + P * e:DV * h + P * e + P]
                    ins = pe.matmul(b.ps[:, 4 + e, lo:hi], v, b.p[:, u % 2, at:at + hi - lo],
                                    start=j == 0, stop=j == ST - 1)
            ins.then_inc(s.o_done, 1)

        def spread(u):
            pe.wait_ge(s.rden_ready, u + 1)
            if u:
                pe.wait_ge(s.dbc_ready, u)
            broadcast(b.ps[:, 7, :], b.rden[:, u % 2, :]).then_inc(s.dbc_done, 1)

        def spread_head(h):
            pe.wait_ge(s.rcol_ready, HEAD_EVENT + h + 1)
            pe.wait_ge(s.dbc_ready, min(2 * h + 4, 2 * HEADS_A))
            if h == HEADS_A - 1:
                pe.wait_ge(s.z_ready, 2 * h)
            broadcast(b.ps[:, 7, :], b.rcol[:, 0:ST]).then_inc(s.head_bcast, 1)

        def head_sums(h):
            pe.wait_ge(s.ysq_ready, h + 1)
            column_sums(b.ps[:, 6, 0:ST], b.ysq[:, :]).then_inc(s.sums_done, 1)
            pe.wait_ge(s.mean_ready, HEAD_EVENT + h + 1)

        stage = STAGE["a_o"]

        def gate_part(u):
            def part(j):
                if j == 0:
                    pe.wait_ge(s.w_lo_ready, stage.first + u + 1)
                    if u:
                        pe.wait_ge(s.os_ready, u)
                ins = project(1, u % 2, 2, b.xg_hi, b.xg_lo, j == 0, j == ST - 1, 2 * j, 2 * j)
                if j == ST - 1:
                    ins.then_inc(s.chunk_done, 1)
            return part

        pe.wait_ge(s.qk_ready, 8)
        pe.wait_ge(s.v_ready, 2 * ST)
        pe.wait_ge(s.cols_ready, 1)
        scores(0, lambda j: None)
        for u in range(2 * HEADS_A):
            if u:
                if u >= 5 and u % 2:
                    pe.wait_ge(s.z_ready, u - 3)
                spread(u - 1)
            if u >= 3 and u % 2:
                head_sums((u - 3) // 2)
            if u + 1 < 2 * HEADS_A:
                scores(u + 1, gate_part(u))
            else:
                for j in range(ST):
                    gate_part(u)(j)
            if u >= 4 and u % 2 == 0:
                spread_head(u // 2 - 2)
            outputs(u)
        early = Early("a_out", 2, b.z_hi, b.z_lo, s.z_lo_ready, 2, 2, 4)
        pe.wait_ge(s.z_ready, 4)
        spread(2 * HEADS_A - 1)
        spread_head(HEADS_A - 2)
        early.do(6)
        head_sums(HEADS_A - 1)
        early.do(2)
        spread_head(HEADS_A - 1)
        early.rest()

    def values(c, slot, bank, tiles, ready=None):
        for kk in range(V_K):
            k = V_K * (c % 2) + kk
            if ready is not None:
                pe.wait_ge(ready[0], ready[1] + k + 1)
            cols = slice(512 * kk, 512 * kk + 512)
            for i in range(ST):
                hi, lo = b.xg_hi[:, k, :], b.xg_lo[:, k, :]
                if tiles:
                    hi, lo = tiles(hi, i), tiles(lo, i)
                else:
                    hi, lo = hi[:, P * i:P * i + P], lo[:, P * i:P * i + P]
                ins = split_matmul(b.ps[:, bank + i, :], hi, lo, b.w_hi[:, slot, cols], b.w_lo[:, slot, cols],
                                   k == 0, k == DT - 1)
        return ins

    def b_values(pas):
        stage, nu = STAGE[f"b_v{pas}"], 4
        for c in range(6):
            group = c // 2
            pe.wait_ge(s.w_lo_ready, stage.first + c + 1)
            if c % 2 == 0:
                if pas == 0 and group == 1:
                    pe.wait_ge(s.rinv_ready, nu + 1)
                if group == 2:
                    pe.wait_ge(s.bv_ready, 12 * pas + 4)
                if pas and group == 0:
                    pe.wait_ge(s.qkb_ready, 6 * (PAIRS_A_PASS + 1))
                if pas and group == 1:
                    pe.wait_ge(s.yb_lo_ready, PAIRS_A_PASS - 1)
                    pe.wait_ge(s.out_ready, 8 * PAIRS_A_PASS)
                    pe.wait_ge(s.pt_ready, 8 * PAIRS_A_PASS)
            ready = (s.xg_lo_ready, DT * nu) if pas == 0 and group == 0 else None
            values(c, c % 2, 4 * (group % 2), order_2 if group else None, ready).then_inc(s.chunk_done, 1)
            if pas == 0 and c == 0:
                norm_sums(nu)
            if pas == 0 and c == 1:
                norm_broadcast(nu)

    def b_slot(pair, k):
        n, buf = 8 * pair + k, pair % 2
        if k < 8:
            o, hd, tp = UNITS[k]
            rows = slice(DH * hd, DH * hd + DH)
            if n >= 2:
                pe.wait_ge(s.neg_ready, n - 1)
            for t in range(2):
                i = 2 * tp + t
                q = slice(P * i, P * i + P)
                at = 2 * P * t
                if o == 0:
                    ks = slice(window(i), window(i) + 2 * P)
                    ins = pe.matmul(b.ps[:, 2 + hd, at:at + 2 * P], b.qkb[rows, buf, 0, q], b.qkb[rows, buf, 1, ks],
                                    start=True, stop=True)
                else:
                    for g in range(2):
                        ins = pe.matmul(b.ps[:, 2 + hd, at + P * g:at + P * g + P], b.qkb[rows, buf, 2 + 2 * g, q],
                                        b.qkb[rows, buf, 3 + 2 * g, q], start=True, stop=True)
            ins.then_inc(s.s2_done, 1)
        if 1 <= k <= 8:
            m = n - 1
            pe.wait_ge(s.prob_ready, 2 * m + 2)
            if m >= 2:
                pe.wait_ge(s.pt_ready, m - 1)
            for q in range(4):
                ins = pe.transpose(b.ps[:, 4 + m % 2, P * q:P * q + P], b.prob[:, P * q:P * q + P], ident)
            ins.then_inc(s.pt_done, 1)
        if k >= 2:
            o, hd, tp = UNITS[k - 2]
            m = n - 2
            pe.wait_ge(s.pt_ready, m + 1)
            if m:
                pe.wait_ge(s.out_ready, m)
            at = 2 * DH * (k % 2)
            cols = slice(P * (pair % PAIRS_A_PASS) + DH * hd, P * (pair % PAIRS_A_PASS) + DH * hd + DH)
            for t in range(2):
                i = 2 * tp + t
                if o:
                    vals = (b.v2[:, i, cols], b.v3[:, i, cols])
                elif i in (0, ST - 1):
                    vals = tuple(b.v1[:, window(i) // P + e, cols] for e in range(2))
                else:
                    vals = tuple(b.vs[:, window(i) // P + e, cols] for e in range(2))
                for e in range(2):
                    ins = pe.matmul(b.ps[:, 6, at + DH * t:at + DH * t + DH],
                                    b.prob_t[:, 2 * P * t + P * e:2 * P * t + P * e + P], vals[e],
                                    start=e == 0, stop=e == 1)
            ins.then_inc(s.pv_done, 1)

    def b_finish(pair):
        pe.wait_ge(s.mix_ready, pair + 1)
        if pair:
            pe.wait_ge(s.yb_lo_ready, pair)
        for i in range(ST):
            ins = pe.transpose(b.ps[:, 7, P * i:P * i + P], b.ssq[:, P * i:P * i + P], ident)
        ins.then_inc(s.yt_done, 1)

    def b_pair(first, attend, project_pair, early=None):
        for slot in range(2 * 6):
            c, odd = slot // 2, slot % 2
            if first is not None and not odd:
                pe.wait_ge(s.w_lo_ready, first + c + 1)
                n = 6 * project_pair + c
                if n >= 2:
                    pe.wait_ge(s.qkb_ready, n - 1)
                if c == 0 and project_pair in (0, PAIRS_A_PASS + 1):
                    pe.wait_ge(s.bv_ready, 12 if project_pair == 0 else 24)
                project(c % 2, c % 2, 2, b.xg_hi, b.xg_lo, True, False, 0, 0)
            if attend is not None and slot < SLOTS:
                if slot == 0:
                    pe.wait_ge(s.qkb_ready, 6 * (attend + 1))
                    if attend % PAIRS_A_PASS == 0:
                        pe.wait_ge(s.bv_ready, 12 * (attend // PAIRS_A_PASS + 1))
                        pe.wait_ge(s.vs_landed, 32 * (attend // PAIRS_A_PASS + 1))
                b_slot(attend, slot)
                if attend and slot == FINISH_SLOT:
                    b_finish(attend - 1)
            if first is not None:
                if odd:
                    project(c % 2, c % 2, 2, b.xg_hi, b.xg_lo, False, True, 6, 6).then_inc(s.chunk_done, 1)
                else:
                    project(c % 2, c % 2, 4, b.xg_hi, b.xg_lo, False, False, 2, 2)
            if early:
                early.do(1 + (slot < 2))

    def dilated():
        b_values(0)
        qk0, qk1 = STAGE["b_qk0"].first, STAGE["b_qk1"].first
        b_pair(qk0, None, 0)
        for pair in range(PAIRS_A_PASS):
            b_pair(qk0 + 6 * (pair + 1), pair, pair + 1)
        b_values(1)
        for pair in range(PAIRS_A_PASS, PAIRS - 1):
            b_pair(qk1 + 6 * (pair - PAIRS_A_PASS), pair, pair + 1)
        early = Early("b_out", 5, b.yb_hi, b.yb_lo, s.yb_lo_ready, 0, 4, 6)
        b_pair(None, PAIRS - 1, None, early)
        b_finish(PAIRS - 1)
        early.rest()

    pe.wait_ge(s.small_landed, 16)
    pe.wait_ge(s.consts_ready, 2)
    up(0, 0)
    down(0, 1)
    mlstm()
    up(1, 2)
    down(1, 3)
    up(2, 3)
    down(2, 4)
    dilated()
    up(3, 5)
    down(3, 6)
    norm_sums(6)
    norm_broadcast(6)


def gpsimd_program(pool, b, s):

    def power(e, cols):
        pool.wait_ge(s.mean_ready, e + 1)
        pool.tensor_tensor(b.rsqrt[:, 0:cols], b.mean_sq[:, 0:cols], b.exponent[:, 0:cols],
                           ALU.pow).then_inc(s.rsqrt_ready, 1)

    def mlstm_masks():
        for u in range(2 * HEADS_A):
            if u >= 4 and u % 2 == 0:
                power(HEAD_EVENT + u // 2 - 2, ST)
            backward = u % 2
            for j in range(ST):
                si, n = (ST - 1 - j if backward else j), ST * u + j
                block = b.wt[:, n % 2, P * si:P * si + P]
                sign = -1 if backward else 1
                pool.wait_ge(s.wt_ready, n + 1)
                pool.affine_select(out=block, in_=block, pattern=[[sign, P]], compare_op=ALU.is_ge, fill=0.0,
                                   base=0, channel_multiplier=-sign).then_inc(s.wt_masked, 1)

    def shift_values(pas):
        pool.wait_ge(s.bv_ready, 12 * pas + 4)
        pool.dma_start(b.vs[0:HALF, :, :], b.v1[HALF:P, 0:ST - 1, :]).then_inc(s.vs_landed, 16)
        pool.dma_start(b.vs[HALF:P, :, :], b.v1[0:HALF, 1:ST, :]).then_inc(s.vs_landed, 16)

    def reorder(pair):
        pool.wait_ge(s.out_ready, 8 * pair + 4)
        pool.wait_ge(s.prob_ready, 16 * pair + 8)
        if pair:
            pool.wait_ge(s.mix_ready, pair)
        for i in range(ST):
            pool.dma_start(b.o2t[:, i, :, :], b.o2[32 * i:32 * i + 32, :, :, :]).then_inc(s.o2t_landed, 16)

    pool.wait_ge(s.consts_ready, 2)
    power(0, ST)
    power(1, ST)
    mlstm_masks()
    for h in (HEADS_A - 2, HEADS_A - 1):
        power(HEAD_EVENT + h, ST)
    for nu in (2, 3):
        power(event(nu), ST)
    power(event(4), 2 * ST)
    for pas in range(NPASS):
        shift_values(pas)
        for pair in range(PAIRS_A_PASS):
            reorder(PAIRS_A_PASS * pas + pair)
    for nu in (5, 6):
        power(event(nu), ST)



def tiled(w, rows=P):
    return w.reshape(w.shape[0] // rows, rows, w.shape[1])


def output_tiles(w):
    k, n = w.shape
    return np.ascontiguousarray(w.reshape(k // P, P, n // P, P).transpose(2, 1, 0, 3)).reshape(n // P, P, k)


def value_chunks(w):
    n = w.shape[1]
    a = w.reshape(2, V_K, P, n // 512, 512).transpose(3, 0, 2, 1, 4)
    return np.ascontiguousarray(a).reshape(2 * (n // 512), P, V_COLS)


def down_chunks(w):
    a = w.reshape(2, DOWN_HALF, P, DT, P).transpose(3, 0, 2, 1, 4)
    return np.ascontiguousarray(a).reshape(2 * DT, P, DOWN_COLS)


def columns(v):
    return np.ascontiguousarray(v.reshape(-1, P).T)


def lay_out(inputs):
    i = {k: np.asarray(v) for k, v in inputs.items()}
    out = {"x_t": np.ascontiguousarray(i["x"][0].T).reshape(DT, P, SEQ)}
    ffns = [("ffn1", 0), ("ffn2", 0), ("ffn1", 1), ("ffn2", 1)]
    for n, (name, layer) in enumerate(ffns):
        gate, up = output_tiles(i[f"{name}_gate"][layer]), output_tiles(i[f"{name}_up"][layer])
        out[f"w_up{n}"] = np.concatenate([gate, up], axis=2)
        out[f"w_down{n}"] = down_chunks(i[f"{name}_down"][layer])
    w = i["a_w_in"][0]
    qk, v = 2 * HEADS_A * DQK, HEADS_A * DV
    out["w_a_qk"] = output_tiles(w[:, :qk])
    out["w_a_v"] = value_chunks(w[:, qk:qk + v])
    out["w_a_o"] = output_tiles(w[:, qk + v:qk + 2 * v])
    gates, gate_b = np.zeros((D, P), np.float32), np.zeros(P, np.float32)
    for k, row in enumerate((0, 64, 32, 96)):
        src = slice(qk + 2 * v + HEADS_A * k, qk + 2 * v + HEADS_A * (k + 1))
        gates[:, row:row + HEADS_A] = w[:, src]
        gate_b[row:row + HEADS_A] = i["a_gate_b"][0][HEADS_A * k:HEADS_A * (k + 1)]
    out["w_a_gates"] = np.ascontiguousarray(gates.reshape(2, DT // 2, P, P).transpose(0, 2, 1, 3)).reshape(2, P, GATE_COLS)
    out["w_a_out"] = output_tiles(i["a_w_out"][0])
    w = i["b_w_in"][0].reshape(D, 3, 3, D)
    v = [value_chunks(np.ascontiguousarray(w[:, g, 2, VCOLS * h:VCOLS * h + VCOLS])) for h in range(NPASS) for g in range(3)]
    out["w_b_v"] = np.concatenate(v)
    tiles = [output_tiles(np.ascontiguousarray(w[:, g, j])) for g in range(3) for j in range(2)]
    out["w_b_qk"] = np.ascontiguousarray(np.stack(tiles, axis=1)).reshape(6 * PAIRS, P, TILE_COLS)
    out["w_b_out"] = output_tiles(i["b_w_out"][0])
    gains = [i["norm_ffn1"][0], i["norm_mix"][0], i["norm_ffn2"][0], i["norm_ffn1"][1], i["norm_mix"][1],
             i["norm_ffn2"][1], i["norm_final"]]
    conv_w = i["a_conv_w"][0].reshape(TAPS, 8, P).transpose(2, 1, 0).reshape(P, 8 * TAPS)
    slopes = np.exp2(-8.0 * (np.arange(HEADS_B) + 1.0) / HEADS_B).astype(np.float32)
    out["small"] = np.ascontiguousarray(np.concatenate(
        [np.eye(P, dtype=np.float32), *[columns(g) for g in gains], conv_w, columns(i["a_conv_b"][0]),
         columns(i["a_head_g"][0]), gate_b[:, None], np.broadcast_to(slopes, (P, HEADS_B))], axis=1))
    q = np.arange(P)[:, None, None]
    first = np.array([window(t) - P * t for t in (0, 1, ST - 1)])[None, :, None]
    dist = np.abs(first + np.arange(2 * P)[None, None, :] - q)
    out["dist1"] = np.where(dist <= HALF, dist, FAR).astype(np.float32)
    j = np.abs(np.arange(P)[None, :] - np.arange(P)[:, None])
    out["dist2"] = np.concatenate([np.where(j <= HALF, 4 * j, FAR), np.where(j % 4 == 0, 4 * j, FAR)],
                                  axis=1).astype(np.float32)[:, None, :]
    return out


def kernel(**inputs):
    import concourse.bacc as bacc
    from concourse.bass_utils import run_bass_kernel_spmd

    arrays = lay_out(inputs)
    nc = bacc.Bacc("TRN2", target_bir_lowering=False, num_devices=1)
    arrays = {f"in_{name}": a for name, a in arrays.items()}
    d = {name[3:]: nc.dram_tensor(name, a.shape, mybir.dt.from_np(a.dtype), kind="ExternalInput").ap()
         for name, a in arrays.items()}
    d["out_t"] = nc.dram_tensor("result_t", (DT, P, SEQ), F32, kind="ExternalOutput").ap()
    build(nc, d)
    r = run_bass_kernel_spmd(nc, [arrays], core_ids=[0])
    out = r.results[0]["result_t"].reshape(D, SEQ)
    return np.ascontiguousarray(out.T)[None]
```

```python
from contextlib import ExitStack

import numpy as np

import concourse.bass as bass
from concourse import mybir
from concourse.alu_op_type import AluOpType as ALU

ACT = mybir.ActivationFunctionType
F32 = mybir.dt.float32
F32R = mybir.dt.float32r
AX = mybir.AxisListType

P = 128
D = 1024
SEQ = 512
FF = 2816
DEPTH = 2
DT = D // P
ST = SEQ // P
FT = FF // P
EPS = 1e-6

HEADS_A = 4
DQK = 128
DV = 256
TAPS = 5
SPAN = 36
BACK = 32

HEADS_B = 16
DH = 64
HALF = 64
PAIRS = HEADS_B // 2
PAIRS_A_PASS = PAIRS // 2
NPASS = 2
VCOLS = D // NPASS
FAR = 1e30
OC = DH + 2


class Stage:

    def __init__(self, name, tensor, chunks, cols, skip=0):
        self.name, self.tensor, self.chunks, self.cols, self.skip = name, tensor, chunks, cols, skip
        self.first = 0


UP_COLS = 2 * DT * P
DOWN_HALF = FT // 2
DOWN_COLS = DOWN_HALF * P
TILE_COLS = DT * P
GATE_COLS = DT * P // 2
V_K = 4
V_COLS = V_K * 512


def stages():
    s = [Stage("up0", "w_up0", FT, UP_COLS), Stage("down0", "w_down0", 2 * DT, DOWN_COLS),
         Stage("a_qk", "w_a_qk", 8, TILE_COLS), Stage("a_gates", "w_a_gates", 2, GATE_COLS),
         Stage("a_v", "w_a_v", 4, V_COLS), Stage("a_o", "w_a_o", 8, TILE_COLS),
         Stage("a_out", "w_a_out", DT, TILE_COLS)]
    for n in (1, 2):
        s += [Stage(f"up{n}", f"w_up{n}", FT, UP_COLS), Stage(f"down{n}", f"w_down{n}", 2 * DT, DOWN_COLS)]
    ahead = 6 * (PAIRS_A_PASS + 1)
    s += [Stage("b_v0", "w_b_v", 6, V_COLS), Stage("b_qk0", "w_b_qk", ahead, TILE_COLS),
          Stage("b_v1", "w_b_v", 6, V_COLS, 6), Stage("b_qk1", "w_b_qk", 6 * PAIRS - ahead, TILE_COLS, ahead)]
    s += [Stage("b_out", "w_b_out", DT, TILE_COLS),
          Stage("up3", "w_up3", FT, UP_COLS), Stage("down3", "w_down3", 2 * DT, DOWN_COLS)]
    at = 0
    for x in s:
        x.first = at
        at += x.chunks
    return s, at


STAGES, CHUNKS = stages()
STAGE = {s.name: s for s in STAGES}
COLS = [s.cols for s in STAGES for _ in range(s.chunks)]

NORMS = ["ffn1_0", "mix_0", "ffn2_0", "ffn1_1", "mix_1", "ffn2_1", "final"]
N_NORMS = len(NORMS)

C_ID = 0
C_GAIN = C_ID + P
C_CONVW = C_GAIN + N_NORMS * DT
C_CONVB = C_CONVW + 8 * TAPS
C_HEADG = C_CONVB + 8
C_GATEB = C_HEADG + 8
C_SLOPE = C_GATEB + 1
C_END = C_SLOPE + HEADS_B


def band(si, backward):
    if backward:
        return 0, P * (si + 1), P * si * (si + 1) // 2
    return P * si, SEQ, sum(SEQ - P * j for j in range(si))


BAND_COLS = sum(SEQ - P * j for j in range(ST))


def window(i):
    return min(max(P * i - HALF, 0), SEQ - 2 * P)


class Named:
    pass


def allocate(nc, ctx):
    b = Named()

    def sb(name, shape, dt=F32):
        return ctx.enter_context(nc.sbuf_tensor(name, shape, dt))

    b.x = sb("x", [P, DT, SEQ])
    b.xg_hi = sb("xg_hi", [P, DT, SEQ], F32R)
    b.xg_lo = sb("xg_lo", [P, DT, SEQ], F32R)
    b.raw = sb("raw", [P, 2, UP_COLS])
    b.w_hi = sb("w_hi", [P, 2, UP_COLS], F32R)
    b.w_lo = sb("w_lo", [P, 2, UP_COLS], F32R)
    b.ssq = sb("ssq", [P, SEQ])
    b.xsq = sb("xsq", [P, SEQ])
    b.rinv = sb("rinv", [P, SEQ])
    b.small = sb("small", [P, C_END])
    b.dist1 = sb("dist1", [P, 3, 2 * P])
    b.dist2 = sb("dist2", [P, 1, 2 * P])
    b.ones = sb("ones", [P, 1])
    b.exponent = sb("exponent", [P, 16])
    b.mean_sq = sb("mean_sq", [P, 16])
    b.rsqrt = sb("rsqrt", [P, 16])
    b.newton = sb("newton", [P, 16])
    b.rcol = sb("rcol", [P, 16])

    base = (nc.sbuf_base + 63) // 64 * 64
    room = nc.sbuf_usable_end - base - 64
    sb("shared", [P, room // 4])

    at = [0]

    def place(name, shape, dt=F32):
        t = nc.alloc_sbuf_tensor_at(name, shape, dt, offset=base + at[0])
        at[0] += (4 * int(np.prod(shape[1:])) + 63) // 64 * 64
        assert at[0] <= room, (name, at, room)
        return t

    at[0] = 0
    b.h_hi = place("h_hi", [P, FT, SEQ], F32R)
    b.h_lo = place("h_lo", [P, FT, SEQ], F32R)
    b.gate = place("gate", [P, 1, SEQ])
    b.up = place("up", [P, 1, SEQ])
    b.silu = place("silu", [P, 1, SEQ])
    b.h = place("h", [P, 1, SEQ])
    at[0] = (2 * FT - DT) * 4 * SEQ
    b.first_sq = place("first_sq", [P, DT, SEQ])
    at[0] = 0
    b.out_t = place("out_t", [P, DT, SEQ])
    at[0] = 0
    b.qk = place("qk", [P, 2 * HEADS_A, SEQ])
    b.v = place("v", [P, ST, D])
    b.p = place("p", [P, 2, BAND_COLS])
    b.wt = place("wt", [P, 2, SEQ])
    b.ysq = place("ysq", [P, SEQ])
    b.part = place("part", [P, 2, SEQ])
    b.dbc = place("dbc", [P, SEQ])
    b.z = place("z", [P, SEQ])
    b.psum = place("psum", [P, SEQ])
    b.mrow = place("mrow", [P, SEQ])
    b.afcol = place("afcol", [P, 2, ST, SPAN])
    b.dcol = place("dcol", [P, 4])
    b.rden = place("rden", [P, 2, 4])
    y_at = at[0]
    b.y = place("y", [P, DT, SEQ])
    og_at = at[0]
    b.og = place("og", [P, DT, SEQ])
    at[0] = y_at
    b.z_hi = place("z_hi", [P, DT, SEQ], F32R)
    at[0] = og_at
    b.z_lo = place("z_lo", [P, DT, SEQ], F32R)
    at[0] = y_at
    b.padded = place("padded", [P, SEQ + TAPS - 1])
    b.conv = place("conv", [P, 2, SEQ])
    b.gates = place("gates", [P, SEQ])
    b.fg = place("fg", [P, SEQ])
    b.soft = place("soft", [P, SEQ])
    b.logf = place("logf", [P, SEQ])
    b.bsum = place("bsum", [P, SEQ])
    b.arow = place("arow", [P, SEQ])
    b.floor = place("floor", [P, SEQ])
    at[0] = 0
    b.v1 = place("v1", [P, ST, VCOLS])
    b.v2 = place("v2", [P, ST, VCOLS])
    b.v3 = place("v3", [P, ST, VCOLS])
    b.vs = place("vs", [P, ST - 1, VCOLS])
    b.qkb = place("qkb", [P, 2, 6, SEQ])
    b.yb_hi = place("yb_hi", [P, DT, SEQ], F32R)
    b.yb_lo = place("yb_lo", [P, DT, SEQ], F32R)
    b.o1 = place("o1", [P, ST, 2, OC])
    b.o2 = place("o2", [P, ST, 2, OC])
    b.o2t = place("o2t", [P, ST, 2, OC])
    b.neg = place("neg", [P, SEQ])
    b.prob = place("prob", [P, SEQ])
    b.prob_t = place("prob_t", [P, SEQ])
    b.mn = place("mn", [P, 8])
    b.wg = place("wg", [P, 2, 8])
    b.wd = place("wd", [P, 2, 8])
    b.den = place("den", [P, 8])
    b.ps = ctx.enter_context(nc.psum_tensor("ps", [P, 8, SEQ], F32))
    return b


def signals(nc, ctx):
    s = Named()

    def sem(name):
        return ctx.enter_context(nc.semaphore(name))

    s.x_landed = [sem(f"x_landed{k}") for k in range(DT // 2)]
    s.first_landed = sem("first_landed")
    s.first_hi_ready = sem("first_hi_ready")
    s.first_lo_ready = sem("first_lo_ready")
    s.small_landed = sem("small_landed")
    s.tables_landed = sem("tables_landed")
    s.w_hi_ready = sem("w_hi_ready")
    s.w_lo_ready = sem("w_lo_ready")
    s.chunk_done = sem("chunk_done")
    s.consts_ready = sem("consts_ready")
    s.x_ready = sem("x_ready")
    s.xg_hi_ready = sem("xg_hi_ready")
    s.xg_lo_ready = sem("xg_lo_ready")
    s.xsq_ready = sem("xsq_ready")
    s.first_sq_ready = sem("first_sq_ready")
    s.ssq_ready = sem("ssq_ready")
    s.sums_done = sem("sums_done")
    s.mean_ready = sem("mean_ready")
    s.rsqrt_ready = sem("rsqrt_ready")
    s.newton_step = sem("newton_step")
    s.rcol_ready = sem("rcol_ready")
    s.bcast_done = sem("bcast_done")
    s.rinv_ready = sem("rinv_ready")
    s.gate_scaled = sem("gate_scaled")
    s.gu_drained = sem("gu_drained")
    s.silu_ready = sem("silu_ready")
    s.h_ready = sem("h_ready")
    s.h_hi_ready = sem("h_hi_ready")
    s.h_lo_ready = sem("h_lo_ready")
    s.qk_drained = sem("qk_drained")
    s.conv_step = sem("conv_step")
    s.qk_ready = sem("qk_ready")
    s.gates_drained = sem("gates_drained")
    s.gate_step = sem("gate_step")
    s.fg_ready = sem("fg_ready")
    s.exp_ready = sem("exp_ready")
    s.ln_ready = sem("ln_ready")
    s.floor_ready = sem("floor_ready")
    s.cols_done = sem("cols_done")
    s.cols_ready = sem("cols_ready")
    s.v_ready = sem("v_ready")
    s.mrow_bcast = sem("mrow_bcast")
    s.s_done = sem("s_done")
    s.wt_ready = sem("wt_ready")
    s.wt_masked = sem("wt_masked")
    s.p_ready = sem("p_ready")
    s.psum_step = sem("psum_step")
    s.den_done = sem("den_done")
    s.den_step = sem("den_step")
    s.rden_ready = sem("rden_ready")
    s.dbc_done = sem("dbc_done")
    s.dbc_ready = sem("dbc_ready")
    s.o_done = sem("o_done")
    s.o_drained = sem("o_drained")
    s.y_ready = sem("y_ready")
    s.part_sq_ready = sem("part_sq_ready")
    s.ysq_ready = sem("ysq_ready")
    s.os_ready = sem("os_ready")
    s.og_ready = sem("og_ready")
    s.z_step = sem("z_step")
    s.z_ready = sem("z_ready")
    s.z_hi_ready = sem("z_hi_ready")
    s.z_lo_ready = sem("z_lo_ready")
    s.head_bcast = sem("head_bcast")
    s.bv_ready = sem("bv_ready")
    s.vs_landed = sem("vs_landed")
    s.qkb_ready = sem("qkb_ready")
    s.s2_done = sem("s2_done")
    s.neg_ready = sem("neg_ready")
    s.min_ready = sem("min_ready")
    s.prob_ready = sem("prob_ready")
    s.pt_done = sem("pt_done")
    s.pt_ready = sem("pt_ready")
    s.pv_done = sem("pv_done")
    s.out_ready = sem("out_ready")
    s.o2t_landed = sem("o2t_landed")
    s.mix_step = sem("mix_step")
    s.mix_exp = sem("mix_exp")
    s.mix_ready = sem("mix_ready")
    s.yt_done = sem("yt_done")
    s.yb_hi_ready = sem("yb_hi_ready")
    s.yb_lo_ready = sem("yb_lo_ready")
    s.final_ready = sem("final_ready")
    s.stored = sem("stored")
    s.raw_landed = [sem(f"raw_landed{slot}") for slot in range(2)]
    return s


def event(nu):
    return nu + HEADS_A * (nu >= 2)


HEAD_EVENT = 2
FIRST_SUMS = 3


def squares_before(nu):
    return FIRST_SUMS + DT * (nu - 1) if nu else 0


UNITS = [(o, hd, tp) for o in (1, 0) for tp in (0, 1) for hd in (0, 1)]
N_UNITS = len(UNITS)
SLOTS = N_UNITS + 2
MIX_SLOTS = (1, 2)
FINISH_SLOT = 4
V_ORDER = (0, 2, 3, 1)
EARLY_TILES = 4
FIRST_QK = 4
QK_TILES = 6


def first_tiles_order(early):
    last = DT - 2
    return ([(m, k) for m in range(2) for k in range(early)] + [(m, k) for k in range(early, last) for m in range(2)]
            + [(m, k) for m in range(2) for k in range(last, DT)])


B_OUT_PRODUCTS = (0, 0, 1, 2, 1, 2, 1, 2, 1, 1)


def b_out_steps(slot):
    start = sum(B_OUT_PRODUCTS[:slot])
    stop = start + B_OUT_PRODUCTS[slot] if slot < SLOTS else None
    return first_tiles_order(DT - 2)[start:stop]


class QkChunk:

    def __init__(self, pair, tile):
        self.pair, self.tile = pair, tile
        later = pair > PAIRS_A_PASS
        self.number = STAGE[f"b_qk{int(later)}"].first + QK_TILES * (pair - later * (PAIRS_A_PASS + 1)) + tile


def qk_chunks(attend):
    pair = 0 if attend is None else attend + 1
    if pair == PAIRS:
        return [QkChunk(PAIRS - 1, QK_TILES - 1)] + [None] * (QK_TILES - 1)
    chunks = [QkChunk(pair, tile) for tile in range(QK_TILES)]
    return chunks[:-1] + [None] if pair == PAIRS - 1 else chunks


CONV_STEP = (1, 2, 3, 5, 6, 8, 9, 10)


def order_2(ap, r):
    return ap[:, r::ST]


def build(nc, d):
    with ExitStack() as ctx:
        b = allocate(nc, ctx)
        s = signals(nc, ctx)
        block = ctx.enter_context(nc.Block())

        @block.sync
        def _(sp):
            sync_program(sp, b, s, d)

        @block.scalar
        def _(act):
            scalar_program(act, b, s)

        @block.vector
        def _(dve):
            vector_program(dve, b, s)

        @block.tensor
        def _(pe):
            tensor_program(pe, b, s)

        @block.gpsimd
        def _(pool):
            gpsimd_program(pool, b, s)


def sync_program(sp, b, s, d):
    def load_x(k):
        sp.dma_start(b.x[:, 2 * k:2 * k + 2, :], d["x_t"][2 * k:2 * k + 2].rearrange("m p t -> p m t")).then_inc(
            s.x_landed[k], 16)

    sp.dma_start(b.small[:, :], d["small"]).then_inc(s.small_landed, 16)
    load_x(0)
    half = UP_COLS // 2
    sp.dma_start(b.raw[:, 0, 0:half], d["w_up0"][0, :, 0:half]).then_inc(s.first_landed, 16)
    for k in range(1, DT // 2):
        load_x(k)

    def load(stage, c, g, slot, wait=True):
        if wait:
            sp.wait_ge(s.w_lo_ready, g - 1)
        src = d[stage.tensor][bass.ds(c + stage.skip, 1)].rearrange("a p c -> p (a c)")
        sp.dma_start(b.raw[:, slot, 0:stage.cols], src).then_inc(s.raw_landed[slot], 16)

    for stage in STAGES:
        start = 0
        if stage.first == 0:
            sp.dma_start(b.raw[:, 0, half:], d["w_up0"][0, :, half:]).then_inc(s.raw_landed[0], 16)
            load(stage, 1, 1, 1, wait=False)
            sp.dma_start(b.dist1[:, :, :], d["dist1"]).then_inc(s.tables_landed, 16)
            sp.dma_start(b.dist2[:, :, :], d["dist2"]).then_inc(s.tables_landed, 16)
            start = 1
        if stage.chunks == 2:
            for j in range(2):
                load(stage, j, stage.first + j, j)
            continue
        with sp.Fori(start, stage.chunks // 2) as i:
            for j in range(2):
                load(stage, i * 2 + j, i * 2 + (stage.first + j), j)

    for m in range(DT):
        sp.wait_ge(s.final_ready, m + 1)
        sp.dma_start(d["out_t"][m], b.out_t[:, m, :]).then_inc(s.stored, 16)
    sp.wait_ge(s.stored, 16 * DT)


def scalar_program(act, b, s):

    def split(g, slot, cols, landed):
        act.wait_ge(s.raw_landed[slot], landed)
        if not (isinstance(g, int) and g < 2):
            act.wait_ge(s.chunk_done, g - 1)
        act.activation(b.w_hi[:, slot, 0:cols], b.raw[:, slot, 0:cols], ACT.Copy).then_inc(s.w_hi_ready, 1)

    def split_ahead(g):
        if g + 2 < CHUNKS:
            split(g + 2, g % 2, COLS[g + 2], 16 * ((g + 2) // 2 + 1))

    def gained(nu, m):
        g = C_GAIN + nu * DT + m
        act.activation(b.xg_hi[:, m, :], b.x[:, m, :], ACT.Copy,
                       scale=b.small[:, g:g + 1]).then_inc(s.xg_hi_ready, 1)

    def squared(nu, m):
        if m or nu > 1:
            act.wait_ge(s.ssq_ready, squares_before(nu) + m)
        act.activation(b.xsq[:, :], b.x[:, m, :], ACT.Square).then_inc(s.xsq_ready, 1)

    def update(nu, m, g):
        if m < DT - 1:
            split_ahead(g)
        act.wait_ge(s.x_ready, DT * (nu - 1) + m + 1)
        if nu < N_NORMS - 1:
            gained(nu, m)
        if m == DT - 1:
            split_ahead(g)
        squared(nu, m)

    def up(n):
        stage, hidden = STAGE[f"up{n}"], FT * n

        def silu(c):
            act.wait_ge(s.gate_scaled, hidden + c + 1)
            act.activation(b.silu[:, 0, :], b.gate[:, 0, :], ACT.Silu).then_inc(s.silu_ready, 1)

        with act.Fori(0, FT // 2 - 1) as i:
            for j in range(2):
                split(i * 2 + (stage.first + j + 2), j, UP_COLS, i * 16 + 16 * (stage.first // 2 + 2))
                silu(i * 2 + j)
        for c in (FT - 2, FT - 1):
            split_ahead(stage.first + c)
            silu(c)

    def down(n, nu):
        stage = STAGE[f"down{n}"]
        for m in range(DT):
            split_ahead(stage.first + 2 * m)
            update(nu, m, stage.first + 2 * m + 1)

    def out_projection(name, nu):
        stage = STAGE[name]
        for m in range(DT):
            update(nu, m, stage.first + m)

    def mlstm():
        def convolved(t):
            act.wait_ge(s.conv_step, TAPS * (t + 1))
            bias = b.small[:, C_CONVB + t:C_CONVB + t + 1]
            act.activation(b.qk[:, t, :], b.conv[:, t % 2, :], ACT.Silu, bias=bias).then_inc(s.qk_ready, 1)

        for c in range(11):
            split_ahead(STAGE["a_qk"].first + c)
            if c - 1 in CONV_STEP:
                convolved(CONV_STEP.index(c - 1))
        convolved(7)
        act.wait_ge(s.gate_step, 3)
        act.activation(b.fg[0:SPAN, :], b.gates[64:64 + SPAN, :], ACT.Copy).then_inc(s.fg_ready, 1)
        act.wait_ge(s.gate_step, 4)
        act.activation(b.soft[0:SPAN, :], b.soft[0:SPAN, :], ACT.Exp).then_inc(s.exp_ready, 1)
        act.wait_ge(s.exp_ready, 1)
        act.activation(b.soft[0:SPAN, :], b.soft[0:SPAN, :], ACT.Ln, bias=1.0).then_inc(s.ln_ready, 1)
        split_ahead(STAGE["a_v"].first + 1)
        act.wait_ge(s.gate_step, 12)
        act.activation(b.floor[0:SPAN, :], b.floor[0:SPAN, :], ACT.Exp, scale=-1.0).then_inc(s.floor_ready, 1)
        for c in range(1, 4):
            if c == 2:
                split_ahead(STAGE["a_v"].first + c)
            if c % 2:
                act.wait_ge(s.chunk_done, STAGE["a_v"].first + c + 1)
                for i in V_ORDER:
                    bank = i if c == 3 else 4 + i
                    cols = slice(512 * (c // 2), 512 * (c // 2) + 512)
                    act.activation(b.v[:, i, cols], b.ps[:, bank, :], ACT.Copy,
                                   scale=b.rcol[:, i:i + 1]).then_inc(s.v_ready, 1)

        split_ahead(STAGE["a_v"].first + 3)

        def weights(u):
            h, backward = u // 2, u % 2
            row = h + BACK * backward
            act.wait_ge(s.mrow_bcast, u + 1)
            if u == 0:
                act.wait_ge(s.cols_ready, 1)
            for j in range(ST):
                si, n = (ST - 1 - j if backward else j), ST * u + j
                lo, hi, _ = band(si, backward)
                if n >= 2:
                    act.wait_ge(s.p_ready, n - 1)
                act.activation(b.wt[:, n % 2, lo:hi], b.ps[:, 0, lo:hi], ACT.Exp,
                               bias=b.afcol[:, 0, si, row:row + 1]).then_inc(s.wt_ready, 1)

        def squares(h):
            act.wait_ge(s.y_ready, h + 1)
            act.activation(b.part[:, :, :], b.y[:, 2 * h:2 * h + 2, :], ACT.Square).then_inc(s.part_sq_ready, 1)

        weights(0)
        stage = STAGE["a_o"]
        for u in range(2 * HEADS_A):
            if u + 1 < 2 * HEADS_A:
                weights(u + 1)
            if u and u % 2 == 0:
                squares(u // 2 - 1)
            split_ahead(stage.first + u)
            if u == 2 * HEADS_A - 1:
                squares(HEADS_A - 1)
            if u % 2:
                for t in (u - 1, u):
                    act.wait_ge(s.os_ready, t + 1)
                    act.activation(b.og[:, t, :], b.og[:, t, :], ACT.Sigmoid).then_inc(s.og_ready, 1)

    def b_values(pas):
        stage = STAGE[f"b_v{pas}"]
        for c in range(6):
            if c < 5:
                split_ahead(stage.first + c)
            if c % 2:
                group = c // 2
                v = (b.v1, b.v2, b.v3)[group]
                act.wait_ge(s.chunk_done, stage.first + c + 1)
                if pas and group == 0:
                    act.wait_ge(s.pv_done, 8 * PAIRS_A_PASS)
                if pas == 0 and group == 0:
                    act.wait_ge(s.rcol_ready, event(4) + 1)
                for i in range(ST):
                    col = i + (ST if group else 0)
                    act.activation(v[:, i, :], b.ps[:, 4 * (group % 2) + i, :], ACT.Copy,
                                   scale=b.rcol[:, col:col + 1]).then_inc(s.bv_ready, 1)
                    if c == 5 and i == 1:
                        split_ahead(stage.first + c)

    def b_slot(pair, k):
        n = 8 * pair + k
        if k < 8:
            o, hd, tp = UNITS[k]
            ob = (b.o1, b.o2)[o]
            act.wait_ge(s.min_ready, n + 1)
            if n:
                act.wait_ge(s.pt_done, n)
            for t in range(2):
                i = 2 * tp + t
                act.activation(b.prob[:, 256 * t:256 * t + 256], b.neg[:, 256 * t:256 * t + 256], ACT.Exp,
                               bias=ob[:, i, hd, DH + 1:DH + 2], scale=-1.0,
                               accum_out=ob[:, i, hd, DH:DH + 1]).then_inc(s.prob_ready, 1)
        if 1 <= k <= 8:
            act.wait_ge(s.pt_done, n)
            if n >= 2:
                act.wait_ge(s.pv_done, n - 1)
            act.activation(b.prob_t[:, :], b.ps[:, 4 + (n - 1) % 2, :], ACT.Copy).then_inc(s.pt_ready, 1)

    def b_mix(pair):
        act.wait_ge(s.mix_step, 9 * pair + 3)
        act.activation(b.wg[:, :, :], b.wg[:, :, :], ACT.Exp).then_inc(s.mix_exp, 1)

    def b_finish(pair):
        act.wait_ge(s.yt_done, pair + 1)
        act.activation(b.yb_hi[:, pair, :], b.ps[:, 7, :], ACT.Copy).then_inc(s.yb_hi_ready, 1)

    def b_pair(chunks, attend):
        for slot in range(2 * 6):
            if attend is not None and slot < SLOTS:
                b_slot(attend, slot)
                if attend and slot == MIX_SLOTS[0]:
                    b_mix(attend - 1)
                if attend and slot == FINISH_SLOT:
                    b_finish(attend - 1)
            if slot % 2 and chunks[slot // 2]:
                split_ahead(chunks[slot // 2].number)

    def dilated():
        b_values(0)
        b_pair(qk_chunks(None), None)
        for pair in range(PAIRS_A_PASS):
            b_pair(qk_chunks(pair), pair)
        b_values(1)
        for pair in range(PAIRS_A_PASS, PAIRS):
            b_pair(qk_chunks(pair), pair)
        b_mix(PAIRS - 1)
        b_finish(PAIRS - 1)

    act.wait_ge(s.small_landed, 16)
    half = UP_COLS // 2
    for m in range(DT):
        if m % 2 == 0:
            act.wait_ge(s.x_landed[m // 2], 16)
        gained(0, m)
        if m == 1:
            act.wait_ge(s.first_landed, 16)
            act.activation(b.w_hi[:, 0, 0:half], b.raw[:, 0, 0:half], ACT.Copy).then_inc(s.first_hi_ready, 1)
    act.wait_ge(s.raw_landed[0], 16)
    act.activation(b.w_hi[:, 0, half:], b.raw[:, 0, half:], ACT.Copy).then_inc(s.w_hi_ready, 1)
    split(1, 1, COLS[1], 16)
    for half in range(2):
        tiles = slice(DT // 2 * half, DT // 2 * (half + 1))
        act.activation(b.first_sq[:, tiles, :], b.x[:, tiles, :], ACT.Square).then_inc(s.first_sq_ready, 1)
    up(0)
    down(0, 1)
    mlstm()
    out_projection("a_out", 2)
    up(1)
    down(1, 3)
    up(2)
    down(2, 4)
    dilated()
    out_projection("b_out", 5)
    up(3)
    down(3, 6)


def vector_program(dve, b, s):

    def split(g, slot, cols):
        dve.wait_ge(s.w_hi_ready, g + 1)
        dve.tensor_tensor(b.w_lo[:, slot, 0:cols], b.raw[:, slot, 0:cols],
                          b.w_hi[:, slot, 0:cols].bitcast(F32), ALU.subtract).then_inc(s.w_lo_ready, 1)

    def split_ahead(g):
        if g + 2 < CHUNKS:
            split(g + 2, g % 2, COLS[g + 2])

    def low_gained(nu, m):
        g = C_GAIN + nu * DT + m
        dve.wait_ge(s.xg_hi_ready, DT * nu + m + 1)
        dve.scalar_tensor_tensor(out=b.xg_lo[:, m, :], in0=b.x[:, m, :], scalar=b.small[:, g:g + 1],
                                 in1=b.xg_hi[:, m, :].bitcast(F32), op0=ALU.mult,
                                 op1=ALU.subtract).then_inc(s.xg_lo_ready, 1)

    def add_squares(nu, m):
        dve.wait_ge(s.xsq_ready, DT * (nu - 1) + m + 1)
        if m == 0:
            dve.tensor_copy(b.ssq[:, :], b.xsq[:, :]).then_inc(s.ssq_ready, 1)
        else:
            dve.wait_ge(s.ssq_ready, squares_before(nu) + m)
            dve.tensor_tensor(b.ssq[:, :], b.ssq[:, :], b.xsq[:, :], ALU.add).then_inc(s.ssq_ready, 1)

    def update(nu, m, bank, scale, g):
        x = b.x[:, m, :]
        dve.wait_ge(s.chunk_done, g + 1)
        dve.scalar_tensor_tensor(out=x, in0=b.ps[:, bank, :], scalar=scale, in1=x,
                                 op0=ALU.mult, op1=ALU.add).then_inc(s.x_ready, 1)
        if m < DT - 1:
            split_ahead(g)
        if nu < N_NORMS - 1:
            low_gained(nu, m)
        if m == DT - 1:
            split_ahead(g)
        add_squares(nu, m)

    def mean_columns(e, cols, n):
        dve.wait_ge(s.sums_done, e + 1)
        dve.tensor_scalar(b.mean_sq[:, 0:cols], b.ps[:, 6, 0:cols], 1.0 / n, EPS, ALU.mult,
                          ALU.add).then_inc(s.mean_ready, 1)

    def newton_columns(e, cols):
        ms, rs, nt = b.mean_sq[:, 0:cols], b.rsqrt[:, 0:cols], b.newton[:, 0:cols]
        dve.wait_ge(s.rsqrt_ready, e + 1)
        dve.tensor_tensor(nt, ms, rs, ALU.mult).then_inc(s.newton_step, 1)
        dve.wait_ge(s.newton_step, 3 * e + 1)
        dve.tensor_tensor(nt, nt, rs, ALU.mult).then_inc(s.newton_step, 1)
        dve.wait_ge(s.newton_step, 3 * e + 2)
        dve.tensor_scalar(nt, nt, -0.5, 1.5, ALU.mult, ALU.add).then_inc(s.newton_step, 1)
        dve.wait_ge(s.newton_step, 3 * e + 3)
        dve.tensor_tensor(b.rcol[:, 0:cols], rs, nt, ALU.mult).then_inc(s.rcol_ready, 1)

    def rsqrt_columns(e, cols, n):
        mean_columns(e, cols, n)
        newton_columns(e, cols)

    def keep_rinv(nu):
        dve.wait_ge(s.bcast_done, nu + 1)
        dve.tensor_copy(b.rinv[:, :], b.ps[:, 7, :]).then_inc(s.rinv_ready, 1)

    def up(n, nu):
        stage, hidden = STAGE[f"up{n}"], FT * n

        def evict(c, par):
            dve.wait_ge(s.chunk_done, c + (stage.first + 1))
            dve.wait_ge(s.rinv_ready, nu + 1)
            dve.tensor_tensor(b.gate[:, 0, :], b.ps[:, 2 * par, :], b.rinv[:, :], ALU.mult).then_inc(s.gate_scaled, 1)
            dve.tensor_tensor(b.up[:, 0, :], b.ps[:, 2 * par + 1, :], b.rinv[:, :], ALU.mult).then_inc(s.gu_drained, 1)
            dve.wait_ge(s.gu_drained, c + (hidden + 1))
            dve.wait_ge(s.silu_ready, c + (hidden + 1))
            dve.tensor_tensor(b.h[:, 0, :], b.silu[:, 0, :], b.up[:, 0, :], ALU.mult).then_inc(s.h_ready, 1)
            tile = bass.ds(c, 1)
            dve.wait_ge(s.h_ready, c + (hidden + 1))
            dve.tensor_copy(b.h_hi[:, tile, :], b.h[:, :, :]).then_inc(s.h_hi_ready, 1)
            dve.wait_ge(s.h_hi_ready, c + (hidden + 1))
            dve.tensor_tensor(b.h_lo[:, tile, :], b.h[:, :, :], b.h_hi[:, tile, :].bitcast(F32),
                              ALU.subtract).then_inc(s.h_lo_ready, 1)

        rsqrt_columns(event(nu), ST, D)
        keep_rinv(nu)
        with dve.Fori(0, FT // 2 - 1) as i:
            for j in range(2):
                split(i * 2 + (stage.first + j + 2), j, UP_COLS)
                evict(i * 2 + j, j)
        for c in (FT - 2, FT - 1):
            split_ahead(stage.first + c)
            evict(c, c % 2)

    def down(n, nu):
        stage = STAGE[f"down{n}"]
        for m in range(DT):
            split_ahead(stage.first + 2 * m)
            update(nu, m, 4 + m % 2, 0.5, stage.first + 2 * m + 1)

    def out_projection(name, nu, bank, later):
        stage = STAGE[name]
        for m in range(DT):
            update(nu, m, (bank if m < 2 else later) + m % 2, 1.0, stage.first + m)

    def mlstm():
        nu = 1
        stage = STAGE["a_qk"]
        dve.memset(b.padded[:, :], 0.0)

        def convolve(t):
            step = TAPS * t
            dve.wait_ge(s.chunk_done, stage.first + t + 1)
            if t:
                dve.wait_ge(s.conv_step, step)
            dve.tensor_tensor(b.padded[:, 2:2 + SEQ], b.ps[:, t % 4, :], b.rinv[:, :], ALU.mult).then_inc(s.qk_drained, 1)
            dve.wait_ge(s.qk_drained, t + 1)
            if t >= 2:
                dve.wait_ge(s.qk_ready, t - 1)
            for k in range(TAPS):
                w = b.small[:, C_CONVW + TAPS * t + k:C_CONVW + TAPS * t + k + 1]
                src = b.padded[:, k:k + SEQ]
                if k == 0:
                    dve.tensor_scalar(b.conv[:, t % 2, :], src, w, None, ALU.mult).then_inc(s.conv_step, 1)
                else:
                    dve.wait_ge(s.conv_step, step + k)
                    dve.scalar_tensor_tensor(out=b.conv[:, t % 2, :], in0=src, scalar=w, in1=b.conv[:, t % 2, :],
                                             op0=ALU.mult, op1=ALU.add).then_inc(s.conv_step, 1)

        for c in range(11):
            split_ahead(stage.first + c)
            if c == 0:
                rsqrt_columns(event(nu), ST, D)
            if c == 1:
                keep_rinv(nu)
                dve.wait_ge(s.rinv_ready, nu + 1)
            if c in CONV_STEP:
                convolve(CONV_STEP.index(c))
        gates_stage = STAGE["a_gates"]
        fwd, bwd, rows = slice(0, HEADS_A), slice(BACK, SPAN), slice(0, SPAN)
        dve.memset(b.bsum[rows, :], 0.0).then_inc(s.gate_step, 1)
        dve.memset(b.mrow[rows, :], 0.0).then_inc(s.gate_step, 1)
        dve.wait_ge(s.chunk_done, gates_stage.first + 2)
        dve.tensor_tensor(b.gates[:, :], b.ps[:, 0, :], b.rinv[:, :], ALU.mult).then_inc(s.gates_drained, 1)
        dve.wait_ge(s.gates_drained, 1)
        dve.tensor_scalar(b.gates[:, :], b.gates[:, :], b.small[:, C_GATEB:C_GATEB + 1], None,
                          ALU.add).then_inc(s.gate_step, 1)
        dve.wait_ge(s.fg_ready, 1)
        dve.scalar_tensor_tensor(out=b.soft[rows, :], in0=b.fg[rows, :], scalar=-1.0, in1=b.fg[rows, :],
                                 op0=ALU.mult, op1=ALU.min).then_inc(s.gate_step, 1)
        dve.wait_ge(s.ln_ready, 1)
        dve.scalar_tensor_tensor(out=b.logf[rows, :], in0=b.fg[rows, :], scalar=0.0, in1=b.soft[rows, :],
                                 op0=ALU.min, op1=ALU.subtract).then_inc(s.gate_step, 1)
        dve.wait_ge(s.gate_step, 5)
        dve.tensor_tensor_scan(b.bsum[fwd, :], b.logf[fwd, :], b.logf[fwd, :], 0.0, ALU.add,
                               ALU.bypass).then_inc(s.gate_step, 1)
        dve.tensor_tensor_scan(b.bsum[bwd, ::-1], b.logf[bwd, ::-1], b.logf[bwd, ::-1], 0.0, ALU.add,
                               ALU.bypass).then_inc(s.gate_step, 1)
        split_ahead(STAGE["a_v"].first + 1)
        dve.wait_ge(s.gate_step, 7)
        dve.tensor_tensor(b.arow[rows, :], b.gates[rows, :], b.bsum[rows, :], ALU.subtract).then_inc(s.gate_step, 1)
        dve.wait_ge(s.gate_step, 8)
        dve.tensor_tensor_scan(b.mrow[fwd, :], b.arow[fwd, :], b.arow[fwd, :], 0.0, ALU.max,
                               ALU.max).then_inc(s.gate_step, 1)
        dve.tensor_tensor_scan(b.mrow[bwd, ::-1], b.arow[bwd, ::-1], b.arow[bwd, ::-1], 0.0, ALU.max,
                               ALU.max).then_inc(s.gate_step, 1)
        dve.wait_ge(s.gate_step, 10)
        dve.tensor_tensor(b.floor[rows, :], b.bsum[rows, :], b.mrow[rows, :], ALU.add).then_inc(s.gate_step, 1)
        dve.wait_ge(s.gate_step, 11)
        dve.tensor_scalar(b.mrow[rows, :], b.mrow[rows, :], -1.0, None, ALU.mult).then_inc(s.gate_step, 1)
        split_ahead(STAGE["a_v"].first + 2)
        dve.wait_ge(s.cols_done, 1)
        dve.tensor_copy(b.afcol[:, :, :, :], b.ps[:, 6, 0:2 * ST * SPAN].rearrange(
            "p (k i r) -> p k i r", k=2, i=ST)).then_inc(s.cols_ready, 1)
        split_ahead(STAGE["a_v"].first + 3)

        def products(u, tiles):
            backward = u % 2
            if u >= 2 and tiles[0] == 0:
                dve.wait_ge(s.o_done, u - 1)
            for j in tiles:
                si, n = (ST - 1 - j if backward else j), ST * u + j
                lo, hi, at = band(si, backward)
                dve.wait_ge(s.wt_masked, n + 1)
                dve.wait_ge(s.s_done, n + 1)
                dve.scalar_tensor_tensor(out=b.p[:, u % 2, at:at + hi - lo], in0=b.ps[:, 2 + n % 2, lo:hi],
                                         scalar=DQK ** -0.5, in1=b.wt[:, n % 2, lo:hi], op0=ALU.mult,
                                         op1=ALU.mult).then_inc(s.p_ready, 1)

        def source_sums(u):
            backward = u % 2
            for j in range(1, ST):
                si = ST - 1 - j if backward else j
                lo, hi, at = band(si, backward)
                if j == 1:
                    start, _, base = band(ST - 1 if backward else 0, backward)
                    others = b.p[:, u % 2, base + lo - start:base + hi - start]
                else:
                    others = b.psum[:, lo:hi]
                    dve.wait_ge(s.psum_step, (ST - 1) * u + j - 1)
                dve.wait_ge(s.p_ready, ST * u + j + 1)
                dve.tensor_tensor(b.psum[:, lo:hi], others, b.p[:, u % 2, at:at + hi - lo],
                                  ALU.add).then_inc(s.psum_step, 1)

        def denominators(u):
            row = u // 2 + BACK * (u % 2)
            den = b.ps[:, 6, 320 + ST * u:320 + ST * u + ST]
            dve.wait_ge(s.den_done, u + 1)
            dve.scalar_tensor_tensor(out=b.dcol[:, :], in0=den, scalar=-1.0, in1=b.afcol[:, 1, :, row],
                                     op0=ALU.mult, op1=ALU.max).then_inc(s.den_step, 1)
            dve.wait_ge(s.den_step, 2 * u + 1)
            dve.tensor_tensor(b.dcol[:, :], den, b.dcol[:, :], ALU.max).then_inc(s.den_step, 1)
            dve.wait_ge(s.den_step, 2 * u + 2)
            dve.reciprocal(b.rden[:, u % 2, :], b.dcol[:, :]).then_inc(s.rden_ready, 1)

        def evict(u):
            h, backward = u // 2, u % 2
            dve.wait_ge(s.dbc_done, u + 1)
            dve.tensor_copy(b.dbc[:, :], b.ps[:, 7, :]).then_inc(s.dbc_ready, 1)
            dve.wait_ge(s.dbc_ready, u + 1)
            dve.wait_ge(s.o_done, u + 1)
            y = b.y[:, 2 * h:2 * h + 2, :]
            out = b.part if backward else y
            if backward and h:
                dve.wait_ge(s.ysq_ready, h)
            for e in range(2):
                ins = dve.tensor_tensor(out[:, e, :], b.ps[:, 4 + e, :], b.dbc[:, :], ALU.mult)
            ins.then_inc(s.o_drained, 1)
            if backward:
                dve.wait_ge(s.o_drained, u + 1)
                dve.tensor_tensor(y, y, b.part[:, :, :], ALU.add).then_inc(s.y_ready, 1)

        def head_squares(h):
            dve.wait_ge(s.part_sq_ready, h + 1)
            dve.tensor_tensor(b.ysq[:, :], b.part[:, 0, :], b.part[:, 1, :], ALU.add).then_inc(s.ysq_ready, 1)

        def gated(t, bank):
            dve.wait_ge(s.og_ready, t + 1)
            if t:
                dve.wait_ge(s.z_lo_ready, t)
            dve.scalar_tensor_tensor(out=b.z[:, :], in0=b.og[:, t, :],
                                     scalar=b.small[:, C_HEADG + t:C_HEADG + t + 1], in1=b.y[:, t, :],
                                     op0=ALU.mult, op1=ALU.mult).then_inc(s.z_step, 1)
            dve.wait_ge(s.z_step, t + 1)
            dve.wait_ge(s.head_bcast, t // 2 + 1)
            dve.tensor_tensor(b.z[:, :], b.ps[:, bank, :], b.z[:, :], ALU.mult).then_inc(s.z_ready, 1)
            dve.wait_ge(s.z_ready, t + 1)
            dve.tensor_copy(b.z_hi[:, t, :], b.z[:, :]).then_inc(s.z_hi_ready, 1)
            dve.wait_ge(s.z_hi_ready, t + 1)
            dve.tensor_tensor(b.z_lo[:, t, :], b.z[:, :], b.z_hi[:, t, :].bitcast(F32),
                              ALU.subtract).then_inc(s.z_lo_ready, 1)

        stage = STAGE["a_o"]

        def gate(u):
            dve.wait_ge(s.chunk_done, stage.first + u + 1)
            dve.tensor_tensor(b.og[:, u, :], b.ps[:, 1, :], b.rinv[:, :], ALU.mult).then_inc(s.os_ready, 1)

        products(0, range(ST))
        source_sums(0)
        last = 2 * HEADS_A - 1
        for u in range(last):
            products(u + 1, range(2))
            if u:
                evict(u - 1)
            if u >= 3 and u % 2:
                mean_columns(HEAD_EVENT + (u - 3) // 2, ST, DV)
            products(u + 1, range(2, ST))
            if u >= 3 and u % 2:
                newton_columns(HEAD_EVENT + (u - 3) // 2, ST)
            if u and u % 2 == 0:
                head_squares(u // 2 - 1)
            denominators(u)
            source_sums(u + 1)
            split_ahead(stage.first + u)
            gate(u)
            if u >= 4 and u % 2 == 0:
                gated(u - 4, 7)
                gated(u - 3, 7)
        evict(last - 1)
        rsqrt_columns(HEAD_EVENT + HEADS_A - 2, ST, DV)
        denominators(last)
        gated(DT - 4, 0)
        evict(last)
        split_ahead(stage.first + last)
        head_squares(HEADS_A - 1)
        gate(last)
        mean_columns(HEAD_EVENT + HEADS_A - 1, ST, DV)
        gated(DT - 3, 0)
        newton_columns(HEAD_EVENT + HEADS_A - 1, ST)
        gated(DT - 2, 7)
        gated(DT - 1, 7)

    def b_values(pas):
        stage = STAGE[f"b_v{pas}"]
        for c in range(6):
            if pas == 0 and c == 1:
                keep_rinv(4)
            split_ahead(stage.first + c)
            if pas == 0 and c == 0:
                rsqrt_columns(event(4), 2 * ST, D)

    def b_slot(pair, k):
        n = 8 * pair + k
        if k < 8:
            o, hd, tp = UNITS[k]
            ob = (b.o1, b.o2)[o]
            head = 2 * pair + hd
            dist = b.dist2[:, :, :].to_broadcast([P, 2, 2 * P]) if o else b.dist1[:, tp:tp + 2, :]
            if pair and k in (0, N_UNITS // 2):
                if k:
                    dve.wait_ge(s.mix_ready, pair)
                else:
                    dve.wait_ge(s.o2t_landed, 64 * pair)
            dve.wait_ge(s.s2_done, n + 1)
            if n:
                dve.wait_ge(s.prob_ready, 2 * n)
            neg = b.neg[:, :].rearrange("p (t k) -> p t k", t=2)
            dve.scalar_tensor_tensor(out=neg, in0=dist, scalar=b.small[:, C_SLOPE + head:C_SLOPE + head + 1],
                                     in1=b.ps[:, 2 + hd, :].rearrange("p (t k) -> p t k", t=2),
                                     op0=ALU.mult, op1=ALU.subtract).then_inc(s.neg_ready, 1)
            dve.wait_ge(s.neg_ready, n + 1)
            dve.tensor_reduce(ob[:, 2 * tp:2 * tp + 2, hd, DH + 1:DH + 2], neg, AX.X, ALU.min).then_inc(s.min_ready, 1)
        if k >= 2:
            o, hd, tp = UNITS[k - 2]
            ob = (b.o1, b.o2)[o]
            dve.wait_ge(s.pv_done, n - 1)
            half = 128 * (k % 2)
            dve.tensor_copy(ob[:, 2 * tp:2 * tp + 2, hd, 0:DH], b.ps[:, 6, half:half + 128].rearrange(
                "p (t d) -> p t d", t=2)).then_inc(s.out_ready, 1)

    def flat(ap, c):
        return ap[:, :, c]

    def orders():
        return [o[:, :, :, :].rearrange("p i h c -> p (i h) c") for o in (b.o1, b.o2t)]

    def b_mix_maxima(pair):
        step = 9 * pair
        o1, o2 = orders()
        dve.wait_ge(s.o2t_landed, 64 * (pair + 1))
        dve.wait_ge(s.prob_ready, 16 * (pair + 1))
        dve.tensor_tensor(b.mn[:, :], flat(o1, DH + 1), flat(o2, DH + 1), ALU.min).then_inc(s.mix_step, 1)
        dve.wait_ge(s.mix_step, step + 1)
        for k, o in enumerate((o1, o2)):
            dve.tensor_tensor(b.wg[:, k, :], b.mn[:, :], flat(o, DH + 1), ALU.subtract).then_inc(s.mix_step, 1)

    def b_mix(pair):
        step = 9 * pair
        o1, o2 = orders()
        dve.wait_ge(s.mix_exp, pair + 1)
        for k, o in enumerate((o1, o2)):
            dve.tensor_tensor(b.wd[:, k, :], b.wg[:, k, :], flat(o, DH), ALU.mult).then_inc(s.mix_step, 1)
        dve.wait_ge(s.mix_step, step + 5)
        dve.tensor_tensor(b.den[:, :], b.wd[:, 0, :], b.wd[:, 1, :], ALU.add).then_inc(s.mix_step, 1)
        dve.wait_ge(s.mix_step, step + 6)
        dve.reciprocal(b.den[:, :], b.den[:, :]).then_inc(s.mix_step, 1)
        dve.wait_ge(s.mix_step, step + 7)
        den = b.den[:, :].unsqueeze(1).to_broadcast([P, 2, 8])
        dve.tensor_tensor(b.wg[:, :, :], b.wg[:, :, :], den, ALU.mult).then_inc(s.mix_step, 1)
        dve.wait_ge(s.mix_step, step + 8)
        if pair:
            dve.wait_ge(s.yt_done, pair)
        for k, (o, out) in enumerate(((o1, b.ssq), (o2, b.xsq))):
            w = b.wg[:, k, :].unsqueeze(2).to_broadcast([P, 8, DH])
            ins = dve.tensor_tensor(out[:, :].rearrange("p (g d) -> p g d", g=8), o[:, :, 0:DH], w, ALU.mult)
        ins.then_inc(s.mix_step, 1)
        dve.wait_ge(s.mix_step, step + 9)
        dve.tensor_tensor(b.ssq[:, :], b.ssq[:, :], b.xsq[:, :], ALU.add).then_inc(s.mix_ready, 1)

    def b_finish(pair):
        dve.wait_ge(s.yb_hi_ready, pair + 1)
        dve.tensor_tensor(b.yb_lo[:, pair, :], b.ps[:, 7, :], b.yb_hi[:, pair, :].bitcast(F32),
                          ALU.subtract).then_inc(s.yb_lo_ready, 1)

    def b_evict(done, project, c):
        dve.wait_ge(s.chunk_done, done)
        if project >= 2 and c == 0:
            dve.wait_ge(s.s2_done, N_UNITS * (project - 1))
        out, src, rinv = b.qkb[:, project % 2, c, :], b.ps[:, c % 2, :], b.rinv[:, :]
        if c < FIRST_QK:
            out = out.rearrange("p (r j) -> p j r", r=ST)
            src, rinv = (a.rearrange("p (j r) -> p j r", r=ST) for a in (src, rinv))
        if c % 2 == 0:
            dve.scalar_tensor_tensor(out=out, in0=src, scalar=DH ** -0.5, in1=rinv, op0=ALU.mult,
                                     op1=ALU.mult).then_inc(s.qkb_ready, 1)
        else:
            dve.tensor_tensor(out, src, rinv, ALU.mult).then_inc(s.qkb_ready, 1)

    def b_pair(chunks, attend):
        for slot in range(2 * 6):
            if attend is not None and slot < SLOTS:
                b_slot(attend, slot)
                if attend and slot == MIX_SLOTS[0]:
                    b_mix_maxima(attend - 1)
                if attend and slot == MIX_SLOTS[1]:
                    b_mix(attend - 1)
                if attend and slot == FINISH_SLOT:
                    b_finish(attend - 1)
            chunk = chunks[slot // 2]
            if slot % 2 and chunk:
                b_evict(chunk.number + 1, chunk.pair, chunk.tile)
                split_ahead(chunk.number)

    def dilated():
        b_values(0)
        dve.wait_ge(s.rinv_ready, 5)
        dve.wait_ge(s.tables_landed, 32)
        b_pair(qk_chunks(None), None)
        for pair in range(PAIRS_A_PASS):
            b_pair(qk_chunks(pair), pair)
        b_values(1)
        for pair in range(PAIRS_A_PASS, PAIRS):
            b_pair(qk_chunks(pair), pair)
        b_mix_maxima(PAIRS - 1)
        b_mix(PAIRS - 1)
        b_finish(PAIRS - 1)

    def final():
        rsqrt_columns(event(6), ST, D)
        dve.wait_ge(s.bcast_done, 7)
        for m in range(DT):
            g = C_GAIN + 6 * DT + m
            dve.scalar_tensor_tensor(out=b.out_t[:, m, :], in0=b.x[:, m, :], scalar=b.small[:, g:g + 1],
                                     in1=b.ps[:, 7, :], op0=ALU.mult, op1=ALU.mult).then_inc(s.final_ready, 1)

    dve.memset(b.ones[:, :], 1.0).then_inc(s.consts_ready, 1)
    dve.memset(b.exponent[:, :], -0.5).then_inc(s.consts_ready, 1)
    dve.wait_ge(s.small_landed, 16)
    half = UP_COLS // 2
    for m in range(DT):
        low_gained(0, m)
        if m == 1:
            dve.wait_ge(s.first_hi_ready, 1)
            dve.tensor_tensor(b.w_lo[:, 0, 0:half], b.raw[:, 0, 0:half], b.w_hi[:, 0, 0:half].bitcast(F32),
                              ALU.subtract).then_inc(s.first_lo_ready, 1)
    dve.wait_ge(s.w_hi_ready, 1)
    dve.tensor_tensor(b.w_lo[:, 0, half:], b.raw[:, 0, half:], b.w_hi[:, 0, half:].bitcast(F32),
                      ALU.subtract).then_inc(s.w_lo_ready, 1)
    split(1, 1, COLS[1])
    sq, n = b.first_sq, DT // 2
    dve.wait_ge(s.first_sq_ready, 2)
    for step in range(FIRST_SUMS):
        if step:
            dve.wait_ge(s.ssq_ready, step)
        out = sq[:, 0:n, :] if n > 1 else b.ssq[:, :].unsqueeze(1)
        dve.tensor_tensor(out, sq[:, 0:n, :], sq[:, n:2 * n, :], ALU.add).then_inc(s.ssq_ready, 1)
        n //= 2
    up(0, 0)
    down(0, 1)
    mlstm()
    out_projection("a_out", 2, 2, 2)
    up(1, 2)
    down(1, 3)
    up(2, 3)
    down(2, 4)
    dilated()
    out_projection("b_out", 5, 0, 4)
    up(3, 5)
    down(3, 6)
    final()


def tensor_program(pe, b, s):
    ident = b.small[:, C_ID:C_ID + P]

    def split_matmul(out, a_hi, a_lo, x_hi, x_lo, start, stop):
        pe.matmul(out, a_hi, x_hi, start=start, stop=False)
        pe.matmul(out, a_hi, x_lo, start=False, stop=False)
        return pe.matmul(out, a_lo, x_hi, start=False, stop=stop)

    def weight_tile(slot, n):
        cols = slice(P * n, P * n + P)
        return b.w_hi[:, slot, cols], b.w_lo[:, slot, cols]

    def column_sums(out, rows, tiles=None):
        for i in range(ST):
            lhs = tiles(rows, i) if tiles else rows[:, P * i:P * i + P]
            ins = pe.matmul(out[:, i:i + 1], lhs, b.ones[:, :], start=True, stop=True)
        return ins

    def broadcast(out, cols):
        for i in range(ST):
            ins = pe.matmul(out[:, P * i:P * i + P], cols[:, i:i + 1].to_broadcast([P, P]), ident,
                            start=True, stop=True)
        return ins

    def norm_sums(nu):
        pe.wait_ge(s.ssq_ready, squares_before(nu + 1))
        ins = column_sums(b.ps[:, 6, 0:ST], b.ssq[:, :])
        if nu == 4:
            ins = column_sums(b.ps[:, 6, ST:2 * ST], b.ssq[:, :], order_2)
        ins.then_inc(s.sums_done, 1)

    def norm_broadcast(nu):
        pe.wait_ge(s.rcol_ready, event(nu) + 1)
        broadcast(b.ps[:, 7, :], b.rcol[:, 0:ST]).then_inc(s.bcast_done, 1)

    def project(bank, slot, tiles, x_hi, x_lo, first=True, last=True, k0=0, w0=0, ready=None):
        for k in range(tiles):
            if ready is not None:
                pe.wait_ge(ready[0], ready[1] + k0 + k + 1)
            w_hi, w_lo = weight_tile(slot, w0 + k)
            ins = split_matmul(b.ps[:, bank, :], w_hi, w_lo, x_hi[:, k0 + k, :], x_lo[:, k0 + k, :],
                               first and k == 0, last and k == tiles - 1)
        return ins

    def late_tile(nu, one, other, before_other):
        ready = (s.xg_lo_ready, DT * nu)
        project(0, one[0], DT - 1, b.xg_hi, b.xg_lo, True, False, w0=one[1], ready=ready)
        before_other()
        project(1, other[0], EARLY_TILES, b.xg_hi, b.xg_lo, True, False, w0=other[1])
        return project(0, one[0], 1, b.xg_hi, b.xg_lo, False, True, DT - 1, one[1] + DT - 1, ready=ready)

    def up(n, nu):
        stage, hidden = STAGE[f"up{n}"], FT * n

        def chunk(c, par, first=False):
            if isinstance(c, int) and c == 0:
                if stage.first == 0:
                    pe.wait_ge(s.first_lo_ready, 1)
                else:
                    pe.wait_ge(s.w_lo_ready, stage.first + 1)
            else:
                pe.wait_ge(s.w_lo_ready, c + (stage.first + 1))
            if not (isinstance(c, int) and c < 2):
                pe.wait_ge(s.gu_drained, c + (hidden - 1))
            if first and nu:
                late_tile(nu, (0, 0), (0, DT), lambda: None)
                project(1, 0, DT - EARLY_TILES, b.xg_hi, b.xg_lo, False, True, EARLY_TILES,
                        DT + EARLY_TILES).then_inc(s.chunk_done, 1)
                norm_sums(nu)
                return
            ready = (s.xg_lo_ready, DT * nu) if first else None
            if isinstance(c, int) and c == 1:
                half = DT // 2
                project(2 * par, par, half, b.xg_hi, b.xg_lo, True, False)
                if nu == 0:
                    norm_sums(nu)
                project(2 * par, par, half, b.xg_hi, b.xg_lo, False, True, half, half)
                norm_broadcast(nu)
            else:
                project(2 * par, par, DT, b.xg_hi, b.xg_lo, ready=ready)
            if first:
                pe.wait_ge(s.w_lo_ready, stage.first + 1)
            project(2 * par + 1, par, DT, b.xg_hi, b.xg_lo, w0=DT).then_inc(s.chunk_done, 1)

        chunk(0, 0, True)
        chunk(1, 1)
        with pe.Fori(1, FT // 2) as i:
            for j in range(2):
                chunk(i * 2 + j, j)

    def down(n, nu):
        stage, hidden = STAGE[f"down{n}"], FT * n

        def pair(m, wait=True):
            for e in range(2):
                if wait:
                    pe.wait_ge(s.x_ready, m + (DT * (nu - 1) + e - 1))
                for half in range(2):
                    pe.wait_ge(s.w_lo_ready, m * 2 + (stage.first + 2 * e + half + 1))
                    pe.wait_ge(s.h_lo_ready, hidden + DOWN_HALF * (half + 1))
                    project(4 + e, half, DOWN_HALF, b.h_hi, b.h_lo, half == 0, half == 1,
                            DOWN_HALF * half).then_inc(s.chunk_done, 1)

        pair(0, False)
        with pe.Fori(1, DT // 2) as i:
            pair(i * 2)

    def first_tiles(stage, z_hi, z_lo, ready, bank, steps):
        for m, k in steps:
            if k == 0:
                pe.wait_ge(s.w_lo_ready, stage.first + m + 1)
            pe.wait_ge(ready, k + 1)
            w_hi, w_lo = weight_tile(m, k)
            ins = split_matmul(b.ps[:, bank + m, :], w_hi, w_lo, z_hi[:, k, :], z_lo[:, k, :], k == 0, k == DT - 1)
            if k == DT - 1:
                ins.then_inc(s.chunk_done, 1)

    def other_tiles(stage, nu, z_hi, z_lo, bank, first_bank):
        for m in range(2, DT):
            pe.wait_ge(s.w_lo_ready, stage.first + m + 1)
            if m >= 4 or bank == first_bank:
                pe.wait_ge(s.x_ready, DT * (nu - 1) + m - 1)
            project(bank + m % 2, m % 2, DT, z_hi, z_lo).then_inc(s.chunk_done, 1)

    def mlstm():
        nu = 1
        stage = STAGE["a_qk"]

        def gate_columns():
            pe.wait_ge(s.floor_ready, 1)
            pe.wait_ge(s.v_ready, ST)
            for k, rows in enumerate((b.arow, b.floor)):
                for i in range(ST):
                    at = (ST * k + i) * SPAN
                    ins = pe.transpose(b.ps[:, 6, at:at + SPAN], rows[0:SPAN, P * i:P * i + P], ident[0:SPAN, 0:SPAN])
            ins.then_inc(s.cols_done, 1)

        pe.wait_ge(s.w_lo_ready, stage.first + 1)
        late_tile(nu, (0, 0), (1, 0), lambda: pe.wait_ge(s.w_lo_ready, stage.first + 2)).then_inc(s.chunk_done, 1)
        norm_sums(nu)
        project(1, 1, DT - EARLY_TILES, b.xg_hi, b.xg_lo, False, True, EARLY_TILES,
                EARLY_TILES).then_inc(s.chunk_done, 1)
        norm_broadcast(nu)
        for c in range(2, 8):
            pe.wait_ge(s.w_lo_ready, stage.first + c + 1)
            if c >= 4:
                pe.wait_ge(s.qk_drained, c - 3)
            project(c % 4, c % 2, DT, b.xg_hi, b.xg_lo).then_inc(s.chunk_done, 1)
        stage = STAGE["a_gates"]
        pe.wait_ge(s.qk_drained, 5)
        for c in range(2):
            pe.wait_ge(s.w_lo_ready, stage.first + c + 1)
            project(0, c, DT // 2, b.xg_hi, b.xg_lo, c == 0, c == 1, DT // 2 * c).then_inc(s.chunk_done, 1)
        stage = STAGE["a_v"]
        for c in range(4):
            pe.wait_ge(s.w_lo_ready, stage.first + c + 1)
            if c == 0:
                pe.wait_ge(s.rinv_ready, nu + 1)
            if c == 2:
                pe.wait_ge(s.gates_drained, 1)
                pe.wait_ge(s.qk_drained, 8)
            values(c, c % 2, 0 if c >= 2 else 4, None,
                   halfway=gate_columns if c == 3 else None).then_inc(s.chunk_done, 1)

        last = 2 * HEADS_A - 1

        def scores(u, with_unit):
            h, backward = u // 2, u % 2
            row = h + BACK * backward
            if u:
                pe.wait_ge(s.wt_ready, ST * u)
            else:
                pe.wait_ge(s.v_ready, ST + 1)
            pe.matmul(b.ps[:, 0, :], ident[0:SPAN, row:row + 1].to_broadcast([SPAN, P]), b.mrow[0:SPAN, :],
                      start=True, stop=True).then_inc(s.mrow_bcast, 1)
            for j in range(ST):
                si, n = (ST - 1 - j if backward else j), ST * u + j
                lo, hi, _ = band(si, backward)
                if n >= 2:
                    pe.wait_ge(s.p_ready, n - 1)
                else:
                    pe.wait_ge(s.v_ready, ST + 2 + n)
                pe.matmul(b.ps[:, 2 + n % 2, lo:hi], b.qk[:, HEADS_A + h, P * si:P * si + P], b.qk[:, h, lo:hi],
                          start=True, stop=True).then_inc(s.s_done, 1)
                if with_unit is not None:
                    beside(with_unit, j)

        def outputs(u):
            h, backward = u // 2, u % 2
            order = range(ST)[::-1] if backward else range(ST)
            pe.wait_ge(s.p_ready, ST * (u + 1))
            pe.wait_ge(s.psum_step, (ST - 1) * (u + 1))
            if u >= 3 and u % 2:
                pe.wait_ge(s.mean_ready, HEAD_EVENT + (u - 3) // 2 + 1)
            for i in range(ST):
                alone = i == (ST - 1 if backward else 0)
                at = band(i, backward)[2] + (P * i if backward else 0)
                rows = b.p[:, u % 2, at:at + P] if alone else b.psum[:, P * i:P * i + P]
                ins = pe.matmul(b.ps[:, 6, 320 + ST * u + i:320 + ST * u + i + 1], rows, b.ones[:, :],
                                start=True, stop=True)
            ins.then_inc(s.den_done, 1)
            if u:
                pe.wait_ge(s.o_drained, u)
            for e in range(2):
                if u == last and e:
                    spread_head(HEADS_A - 2)
                for j, si in enumerate(order):
                    lo, hi, at = band(si, backward)
                    v = b.v[:, si, DV * h + P * e:DV * h + P * e + P]
                    ins = pe.matmul(b.ps[:, 4 + e, lo:hi], v, b.p[:, u % 2, at:at + hi - lo],
                                    start=j == 0, stop=j == ST - 1)
            ins.then_inc(s.o_done, 1)

        def spread(u):
            pe.wait_ge(s.rden_ready, u + 1)
            if u:
                pe.wait_ge(s.dbc_ready, u)
            broadcast(b.ps[:, 7, :], b.rden[:, u % 2, :]).then_inc(s.dbc_done, 1)

        def spread_head(h):
            pe.wait_ge(s.rcol_ready, HEAD_EVENT + h + 1)
            if h != HEADS_A - 2:
                pe.wait_ge(s.dbc_ready, min(2 * h + 4, 2 * HEADS_A))
            broadcast(b.ps[:, 0 if h == HEADS_A - 2 else 7, :], b.rcol[:, 0:ST]).then_inc(s.head_bcast, 1)

        def head_sums(h):
            pe.wait_ge(s.ysq_ready, h + 1)
            column_sums(b.ps[:, 6, 0:ST], b.ysq[:, :]).then_inc(s.sums_done, 1)

        stage = STAGE["a_o"]

        def gate_part(u, j):
            if j == 0:
                pe.wait_ge(s.w_lo_ready, stage.first + u + 1)
                if u:
                    pe.wait_ge(s.os_ready, u)
                else:
                    pe.wait_ge(s.v_ready, 2 * ST)
                    pe.wait_ge(s.cols_ready, 1)
            ins = project(1, u % 2, 2, b.xg_hi, b.xg_lo, j == 0, j == ST - 1, 2 * j, 2 * j)
            if j == ST - 1:
                ins.then_inc(s.chunk_done, 1)

        def beside(u, j):
            gate_part(u, j)
            if u and j == (u >= 5 and u % 2):
                if u >= 5 and u % 2:
                    pe.wait_ge(s.z_ready, u - 3)
                spread(u - 1)
            if j == 2 - (u == 3) and u >= 3 and u % 2:
                head_sums((u - 3) // 2)

        pe.wait_ge(s.qk_ready, 8)
        scores(0, None)
        for u in range(last):
            scores(u + 1, u)
            if u >= 4 and u % 2 == 0:
                spread_head(u // 2 - 2)
            outputs(u)
        for j in range(ST - 1):
            beside(last, j)
        outputs(last)
        spread(last)
        gate_part(last, ST - 1)
        out, steps = STAGE["a_out"], first_tiles_order(DT // 2)
        first_tiles(out, b.z_hi, b.z_lo, s.z_lo_ready, 2, steps[0:4])
        head_sums(HEADS_A - 1)
        first_tiles(out, b.z_hi, b.z_lo, s.z_lo_ready, 2, steps[4:8])
        spread_head(HEADS_A - 1)
        first_tiles(out, b.z_hi, b.z_lo, s.z_lo_ready, 2, steps[8:])
        other_tiles(out, nu + 1, b.z_hi, b.z_lo, 2, 2)

    def values(c, slot, bank, tiles, ready=None, free=None, halfway=None):
        for kk in range(V_K):
            k = V_K * (c % 2) + kk
            if ready is not None:
                pe.wait_ge(ready[0], ready[1] + k + 1)
            if halfway and kk == V_K // 2:
                halfway()
            cols = slice(512 * kk, 512 * kk + 512)
            for i in range(ST):
                if free and kk == 0:
                    free(i)
                hi, lo = b.xg_hi[:, k, :], b.xg_lo[:, k, :]
                if tiles:
                    hi, lo = tiles(hi, i), tiles(lo, i)
                else:
                    hi, lo = hi[:, P * i:P * i + P], lo[:, P * i:P * i + P]
                ins = split_matmul(b.ps[:, bank + i, :], hi, lo, b.w_hi[:, slot, cols], b.w_lo[:, slot, cols],
                                   k == 0, k == DT - 1)
        return ins

    def b_values(pas):
        stage, nu = STAGE[f"b_v{pas}"], 4
        for c in range(6):
            group = c // 2
            pe.wait_ge(s.w_lo_ready, stage.first + c + 1)

            def free(i, group=group):
                if group == 0 and pas:
                    if i < 2:
                        pe.wait_ge(s.qkb_ready, 6 * (PAIRS_A_PASS + 1) - 1 + i)
                if group == 1:
                    if pas == 0 and i == ST - 1:
                        pe.wait_ge(s.rinv_ready, nu + 1)
                    if pas and i == 0:
                        pe.wait_ge(s.yb_lo_ready, PAIRS_A_PASS - 1)
                        pe.wait_ge(s.out_ready, 8 * PAIRS_A_PASS)
                        pe.wait_ge(s.pt_ready, 8 * PAIRS_A_PASS)
                if group == 2 and i == 0:
                    pe.wait_ge(s.bv_ready, 12 * pas + 4)

            ready = (s.xg_lo_ready, DT * nu) if pas == 0 and group == 0 else None
            values(c, c % 2, 4 * (group % 2), order_2 if group else None, ready,
                   None if c % 2 else free).then_inc(s.chunk_done, 1)
            if pas == 0 and c == 0:
                norm_sums(nu)
            if pas == 0 and c == 1:
                norm_broadcast(nu)

    def b_slot(pair, k):
        n, buf = 8 * pair + k, pair % 2
        if k < 8:
            o, hd, tp = UNITS[k]
            rows = slice(DH * hd, DH * hd + DH)
            if n >= 2:
                pe.wait_ge(s.neg_ready, n - 1)
            for t in range(2):
                i = 2 * tp + t
                q = slice(P * i, P * i + P)
                at = 2 * P * t
                if o == 0:
                    ks = slice(window(i), window(i) + 2 * P)
                    ins = pe.matmul(b.ps[:, 2 + hd, at:at + 2 * P], b.qkb[rows, buf, 4, q], b.qkb[rows, buf, 5, ks],
                                    start=True, stop=True)
                else:
                    for g in range(2):
                        ins = pe.matmul(b.ps[:, 2 + hd, at + P * g:at + P * g + P], b.qkb[rows, buf, 2 * g, q],
                                        b.qkb[rows, buf, 1 + 2 * g, q], start=True, stop=True)
            ins.then_inc(s.s2_done, 1)
        if 1 <= k <= 8:
            m = n - 1
            pe.wait_ge(s.prob_ready, 2 * m + 2)
            if m >= 2:
                pe.wait_ge(s.pt_ready, m - 1)
            for q in range(4):
                ins = pe.transpose(b.ps[:, 4 + m % 2, P * q:P * q + P], b.prob[:, P * q:P * q + P], ident)
            ins.then_inc(s.pt_done, 1)
        if k >= 2:
            o, hd, tp = UNITS[k - 2]
            m = n - 2
            pe.wait_ge(s.pt_ready, m + 1)
            if m:
                pe.wait_ge(s.out_ready, m)
            at = 2 * DH * (k % 2)
            cols = slice(P * (pair % PAIRS_A_PASS) + DH * hd, P * (pair % PAIRS_A_PASS) + DH * hd + DH)
            for t in range(2):
                i = 2 * tp + t
                if o:
                    vals = (b.v2[:, i, cols], b.v3[:, i, cols])
                elif i in (0, ST - 1):
                    vals = tuple(b.v1[:, window(i) // P + e, cols] for e in range(2))
                else:
                    vals = tuple(b.vs[:, window(i) // P + e, cols] for e in range(2))
                for e in range(2):
                    ins = pe.matmul(b.ps[:, 6, at + DH * t:at + DH * t + DH],
                                    b.prob_t[:, 2 * P * t + P * e:2 * P * t + P * e + P], vals[e],
                                    start=e == 0, stop=e == 1)
            ins.then_inc(s.pv_done, 1)

    def b_finish(pair):
        pe.wait_ge(s.mix_ready, pair + 1)
        if pair:
            pe.wait_ge(s.yb_lo_ready, pair)
        for i in range(ST):
            ins = pe.transpose(b.ps[:, 7, P * i:P * i + P], b.ssq[:, P * i:P * i + P], ident)
        ins.then_inc(s.yt_done, 1)

    def b_pair(chunks, attend):
        for slot in range(2 * QK_TILES):
            chunk, odd = chunks[slot // 2], slot % 2
            bank = chunk.tile % 2 if chunk else None
            if chunk and not odd:
                pe.wait_ge(s.w_lo_ready, chunk.number + 1)
                n = QK_TILES * chunk.pair + chunk.tile
                if n >= 2:
                    pe.wait_ge(s.qkb_ready, n - 1)
                if chunk.tile < 2 and chunk.pair in (0, PAIRS_A_PASS + 1):
                    pe.wait_ge(s.bv_ready, (8 if chunk.pair == 0 else 20) + chunk.tile + 1)
                project(bank, bank, 2, b.xg_hi, b.xg_lo, True, False, 0, 0)
            if attend is not None and slot < SLOTS:
                if slot == 0:
                    pe.wait_ge(s.qkb_ready, QK_TILES * attend + FIRST_QK)
                    if attend % PAIRS_A_PASS == 0:
                        pe.wait_ge(s.bv_ready, 12 * (attend // PAIRS_A_PASS + 1))
                        pe.wait_ge(s.vs_landed, 32 * (attend // PAIRS_A_PASS + 1))
                if slot == N_UNITS // 2:
                    pe.wait_ge(s.qkb_ready, QK_TILES * (attend + 1))
                b_slot(attend, slot)
                if attend and slot == FINISH_SLOT:
                    b_finish(attend - 1)
            if chunk:
                if odd:
                    project(bank, bank, 2, b.xg_hi, b.xg_lo, False, True, 6, 6).then_inc(s.chunk_done, 1)
                else:
                    project(bank, bank, 4, b.xg_hi, b.xg_lo, False, False, 2, 2)
            elif attend == PAIRS - 1 and slot < SLOTS:
                first_tiles(STAGE["b_out"], b.yb_hi, b.yb_lo, s.yb_lo_ready, 0, b_out_steps(slot))

    def dilated():
        b_values(0)
        b_pair(qk_chunks(None), None)
        for pair in range(PAIRS_A_PASS):
            b_pair(qk_chunks(pair), pair)
        b_values(1)
        for pair in range(PAIRS_A_PASS, PAIRS):
            b_pair(qk_chunks(pair), pair)
        b_finish(PAIRS - 1)
        out = STAGE["b_out"]
        first_tiles(out, b.yb_hi, b.yb_lo, s.yb_lo_ready, 0, b_out_steps(SLOTS))
        other_tiles(out, 5, b.yb_hi, b.yb_lo, 4, 0)

    pe.wait_ge(s.small_landed, 16)
    pe.wait_ge(s.consts_ready, 2)
    up(0, 0)
    down(0, 1)
    mlstm()
    up(1, 2)
    down(1, 3)
    up(2, 3)
    down(2, 4)
    dilated()
    up(3, 5)
    down(3, 6)
    norm_sums(6)
    norm_broadcast(6)


def gpsimd_program(pool, b, s):

    def power(e, cols):
        pool.wait_ge(s.mean_ready, e + 1)
        pool.tensor_tensor(b.rsqrt[:, 0:cols], b.mean_sq[:, 0:cols], b.exponent[:, 0:cols],
                           ALU.pow).then_inc(s.rsqrt_ready, 1)

    def mlstm_masks():
        for u in range(2 * HEADS_A):
            backward = u % 2
            for j in range(ST):
                si, n = (ST - 1 - j if backward else j), ST * u + j
                block = b.wt[:, n % 2, P * si:P * si + P]
                sign = -1 if backward else 1
                pool.wait_ge(s.wt_ready, n + 1)
                pool.affine_select(out=block, in_=block, pattern=[[sign, P]], compare_op=ALU.is_ge, fill=0.0,
                                   base=0, channel_multiplier=-sign).then_inc(s.wt_masked, 1)
            if u >= 4 and u % 2 == 0:
                power(HEAD_EVENT + u // 2 - 2, ST)

    def shift_values(pas):
        pool.wait_ge(s.bv_ready, 12 * pas + 4)
        pool.dma_start(b.vs[0:HALF, :, :], b.v1[HALF:P, 0:ST - 1, :]).then_inc(s.vs_landed, 16)
        pool.dma_start(b.vs[HALF:P, :, :], b.v1[0:HALF, 1:ST, :]).then_inc(s.vs_landed, 16)

    def reorder(pair):
        pool.wait_ge(s.out_ready, 8 * pair + 4)
        pool.wait_ge(s.prob_ready, 16 * pair + 8)
        if pair:
            pool.wait_ge(s.mix_ready, pair)
        for i in range(ST):
            pool.dma_start(b.o2t[:, i, :, :], b.o2[32 * i:32 * i + 32, :, :, :]).then_inc(s.o2t_landed, 16)

    pool.wait_ge(s.consts_ready, 2)
    power(0, ST)
    power(1, ST)
    mlstm_masks()
    for h in (HEADS_A - 2, HEADS_A - 1):
        power(HEAD_EVENT + h, ST)
    for nu in (2, 3):
        power(event(nu), ST)
    power(event(4), 2 * ST)
    for pas in range(NPASS):
        shift_values(pas)
        for pair in range(PAIRS_A_PASS):
            reorder(PAIRS_A_PASS * pas + pair)
    for nu in (5, 6):
        power(event(nu), ST)



def tiled(w, rows=P):
    return w.reshape(w.shape[0] // rows, rows, w.shape[1])


def output_tiles(w):
    k, n = w.shape
    return np.ascontiguousarray(w.reshape(k // P, P, n // P, P).transpose(2, 1, 0, 3)).reshape(n // P, P, k)


def value_chunks(w):
    n = w.shape[1]
    a = w.reshape(2, V_K, P, n // 512, 512).transpose(3, 0, 2, 1, 4)
    return np.ascontiguousarray(a).reshape(2 * (n // 512), P, V_COLS)


def down_chunks(w):
    a = w.reshape(2, DOWN_HALF, P, DT, P).transpose(3, 0, 2, 1, 4)
    return np.ascontiguousarray(a).reshape(2 * DT, P, DOWN_COLS)


def columns(v):
    return np.ascontiguousarray(v.reshape(-1, P).T)


def lay_out(inputs):
    i = {k: np.asarray(v) for k, v in inputs.items()}
    out = {"x_t": np.ascontiguousarray(i["x"][0].T).reshape(DT, P, SEQ)}
    ffns = [("ffn1", 0), ("ffn2", 0), ("ffn1", 1), ("ffn2", 1)]
    for n, (name, layer) in enumerate(ffns):
        gate, up = output_tiles(i[f"{name}_gate"][layer]), output_tiles(i[f"{name}_up"][layer])
        out[f"w_up{n}"] = np.concatenate([gate, up], axis=2)
        out[f"w_down{n}"] = down_chunks(i[f"{name}_down"][layer])
    w = i["a_w_in"][0]
    qk, v = 2 * HEADS_A * DQK, HEADS_A * DV
    out["w_a_qk"] = output_tiles(w[:, :qk])
    out["w_a_v"] = value_chunks(w[:, qk:qk + v])
    out["w_a_o"] = output_tiles(w[:, qk + v:qk + 2 * v])
    gates, gate_b = np.zeros((D, P), np.float32), np.zeros(P, np.float32)
    for k, row in enumerate((0, 64, 32, 96)):
        src = slice(qk + 2 * v + HEADS_A * k, qk + 2 * v + HEADS_A * (k + 1))
        gates[:, row:row + HEADS_A] = w[:, src]
        gate_b[row:row + HEADS_A] = i["a_gate_b"][0][HEADS_A * k:HEADS_A * (k + 1)]
    out["w_a_gates"] = np.ascontiguousarray(gates.reshape(2, DT // 2, P, P).transpose(0, 2, 1, 3)).reshape(2, P, GATE_COLS)
    out["w_a_out"] = output_tiles(i["a_w_out"][0])
    w = i["b_w_in"][0].reshape(D, 3, 3, D)
    v = [value_chunks(np.ascontiguousarray(w[:, g, 2, VCOLS * h:VCOLS * h + VCOLS])) for h in range(NPASS) for g in range(3)]
    out["w_b_v"] = np.concatenate(v)
    tiles = [output_tiles(np.ascontiguousarray(w[:, g, j])) for g in (1, 2, 0) for j in range(2)]
    out["w_b_qk"] = np.ascontiguousarray(np.stack(tiles, axis=1)).reshape(6 * PAIRS, P, TILE_COLS)
    out["w_b_out"] = output_tiles(i["b_w_out"][0])
    gains = [i["norm_ffn1"][0], i["norm_mix"][0], i["norm_ffn2"][0], i["norm_ffn1"][1], i["norm_mix"][1],
             i["norm_ffn2"][1], i["norm_final"]]
    conv_w = i["a_conv_w"][0].reshape(TAPS, 8, P).transpose(2, 1, 0).reshape(P, 8 * TAPS)
    slopes = np.exp2(-8.0 * (np.arange(HEADS_B) + 1.0) / HEADS_B).astype(np.float32)
    out["small"] = np.ascontiguousarray(np.concatenate(
        [np.eye(P, dtype=np.float32), *[columns(g) for g in gains], conv_w, columns(i["a_conv_b"][0]),
         columns(i["a_head_g"][0]), gate_b[:, None], np.broadcast_to(slopes, (P, HEADS_B))], axis=1))
    q = np.arange(P)[:, None, None]
    first = np.array([window(t) - P * t for t in (0, 1, ST - 1)])[None, :, None]
    dist = np.abs(first + np.arange(2 * P)[None, None, :] - q)
    out["dist1"] = np.where(dist <= HALF, dist, FAR).astype(np.float32)
    j = np.abs(np.arange(P)[None, :] - np.arange(P)[:, None])
    out["dist2"] = np.concatenate([np.where(j <= HALF, 4 * j, FAR), np.where(j % 4 == 0, 4 * j, FAR)],
                                  axis=1).astype(np.float32)[:, None, :]
    return out


def kernel(**inputs):
    import concourse.bacc as bacc
    from concourse.bass_utils import run_bass_kernel_spmd

    arrays = lay_out(inputs)
    nc = bacc.Bacc("TRN2", target_bir_lowering=False, num_devices=1)
    arrays = {f"in_{name}": a for name, a in arrays.items()}
    d = {name[3:]: nc.dram_tensor(name, a.shape, mybir.dt.from_np(a.dtype), kind="ExternalInput").ap()
         for name, a in arrays.items()}
    d["out_t"] = nc.dram_tensor("result_t", (DT, P, SEQ), F32, kind="ExternalOutput").ap()
    build(nc, d)
    r = run_bass_kernel_spmd(nc, [arrays], core_ids=[0])
    out = r.results[0]["result_t"].reshape(D, SEQ)
    return np.ascontiguousarray(out.T)[None]
```
